# Optimizing a Trainium2 kernel written in Bass

```python
import jax, jax.numpy as jnp
from jax import lax
import numpy as np

D_MODEL = 1024
BATCH = 1
SEQ = 256
DEPTH = 2

HEAD_DIM = 64
ROPE_THETA = 10000.0
RMS_EPS = 1e-6

ATTN_HEADS = 8
ATTN_WIDTH = ATTN_HEADS * HEAD_DIM
MOBA_BLOCK = 256
MOBA_TOPK = 3
MOBA_QUERY_CHUNK = 16
NEG_INF = -1e30

CONV_WIDTH = 512
CONV_GROUPS = 8
CONV_KERNEL = 3

RET_HEADS = 4
RET_QK_WIDTH = RET_HEADS * HEAD_DIM
RET_V_DIM = 2 * HEAD_DIM
RET_V_WIDTH = RET_HEADS * RET_V_DIM
RET_CHUNK = 128

N_BRANCHES = 3
IN_PROJ_WIDTH = 3 * ATTN_WIDTH + 3 * CONV_WIDTH + 2 * RET_QK_WIDTH + 2 * RET_V_WIDTH + N_BRANCHES * D_MODEL

D_FF = 3584
N_EXPERTS = 8
TOP_K = 2
D_FF_EXPERT = 3584
N_DENSE = (DEPTH + 1) // 2
N_MOE = DEPTH // 2

kernel_name = "hybrid_moba_shortconv_retention_moe_block"

def rmsnorm(x, w):
    xf = x.astype(jnp.float32)
    y = xf * lax.rsqrt(jnp.mean(xf * xf, axis=-1, keepdims=True) + RMS_EPS)
    return y.astype(x.dtype) * w

def rope_tables(seq, dim):
    inv_freq = 1.0 / (ROPE_THETA ** (jnp.arange(0, dim, 2, dtype=jnp.float32) / dim))
    ang = jnp.arange(seq, dtype=jnp.float32)[:, None] * inv_freq[None, :]
    return jnp.cos(ang), jnp.sin(ang)

def apply_rope(x, cos, sin):
    x1, x2 = jnp.split(x, 2, axis=-1)
    c = cos[None, :, None, :]
    s = sin[None, :, None, :]
    return jnp.concatenate([x1 * c - x2 * s, x2 * c + x1 * s], axis=-1).astype(x.dtype)

def moba_attention(q, k, v):
    b, s, h, d = q.shape
    bh = b * h
    nb = -(-s // MOBA_BLOCK)
    pad = nb * MOBA_BLOCK - s
    k_p = jnp.pad(k, ((0, 0), (0, pad), (0, 0), (0, 0)))
    v_p = jnp.pad(v, ((0, 0), (0, pad), (0, 0), (0, 0)))
    kb = k_p.reshape(b, nb, MOBA_BLOCK, h, d).transpose(0, 3, 1, 2, 4).reshape(bh, nb, MOBA_BLOCK, d)
    vb = v_p.reshape(b, nb, MOBA_BLOCK, h, d).transpose(0, 3, 1, 2, 4).reshape(bh, nb, MOBA_BLOCK, d)
    qh = (q * HEAD_DIM ** -0.5).transpose(0, 2, 1, 3).reshape(bh, s, d)

    k_mean = jnp.mean(kb.astype(jnp.float32), axis=2)
    q_blk = jnp.arange(s) // MOBA_BLOCK
    gate = jnp.einsum('nsd,nkd->nsk', qh.astype(jnp.float32), k_mean)
    past = jnp.arange(nb)[None, :] < q_blk[:, None]
    gate = jnp.where(past[None], gate, -jnp.inf)
    n_sel = min(MOBA_TOPK, nb)
    _, sel = lax.top_k(gate, n_sel)
    valid = sel < q_blk[None, :, None]

    nq = s // MOBA_QUERY_CHUNK
    qc = qh.reshape(bh, nq, MOBA_QUERY_CHUNK, d).swapaxes(0, 1)
    selc = sel.reshape(bh, nq, MOBA_QUERY_CHUNK, n_sel).swapaxes(0, 1)
    valc = valid.reshape(bh, nq, MOBA_QUERY_CHUNK, n_sel).swapaxes(0, 1)
    bh_idx = jnp.arange(bh)[:, None, None]

    def one_chunk(args):
        c, q_c, sel_c, val_c = args
        j = (c * MOBA_QUERY_CHUNK) // MOBA_BLOCK
        k_sel = kb[bh_idx, sel_c]
        v_sel = vb[bh_idx, sel_c]
        s_sel = jnp.einsum('nqd,nqkld->nqkl', q_c, k_sel).astype(jnp.float32)
        s_sel = jnp.where(val_c[..., None], s_sel, NEG_INF)
        k_own = lax.dynamic_index_in_dim(kb, j, axis=1, keepdims=False)
        v_own = lax.dynamic_index_in_dim(vb, j, axis=1, keepdims=False)
        s_own = jnp.einsum('nqd,nld->nql', q_c, k_own).astype(jnp.float32)
        qpos = c * MOBA_QUERY_CHUNK + jnp.arange(MOBA_QUERY_CHUNK)
        kpos = j * MOBA_BLOCK + jnp.arange(MOBA_BLOCK)
        s_own = jnp.where((kpos[None, :] <= qpos[:, None])[None], s_own, NEG_INF)
        logits = jnp.concatenate([s_sel.reshape(bh, MOBA_QUERY_CHUNK, n_sel * MOBA_BLOCK), s_own], axis=-1)
        p = jax.nn.softmax(logits, axis=-1).astype(v.dtype)
        p_sel = p[..., :n_sel * MOBA_BLOCK].reshape(bh, MOBA_QUERY_CHUNK, n_sel, MOBA_BLOCK)
        p_own = p[..., n_sel * MOBA_BLOCK:]
        return (jnp.einsum('nqkl,nqkld->nqd', p_sel, v_sel)
                + jnp.einsum('nql,nld->nqd', p_own, v_own))

    out = lax.map(one_chunk, (jnp.arange(nq), qc, selc, valc))
    return out.swapaxes(0, 1).reshape(b, h, s, d).transpose(0, 2, 1, 3)

def retention(q, k, v):
    b, s, h, dk = q.shape
    dv = v.shape[-1]
    nc = s // RET_CHUNK
    log_g = jnp.log1p(-jnp.exp2(-5.0 - jnp.arange(h, dtype=jnp.float32)))
    n = jnp.arange(RET_CHUNK, dtype=jnp.float32)
    diff = n[:, None] - n[None, :]
    decay = jnp.where(diff[None] >= 0,
                      jnp.exp(jnp.maximum(diff, 0.0)[None] * log_g[:, None, None]), 0.0)
    xi = jnp.exp((n + 1.0)[None, :] * log_g[:, None]).T
    zeta = jnp.exp((RET_CHUNK - 1.0 - n)[None, :] * log_g[:, None]).T
    chunk_decay = jnp.exp(RET_CHUNK * log_g)

    def to_chunks(t):
        return t.astype(jnp.float32).reshape(b, nc, RET_CHUNK, h, t.shape[-1]).swapaxes(0, 1)

    def body(state, xs):
        q_i, k_i, v_i = xs
        scores = jnp.einsum('bnhd,bmhd->bhnm', q_i, k_i) * decay[None]
        o = jnp.einsum('bhnm,bmhe->bnhe', scores, v_i)
        o = o + jnp.einsum('bnhd,bhde->bnhe', q_i, state) * xi[None, :, :, None]
        state = (state * chunk_decay[None, :, None, None]
                 + jnp.einsum('bmhd,bmhe->bhde', k_i * zeta[None, :, :, None], v_i))
        return state, o

    state0 = jnp.zeros((b, h, dk, dv), jnp.float32)
    _, o = lax.scan(body, state0, (to_chunks(q), to_chunks(k), to_chunks(v)))
    return o.swapaxes(0, 1).reshape(b, s, h, dv).astype(v.dtype)

def hybrid_mixer(h, w_in, conv_w, conv_b, ret_norm_w, w_br_attn, w_br_conv, w_br_ret, w_out, cos, sin):
    b, s, _ = h.shape
    widths = (ATTN_WIDTH, ATTN_WIDTH, ATTN_WIDTH, CONV_WIDTH, CONV_WIDTH, CONV_WIDTH,
              RET_QK_WIDTH, RET_QK_WIDTH, RET_V_WIDTH, RET_V_WIDTH, N_BRANCHES * D_MODEL)
    points, acc = [], 0
    for wdt in widths[:-1]:
        acc += wdt
        points.append(acc)
    proj = h @ w_in
    aq, ak, av, cb, cc, ch, rq, rk, rv, rg, gates = jnp.split(proj, points, axis=-1)

    aq = apply_rope(aq.reshape(b, s, ATTN_HEADS, HEAD_DIM), cos, sin)
    ak = apply_rope(ak.reshape(b, s, ATTN_HEADS, HEAD_DIM), cos, sin)
    av = av.reshape(b, s, ATTN_HEADS, HEAD_DIM)
    y_attn = moba_attention(aq, ak, av).reshape(b, s, ATTN_WIDTH)

    u = cc * ch
    conv = lax.conv_general_dilated(u, conv_w[:, None, :], window_strides=(1,),
                                    padding=((CONV_KERNEL - 1, 0),),
                                    dimension_numbers=('NWC', 'WIO', 'NWC'),
                                    feature_group_count=CONV_WIDTH) + conv_b
    y_conv = cb * conv

    rq = apply_rope(rq.reshape(b, s, RET_HEADS, HEAD_DIM), cos, sin)
    rk = apply_rope(rk.reshape(b, s, RET_HEADS, HEAD_DIM), cos, sin) * HEAD_DIM ** -0.5
    rv = rv.reshape(b, s, RET_HEADS, RET_V_DIM)
    o = retention(rq, rk, rv)
    o = rmsnorm(o, ret_norm_w.reshape(RET_HEADS, RET_V_DIM)).reshape(b, s, RET_V_WIDTH)
    y_ret = jax.nn.silu(rg) * o

    g_attn, g_conv, g_ret = jnp.split(jax.nn.sigmoid(gates), N_BRANCHES, axis=-1)
    merged = (g_attn * (y_attn @ w_br_attn)
              + g_conv * (y_conv @ w_br_conv)
              + g_ret * (y_ret @ w_br_ret))
    return merged @ w_out

def swiglu(h, w_gate, w_up, w_down):
    return (jax.nn.silu(h @ w_gate) * (h @ w_up)) @ w_down

def moe_swiglu(h, w_router, w_gate, w_up, w_down):
    logits = (h @ w_router).astype(jnp.float32)
    top_v, top_i = lax.top_k(logits, TOP_K)
    top_p = jax.nn.softmax(top_v, axis=-1)
    combine = jnp.sum(jax.nn.one_hot(top_i, N_EXPERTS, dtype=jnp.float32) * top_p[..., None], axis=-2)
    combine = combine.astype(h.dtype)
    out = jnp.zeros_like(h)
    for e in range(N_EXPERTS):
        out = out + combine[..., e:e + 1] * swiglu(h, w_gate[e], w_up[e], w_down[e])
    return out

def setup_inputs(seed: int = 0) -> dict:
    key = jax.random.key(seed)
    ks = jax.random.split(key, 20)
    f32 = jnp.float32

    def nrm(k, shape, scale):
        return jax.random.normal(k, shape, f32) * scale

    def gain(k, shape):
        return 1.0 + 0.02 * jax.random.normal(k, shape, f32)

    return {
        "x": nrm(ks[0], (BATCH, SEQ, D_MODEL), 1.0),
        "mix_norm_w": gain(ks[1], (DEPTH, D_MODEL)),
        "w_in": nrm(ks[2], (DEPTH, D_MODEL, IN_PROJ_WIDTH), D_MODEL ** -0.5),
        "conv_w": nrm(ks[3], (DEPTH, CONV_KERNEL, CONV_WIDTH), CONV_KERNEL ** -0.5),
        "conv_b": nrm(ks[4], (DEPTH, CONV_WIDTH), 0.01),
        "ret_norm_w": gain(ks[5], (DEPTH, RET_V_WIDTH)),
        "w_br_attn": nrm(ks[6], (DEPTH, ATTN_WIDTH, D_MODEL), ATTN_WIDTH ** -0.5),
        "w_br_conv": nrm(ks[7], (DEPTH, CONV_WIDTH, D_MODEL), CONV_WIDTH ** -0.5),
        "w_br_ret": nrm(ks[8], (DEPTH, RET_V_WIDTH, D_MODEL), RET_V_WIDTH ** -0.5),
        "w_out": nrm(ks[9], (DEPTH, D_MODEL, D_MODEL), D_MODEL ** -0.5),
        "ffn_norm_w": gain(ks[10], (DEPTH, D_MODEL)),
        "dense_w_gate": nrm(ks[11], (N_DENSE, D_MODEL, D_FF), D_MODEL ** -0.5),
        "dense_w_up": nrm(ks[12], (N_DENSE, D_MODEL, D_FF), D_MODEL ** -0.5),
        "dense_w_down": nrm(ks[13], (N_DENSE, D_FF, D_MODEL), D_FF ** -0.5),
        "moe_router": nrm(ks[14], (N_MOE, D_MODEL, N_EXPERTS), D_MODEL ** -0.5),
        "moe_w_gate": nrm(ks[15], (N_MOE, N_EXPERTS, D_MODEL, D_FF_EXPERT), D_MODEL ** -0.5),
        "moe_w_up": nrm(ks[16], (N_MOE, N_EXPERTS, D_MODEL, D_FF_EXPERT), D_MODEL ** -0.5),
        "moe_w_down": nrm(ks[17], (N_MOE, N_EXPERTS, D_FF_EXPERT, D_MODEL), D_FF_EXPERT ** -0.5),
        "final_norm_w": gain(ks[18], (D_MODEL,)),
    }

def reference(x, mix_norm_w, w_in, conv_w, conv_b, ret_norm_w, w_br_attn, w_br_conv, w_br_ret,
              w_out, ffn_norm_w, dense_w_gate, dense_w_up, dense_w_down, moe_router,
              moe_w_gate, moe_w_up, moe_w_down, final_norm_w):
    cos, sin = rope_tables(x.shape[1], HEAD_DIM)
    for layer in range(DEPTH):
        h = rmsnorm(x, mix_norm_w[layer])
        x = x + hybrid_mixer(h, w_in[layer], conv_w[layer], conv_b[layer], ret_norm_w[layer],
                             w_br_attn[layer], w_br_conv[layer], w_br_ret[layer], w_out[layer],
                             cos, sin)
        h = rmsnorm(x, ffn_norm_w[layer])
        if layer % 2 == 0:
            i = layer // 2
            x = x + swiglu(h, dense_w_gate[i], dense_w_up[i], dense_w_down[i])
        else:
            i = layer // 2
            x = x + moe_swiglu(h, moe_router[i], moe_w_gate[i], moe_w_up[i], moe_w_down[i])
    return rmsnorm(x, final_norm_w)


_drawn_inputs = setup_inputs


def setup_inputs(seed=0):
    import zlib

    import numpy as np

    out = dict(_drawn_inputs(seed))
    spreads = {}
    factors = {}
    for name, (base, spread) in spreads.items():
        noise = np.random.default_rng([zlib.crc32(name.encode()), seed]).standard_normal(out[name].shape)
        drawn = base * np.exp(spread * noise) if base else spread * noise
        out[name] = __import__('jax').numpy.asarray(drawn.astype(out[name].dtype))
    for name, factor in factors.items():
        out[name] = (out[name] * factor).astype(out[name].dtype)
    return out
```

```python
from contextlib import ExitStack

import numpy as np

import concourse.bass as bass
from concourse import mybir

F32 = mybir.dt.float32
F32R = mybir.dt.float32r
BF16 = mybir.dt.bfloat16
I32 = mybir.dt.int32
U32 = mybir.dt.uint32
ALU = mybir.AluOpType
ACT = mybir.ActivationFunctionType
AX_X = mybir.AxisListType.X

P = 128
DEPTH = 2
SEQ = 256
D = 1024
KT = D // P
HEAD = 64
EPS = 1e-6
ATTN_HEADS = 8
RET_HEADS = 4
BR_W = 512
BT = BR_W // P
FF = 3584
FCH = FF // 512
NEXP = 8

UNIT = 2048
RAW = 6
SPLIT = 3
MIX_UNITS = 40
FFN_UNITS = 6 * FCH
CHUNKS = (0, 1, 2, 6, 7, 4, 5, 3, 8, 9, 10, 11, 12, 13, 14)
BR_ATTN, BR_CONV, BR_RET, OUT_PROJ = 22, 28, 34, 36

CONST_PARTS = (("ident", 128), ("cos", 128), ("sin", 128), ("decay", 512), ("xi", 256), ("zeta", 4),
               ("iota", 128), ("before", 128), ("ones", 128), ("pick", 640))
CONST_AT = {}
CONST_W = 0
for _name, _w in CONST_PARTS:
    CONST_AT[_name] = (CONST_W, CONST_W + _w)
    CONST_W += _w


def shape_constants():
    c = np.zeros((P, CONST_W), np.float32)

    def put(name, a):
        lo, hi = CONST_AT[name]
        c[:a.shape[0], lo:hi] = a

    inv_freq = (1.0 / (np.float32(10000.0) ** (np.arange(0, HEAD, 2, dtype=np.float32) / HEAD))).astype(np.float32)
    ang = np.arange(SEQ, dtype=np.float32)[:, None] * inv_freq[None, :]
    cos, sin = np.cos(ang), np.sin(ang)
    tokens = lambda a: a.reshape(2, P, HEAD).transpose(1, 0, 2).reshape(P, 2 * HEAD)
    put("cos", tokens(np.concatenate([cos, cos], 1)))
    put("sin", tokens(np.concatenate([-sin, sin], 1)))
    log_g = np.log1p(-np.exp2(-5.0 - np.arange(RET_HEADS, dtype=np.float32))).astype(np.float32)
    n = np.arange(P, dtype=np.float32)
    diff = n[None, :] - n[:, None]
    scale = np.float32(HEAD ** -0.5)
    decay = np.where(diff[None] >= 0, np.exp(np.maximum(diff, 0)[None] * log_g[:, None, None]), 0) * scale
    put("decay", decay.transpose(1, 0, 2).reshape(P, RET_HEADS * P))
    xi = np.exp((n + 1)[None, :] * log_g[:, None])
    put("xi", np.repeat(xi.reshape(2, 2, P), HEAD, axis=1).reshape(2, P, P).transpose(1, 0, 2).reshape(P, 2 * P))
    put("zeta", (np.exp((P - 1 - n)[None, :] * log_g[:, None]) * scale).T)
    put("ident", np.eye(P))
    put("iota", np.tile(n, (P, 1)))
    put("before", np.triu(np.ones((P, P)), 1))
    put("ones", np.ones((P, P)))
    put("pick", np.kron(np.eye(5), np.ones((1, P))))
    masks = np.zeros((P, 3 * P), np.float32)
    masks[:, :P] = np.eye(P)
    masks[:, 2 * P:] = np.triu(np.full((P, P), -1e30), 1)
    return c, masks


class Signal:

    def __init__(self, sem, per_layer=0):
        self.sem, self.per_layer = sem, per_layer

    def wait(self, eng, k, layer=0):
        eng.wait_ge(self.sem, layer * self.per_layer + k)


class Chain:

    def __init__(self, sem, eng):
        self.sem, self.eng, self.n = sem, eng, 0

    def __call__(self, ins):
        self.n += 1
        ins.then_inc(self.sem, 1)
        self.eng.wait_ge(self.sem, self.n)


def hybrid_trunk_kernel(nc, x, mix_norm_w, w_in, conv_w, conv_b, ret_norm_w, w_br_attn, w_br_conv,
                        w_br_ret, w_out, ffn_norm_w, dense_w_gate, dense_w_up, dense_w_down,
                        moe_router, moe_w_gate, moe_w_up, moe_w_down, final_norm_w,
                        consts, masks, out):
    ctx = ExitStack()
    with ctx:
        at = [(nc.sbuf_base + 31) // 32 * 32]

        def place(name, shape, dt):
            size = int(np.prod(shape[1:])) * (2 if dt == BF16 else 4)
            t = nc.alloc_sbuf_tensor_at(name, shape, dt, offset=at[0])
            at[0] += (size + 31) // 32 * 32
            return t

        raw = place("raw", [P, RAW, UNIT], F32)
        w_hi = place("w_hi", [P, SPLIT, UNIT], F32R)
        w_lo = place("w_lo", [P, SPLIT, UNIT], F32R)
        res = place("res", [P, 2, D], F32)
        wide = place("wide", [P, 2, D], F32)
        cst = place("cst", [P, CONST_W], F32)
        msk = place("msk", [P, 3 * P], BF16)
        zeros = place("zeros", [P, 512], BF16)
        norm_w = place("norm_w", [5, D], F32)
        chan_rows = place("chan_rows", [40, P], F32)
        chan = place("chan", [P, 40], F32)
        stat = place("stat", [P, 64], F32)
        router = place("router", [P, KT, NEXP], F32)
        region = at[0]
        xT_hi = place("xT_hi", [P, KT, SEQ], F32R)
        xT_lo = place("xT_lo", [P, KT, SEQ], F32R)
        after_xT = at[0]
        ret_qk = place("ret_qk", [P, 2, 512], F32)
        gates_at = at[0]
        qT = place("qT", [P, BT, SEQ], F32)
        kT = place("kT", [P, BT, SEQ], F32)
        v_at = at[0]
        v_attn = place("v_attn", [P, 2, BR_W], F32)
        probs = place("probs", [P, 4, 384], F32)
        probsT = place("probsT", [P, 4, 384], F32)
        yA_hi = place("yA_hi", [P, BT, SEQ], F32R)
        yA_lo = place("yA_lo", [P, BT, SEQ], F32R)
        yC_hi = place("yC_hi", [P, BT, SEQ], F32R)
        yC_lo = place("yC_lo", [P, BT, SEQ], F32R)
        uT = place("uT", [P, BT, SEQ + 2], F32)
        rqT = place("rqT", [P, 2, SEQ], F32)
        rkT = place("rkT", [P, 2, SEQ], F32)
        rqxT = place("rqxT", [P, 2, P], F32)
        kzeta = place("kzeta", [P, 4 * HEAD], F32)
        state = place("state", [P, 2 * P], F32)
        v_ret = place("v_ret", [P, 2, BR_W], F32)
        ret_gate = place("ret_gate", [P, 2, BR_W], F32)
        assert at[0] <= nc.sbuf_usable_end, at[0]
        gates = nc.alloc_sbuf_tensor_at("gates", [P, 2, D], F32, offset=gates_at)
        ret_o = nc.alloc_sbuf_tensor_at("ret_o", [P, 2, BR_W], F32, offset=v_at)
        rope_tmp = probsT[:].rearrange("p a b -> p (a b)")[:, 0:512]
        decayed = probsT[:].rearrange("p a b -> p (a b)")[:, 0:1024]
        squares = probs[:].rearrange("p a b -> p (a b)")[:, 0:1024]
        conv = wide[:, 0, :].rearrange("p (c t) -> p c t", c=BT)
        conv_c = wide[:, 1, :].rearrange("p (c t) -> p c t", c=BT)
        at[0] = after_xT
        dn_act = place("dn_act", [P, 2, 512], F32)
        dn_sil = place("dn_sil", [P, 2, 512], F32)
        dnT_hi = place("dnT_hi", [P, 4, SEQ], F32R)
        dnT_lo = place("dnT_lo", [P, 4, SEQ], F32R)
        at[0] = after_xT
        tok_hi = place("tok_hi", [P, 2, D], F32R)
        tok_lo = place("tok_lo", [P, 2, D], F32R)
        ex_hi = place("ex_hi", [P, KT, P], F32R)
        ex_lo = place("ex_lo", [P, KT, P], F32R)
        put_in = place("put_in", [P, 2, P], F32R)
        put_back = place("put_back", [P, SEQ], F32R)
        ex_act = place("ex_act", [P, 512], F32)
        ex_sil = place("ex_sil", [P, 512], F32)
        exT_hi = place("exT_hi", [P, 4, P], F32R)
        exT_lo = place("exT_lo", [P, 4, P], F32R)
        ey_hi = place("ey_hi", [P, D], F32R)
        ey_lo = place("ey_lo", [P, D], F32R)
        rt_hi = place("rt_hi", [P, KT, NEXP], F32R)
        rt_lo = place("rt_lo", [P, KT, NEXP], F32R)
        logits = place("logits", [P, 2, NEXP], F32)
        top = place("top", [P, 2, NEXP], F32)
        top_at = place("top_at", [P, 2, NEXP], U32)
        top_f = place("top_f", [P, 2, NEXP], F32)
        first = place("first", [P, 2, NEXP], F32)
        second = place("second", [P, 2, NEXP], F32)
        chosen = place("chosen", [P, 2, NEXP], F32)
        share = place("share", [P, 2, NEXP], F32)
        slot_of = place("slot_of", [P, 2, NEXP], F32)
        prob = place("prob", [P, 8], F32)
        slot_w = place("slot_w", [P, 1], F32)
        crowded = place("crowded", [P, 1], I32)
        assert at[0] <= nc.sbuf_usable_end, at[0]

        ps = ctx.enter_context(nc.psum_tensor("ps", [P, 8, 512], F32))

        def const(name, rows=P):
            lo, hi = CONST_AT[name]
            return cst[0:rows, lo:hi]

        ident = const("ident")

        def sem(name):
            return ctx.enter_context(nc.semaphore(name))

        def signal(name, per_layer=0):
            return Signal(sem(name), per_layer)

        consts_in = sem("consts_in")
        x_in = sem("x_in")
        landed = [sem(f"landed{i}") for i in range(RAW)]
        hi_ready = sem("hi_ready")
        lo_ready = sem("lo_ready")
        unit_used = sem("unit_used")
        zeros_set = sem("zeros_set")
        pads_set = sem("pads_set")
        masks_cast = sem("masks_cast")
        chan_ps = sem("chan_ps")
        chan_set = sem("chan_set")
        tensor_chain = sem("tensor_chain")
        scalar_chain = sem("scalar_chain")
        vector_chain = sem("vector_chain")
        sq_summed = sem("sq_summed")
        root_ready = sem("root_ready")
        norm_w_ps = sem("norm_w_ps")
        normed = sem("normed")
        normed_ps = sem("normed_ps")
        xT_hi_ready = sem("xT_hi_ready")
        xT_lo_ready = sem("xT_lo_ready")
        res_added = sem("res_added")
        rope_done = signal("rope_done", 3)
        v_copied = signal("v_copied", 2)
        qkT_ps = signal("qkT_ps", 1)
        qT_ready = signal("qT_ready", 1)
        kT_ready = signal("kT_ready", 1)
        scores_ps = signal("scores_ps", 2)
        max_ready = signal("max_ready", 2)
        exp_done = signal("exp_done", 2)
        probs_ready = signal("probs_ready", 2)
        probsT_ps = signal("probsT_ps", 2)
        probsT_ready0 = signal("probsT_ready0", 2)
        probsT_ready1 = signal("probsT_ready1", 2)
        attn_ps = signal("attn_ps", 2)
        attn_hi = signal("attn_hi", 2)
        attn_lo = signal("attn_lo", 2)
        conv_c_copied = signal("conv_c_copied", 1)
        conv_u_ready = signal("conv_u_ready", 1)
        conv_y_ready = signal("conv_y_ready", 1)
        conv_hi = signal("conv_hi", 1)
        conv_lo = signal("conv_lo", 1)
        ret_qkT_ps = signal("ret_qkT_ps", 1)
        rqT_ready = signal("rqT_ready", 1)
        rkT_ready = signal("rkT_ready", 1)
        ret_scores_ps = signal("ret_scores_ps", 1)
        decayed_ready = signal("decayed_ready", 1)
        ret_o_ps = signal("ret_o_ps", 1)
        ret_sq_done = signal("ret_sq_done", 1)
        ret_ss_ready = signal("ret_ss_ready", 1)
        ret_root = signal("ret_root", 1)
        ret_gate_ready = signal("ret_gate_ready", 1)
        ret_y_ready = signal("ret_y_ready", 1)
        ret_yT_ps = signal("ret_yT_ps", 1)
        ret_hi = signal("ret_hi", 1)
        ret_lo = signal("ret_lo", 1)
        gate_ready = signal("gate_ready", 6)
        merged = signal("merged", 3)
        mergedT_ps = signal("mergedT_ps", 4)
        mT_hi = signal("mT_hi", 4)
        mT_lo = signal("mT_lo", 4)
        dn_silu = sem("dn_silu")
        dn_ready = sem("dn_ready")
        dnT_ps = sem("dnT_ps")
        dnT_hi_ready = sem("dnT_hi_ready")
        dnT_lo_ready = sem("dnT_lo_ready")
        ex_silu = sem("ex_silu")
        ex_ready = sem("ex_ready")
        exT_ps = sem("exT_ps")
        exT_hi_ready = sem("exT_hi_ready")
        exT_lo_ready = sem("exT_lo_ready")
        tok_hi_ready = sem("tok_hi_ready")
        tok_lo_ready = sem("tok_lo_ready")
        router_hi = sem("router_hi")
        router_lo = sem("router_lo")
        logits_ps = sem("logits_ps")
        gap_ready = sem("gap_ready")
        gap_exp = sem("gap_exp")
        chosen_ready = sem("chosen_ready")
        places_ps = sem("places_ps")
        routed = sem("routed")
        put_in_ready = sem("put_in_ready")
        put_back_ps = sem("put_back_ps")
        put_back_ready = sem("put_back_ready")
        slot_w_ready = sem("slot_w_ready")
        gathered_ps = sem("gathered_ps")
        ex_hi_ready = sem("ex_hi_ready")
        ex_lo_ready = sem("ex_lo_ready")
        ey_hi_ready = sem("ey_hi_ready")
        ey_lo_ready = sem("ey_lo_ready")
        back_ps = sem("back_ps")
        ex_added = sem("ex_added")
        slots_moved = sem("slots_moved")
        res_final = sem("res_final")
        out_ready = sem("out_ready")
        out_stored = sem("out_stored")

        MIX0 = (0, MIX_UNITS + FFN_UNITS)
        DENSE0 = MIX_UNITS
        MOE0 = 2 * MIX_UNITS + FFN_UNITS
        CROWD0 = MOE0 + NEXP * FFN_UNITS + 3

        def wait_split(eng, j, r):
            eng.wait_ge(lo_ready, r * RAW + (j + 1))

        def split_hi(act, j, r=0):
            act.wait_ge(landed[j % RAW], r * 16 + (j // RAW + 1) * 16)
            if j >= SPLIT:
                act.wait_ge(unit_used, r * RAW + (j - SPLIT + 1))
            nc.scalar.activation(w_hi[:, j % SPLIT, :], raw[:, j % RAW, :], ACT.Copy).then_inc(hi_ready, 1)

        def split_lo(dve, j, r=0):
            dve.wait_ge(hi_ready, r * RAW + (j + 1))
            if j >= SPLIT:
                dve.wait_ge(unit_used, r * RAW + (j - SPLIT + 1))
            nc.vector.tensor_tensor(w_lo[:, j % SPLIT, :], raw[:, j % RAW, :],
                                    w_hi[:, j % SPLIT, :].bitcast(F32), ALU.subtract).then_inc(lo_ready, 1)

        block = ctx.enter_context(nc.Block())

        @block.sync
        def _(sp):
            sp.dma_start(res[:], x.rearrange("b (t p) d -> p (b t) d", p=P)).then_inc(x_in, 16)

            def load(j, src, r=0):
                if j >= RAW:
                    sp.wait_ge(lo_ready, r * RAW + (j - RAW + 1))
                shape = src.shape
                dst = raw[:, j % RAW, :].rearrange("p (k n) -> p k n", n=shape[-1])
                sp.dma_start(dst, src).then_inc(landed[j % RAW], 16)

            def wide_unit(w, k_half, col):
                return w[bass.ds(k_half, 512), bass.ds(col, 512)].rearrange("(k p) n -> p k n", p=P)

            def deep_unit(w, row):
                return w[bass.ds(row, 2 * P), :].rearrange("(k p) n -> p k n", p=P)

            def load_mixer(layer):
                n = MIX0[layer]
                for c, chunk in enumerate(CHUNKS):
                    for half in range(2):
                        load(n, wide_unit(w_in[layer], half * 512, chunk * 512))
                        n += 1
                    if c in (10, 12, 14):
                        w = {10: w_br_attn, 12: w_br_conv, 14: w_br_ret}[c]
                        for h in range(2):
                            load(n, deep_unit(w[layer], h * 2 * P))
                            n += 1
                for h in range(4):
                    load(n, deep_unit(w_out[layer], h * 2 * P))
                    n += 1

            load_mixer(0)
            gate, up, down = dense_w_gate[0], dense_w_up[0], dense_w_down[0]
            for h in range(2):
                load(DENSE0 + h, wide_unit(gate, h * 512, 0))
            with sp.Fori(0, 6) as i:
                for h in range(2):
                    load(DENSE0 + 2 + h, wide_unit(up, h * 512, i * 512), i)
                for h in range(2):
                    load(DENSE0 + 4 + h, wide_unit(gate, h * 512, i * 512 + 512), i)
                for h in range(2):
                    load(DENSE0 + 6 + h, deep_unit(down, i * 512 + h * 2 * P), i)
            for h in range(2):
                load(DENSE0 + 38 + h, wide_unit(up, h * 512, (FCH - 1) * 512))
            for h in range(2):
                load(DENSE0 + 40 + h, deep_unit(down, (FCH - 1) * 512 + h * 2 * P))
            load_mixer(1)

            gate = moe_w_gate[0].rearrange("e k f -> (e k) f")
            up = moe_w_up[0].rearrange("e k f -> (e k) f")
            down = moe_w_down[0].rearrange("e f d -> (e f) d")

            def load_experts(base):
                with sp.Fori(0, NEXP) as e:
                    for h in range(2):
                        load(base + h, wide_unit(gate, e * D + h * 512, 0), e * FCH)
                    for h in range(2):
                        load(base + 2 + h, wide_unit(up, e * D + h * 512, 0), e * FCH)
                    with sp.Fori(0, 6) as i:
                        r = e * FCH + i
                        for h in range(2):
                            load(base + 4 + h, wide_unit(gate, e * D + h * 512, i * 512 + 512), r)
                        for h in range(2):
                            load(base + 6 + h, wide_unit(up, e * D + h * 512, i * 512 + 512), r)
                        for h in range(2):
                            load(base + 8 + h, deep_unit(down, e * FF + i * 512 + h * 2 * P), r)
                    for h in range(2):
                        load(base + 40 + h, deep_unit(down, e * FF + ((FCH - 1) * 512 + h * 2 * P)), e * FCH)
                for j in range(3):
                    n = base + NEXP * FFN_UNITS + j
                    sp.wait_ge(lo_ready, n - RAW + 1)
                    sp.dma_start(raw[:, n % RAW, 0:64], consts[:, 0:64]).then_inc(landed[n % RAW], 16)

            load_experts(MOE0)
            sp.wait_ge(routed, 1)
            flag = sp.value_load(crowded[0:1, 0:1], min_val=0, max_val=1)
            with sp.If(flag > 0):
                load_experts(CROWD0)
                sp.wait_ge(lo_ready, CROWD0 + NEXP * FFN_UNITS + 3)
            with sp.Else():
                sp.wait_ge(lo_ready, CROWD0)
            for t in range(2):
                sp.wait_ge(out_ready, t + 1)
                sp.dma_start(out[0, t * P:(t + 1) * P, :], wide[:, t, :]).then_inc(out_stored, 16)
            sp.wait_ge(out_stored, 32)

        @block.gpsimd
        def _(pool):
            nc.gpsimd.memset(zeros[:], 0.0).then_inc(zeros_set, 1)
            nc.gpsimd.memset(uT[:, :, 0:2], 0.0).then_inc(pads_set, 1)

        @block.tensor
        def _(pe):
            mm = nc.tensor.matmul
            chain = Chain(tensor_chain, pe)

            def three(o, a_hi, a_lo, b_hi, b_lo, start, stop):
                mm(o, a_hi, b_hi, start=start, stop=False, skip_group_check=True)
                mm(o, a_hi, b_lo, start=False, stop=False, skip_group_check=True)
                return mm(o, a_lo, b_hi, start=False, stop=stop, skip_group_check=True)

            def wide_unit(j, x_hi, x_lo, kt0, banks, r=0):
                wait_split(pe, j, r)
                s = j % SPLIT
                for k in range(4):
                    cols = slice(k * 512, k * 512 + 512)
                    for t, bank in enumerate(banks):
                        tok = slice(t * P, t * P + P)
                        last = three(ps[:, bank, :], x_hi[:, kt0 + k, tok], x_lo[:, kt0 + k, tok],
                                     w_hi[:, s, cols], w_lo[:, s, cols],
                                     start=(kt0 == 0 and k == 0), stop=(kt0 == 4 and k == 3))
                last.then_inc(unit_used, 1)

            def deep_unit(j, x_hi, x_lo, kt0, banks, start, stop, r=0):
                wait_split(pe, j, r)
                s = j % SPLIT
                for k in range(2):
                    for t, pair in enumerate(banks):
                        tok = slice(t * P, t * P + P)
                        for half, bank in enumerate(pair):
                            cols = slice(k * 1024 + half * 512, k * 1024 + half * 512 + 512)
                            last = three(ps[:, bank, :], x_hi[:, kt0 + k, tok],
                                         x_lo[:, kt0 + k, tok], w_hi[:, s, cols], w_lo[:, s, cols],
                                         start=(start and k == 0), stop=(stop and k == 1))
                last.then_inc(unit_used, 1)

            def channel_unit(j, kt0, bank0):
                wait_split(pe, j, 0)
                s = j % SPLIT
                for k in range(4):
                    for cb in range(4):
                        cols = slice(k * 512 + cb * P, k * 512 + cb * P + P)
                        o = ps[:, bank0 + cb // 2, (cb % 2) * SEQ:(cb % 2) * SEQ + SEQ]
                        last = three(o, w_hi[:, s, cols], w_lo[:, s, cols], xT_hi[:, kt0 + k, :],
                                     xT_lo[:, kt0 + k, :], start=(kt0 == 0 and k == 0 and cb % 2 == 0),
                                     stop=(kt0 == 4 and k == 3))
                last.then_inc(unit_used, 1)

            SUMS, EX_SUMS = ((4, 5), (6, 7)), ((2, 3),)

            def transpose(o, i):
                return nc.tensor.transpose(o, i, ident[0:i.shape[0], 0:i.shape[0]])

            def open_sums(banks):
                for b in banks:
                    mm(ps[:, b, :], zeros[:, 0:P], zeros[:], start=True, stop=False, skip_group_check=True)

            def norm(q, transposed=True):
                row = (0, 2, 1, 3, 4)[q]
                for half in range(2):
                    last = mm(ps[:, half, :], const("pick", 5)[:, row * P:row * P + P],
                              norm_w[:, half * 512:half * 512 + 512], start=True, stop=True)
                last.then_inc(norm_w_ps, 1)
                if transposed:
                    for t in range(2):
                        pe.wait_ge(normed, 2 * q + t + 1)
                        for k in range(KT):
                            last = transpose(ps[:, 2 + 2 * t + k // 4, (k % 4) * P:(k % 4) * P + P],
                                             wide[:, t, k * P:k * P + P])
                        last.then_inc(normed_ps, 1)
                    pe.wait_ge(xT_lo_ready, 4 * (q + 1))

            def mixer(L):
                base = MIX0[L]

                def attention_scores(g):
                    for odd in range(2):
                        for j in (odd, odd + 2):
                            hp, r = (4 * g + j) // 2, HEAD * odd
                            o = ps[:, 5 + j // 2, odd * SEQ:odd * SEQ + SEQ]
                            mm(o, msk[:, 0:P], msk[:, P:3 * P], start=True, stop=False)
                            mm(o, qT[r:r + HEAD, hp, P:SEQ], kT[r:r + HEAD, hp, :], start=False, stop=True)
                            o = ps[:, 7, j * P:j * P + P]
                            mm(o, msk[:, 0:P], msk[:, 2 * P:3 * P], start=True, stop=False)
                            last = mm(o, qT[r:r + HEAD, hp, 0:P], kT[r:r + HEAD, hp, 0:P], start=False, stop=True)
                        if odd == 0:
                            chain(last)
                    last.then_inc(scores_ps.sem, 1)

                def transpose_probs(g):
                    probs_ready.wait(pe, g + 1, L)
                    for j in range(4):
                        b, c = 5 + j // 2, (j % 2) * SEQ
                        transpose(ps[:, b, c:c + P], probs[:, j, 2 * P:3 * P])
                        transpose(ps[:, b, c + P:c + 2 * P], probs[:, j, 0:P])
                        last = transpose(ps[:, 7, j * P:j * P + P], probs[:, j, P:2 * P])
                    last.then_inc(probsT_ps.sem, 1)

                def attention_values(g):
                    probsT_ready0.wait(pe, g + 1, L)
                    probsT_ready1.wait(pe, g + 1, L)
                    if g == 1:
                        attn_hi.wait(pe, 1, L)
                        attn_lo.wait(pe, 1, L)
                    for j in range(4):
                        h, r, c = 4 * g + j, HEAD * (j % 2), (j // 2) * SEQ
                        mm(ps[r:r + HEAD, 4, c:c + SEQ], v_attn[:, 0, h * HEAD:h * HEAD + HEAD],
                           probsT[:, j, 0:SEQ], start=True, stop=True)
                        last = mm(ps[r:r + HEAD, 4, c + P:c + SEQ], v_attn[:, 1, h * HEAD:h * HEAD + HEAD],
                                  probsT[:, j, SEQ:SEQ + P], start=False, stop=True, skip_group_check=True)
                    last.then_inc(attn_ps.sem, 1)

                def chunk(c, n):
                    if c in (5, 6, 7):
                        for half in range(2):
                            channel_unit(n + half, 4 * half, 2 * (c % 2))
                    else:
                        for half in range(2):
                            wide_unit(n + half, xT_hi, xT_lo, 4 * half, [2 * (c % 2), 2 * (c % 2) + 1])

                n = base
                chunk(0, n)
                chunk(1, n + 2)
                rope_done.wait(pe, 1, L)
                chunk(2, n + 4)
                rope_done.wait(pe, 2, L)
                for c in range(4):
                    for t in range(2):
                        col = (c % 2) * SEQ + t * P
                        transpose(ps[:, 4 + c // 2, col:col + P], wide[:, t, c * P:c * P + P])
                        last = transpose(ps[:, 6 + c // 2, col:col + P], wide[:, t, 512 + c * P:512 + c * P + P])
                last.then_inc(qkT_ps.sem, 1)
                chunk(3, n + 6)
                qT_ready.wait(pe, 1, L)
                kT_ready.wait(pe, 1, L)
                attention_scores(0)
                v_copied.wait(pe, 1, L)
                chunk(4, n + 8)
                transpose_probs(0)
                rope_done.wait(pe, 3, L)
                chunk(5, n + 10)
                attention_values(0)
                attention_scores(1)
                v_copied.wait(pe, 2, L)
                chunk(6, n + 12)
                transpose_probs(1)
                conv_c_copied.wait(pe, 1, L)
                chunk(7, n + 14)
                attention_values(1)
                for c in range(2):
                    for t in range(2):
                        col = c * SEQ + t * P
                        transpose(ps[:, 5, col:col + P], ret_qk[:, t, c * P:c * P + P])
                        last = transpose(ps[:, 6, col:col + P], ret_qk[:, t, SEQ + c * P:SEQ + c * P + P])
                last.then_inc(ret_qkT_ps.sem, 1)
                conv_u_ready.wait(pe, 1, L)
                chunk(8, n + 16)
                rqT_ready.wait(pe, 1, L)
                rkT_ready.wait(pe, 1, L)
                for odd in range(2):
                    for h in (odd, odd + 2):
                        hp, r = h // 2, HEAD * odd
                        for t in range(2):
                            tok = slice(t * P, t * P + P)
                            mm(ps[:, 5 + t, h * P:h * P + P], rkT[r:r + HEAD, hp, tok], rqT[r:r + HEAD, hp, tok],
                               start=True, stop=True)
                        last = mm(ps[r:r + HEAD, 7, hp * P:hp * P + P], kzeta[:, h * HEAD:h * HEAD + HEAD],
                                  v_ret[:, 0, h * P:h * P + P], start=True, stop=True)
                    if odd == 0:
                        chain(last)
                last.then_inc(ret_scores_ps.sem, 1)
                conv_y_ready.wait(pe, 1, L)
                chunk(9, n + 18)
                decayed_ready.wait(pe, 1, L)
                for odd in range(2):
                    for h in (odd, odd + 2):
                        hp, r, cols = h // 2, HEAD * odd, slice(h * P, h * P + P)
                        for t in range(2):
                            mm(ps[:, 5 + t, cols], decayed[:, t * 512 + h * P:t * 512 + h * P + P],
                               v_ret[:, t, cols], start=True, stop=(t == 0))
                        last = mm(ps[:, 6, cols], rqxT[r:r + HEAD, hp, :], state[r:r + HEAD, hp * P:hp * P + P],
                                  start=False, stop=True)
                    if odd == 0:
                        chain(last)
                last.then_inc(ret_o_ps.sem, 1)
                ret_gate_ready.wait(pe, 1, L)
                chunk(10, n + 20)
                ret_y_ready.wait(pe, 1, L)
                attn_hi.wait(pe, 2, L)
                attn_lo.wait(pe, 2, L)
                for h in range(2):
                    deep_unit(base + BR_ATTN + h, yA_hi, yA_lo, 2 * h, SUMS, h == 0, h == 1)
                gate_ready.wait(pe, 2, L)
                for c in range(BT):
                    for t in range(2):
                        col = (c % 2) * SEQ + t * P
                        last = transpose(ps[:, c // 2, col:col + P], ret_o[:, t, c * P:c * P + P])
                last.then_inc(ret_yT_ps.sem, 1)
                chunk(11, n + 24)
                ret_hi.wait(pe, 1, L)
                ret_lo.wait(pe, 1, L)
                chunk(12, n + 26)
                merged.wait(pe, 1, L)
                conv_hi.wait(pe, 1, L)
                conv_lo.wait(pe, 1, L)
                for h in range(2):
                    deep_unit(base + BR_CONV + h, yC_hi, yC_lo, 2 * h, SUMS, h == 0, h == 1)
                gate_ready.wait(pe, 3, L)
                chunk(13, n + 30)
                gate_ready.wait(pe, 4, L)
                chunk(14, n + 32)
                merged.wait(pe, 2, L)
                for h in range(2):
                    deep_unit(base + BR_RET + h, yA_hi, yA_lo, 2 * h, SUMS, h == 0, h == 1)
                merged.wait(pe, 3, L)
                for t in range(2):
                    for half in range(2):
                        for k in range(4):
                            last = transpose(ps[:, 2 * t + half, k * P:k * P + P],
                                             wide[:, t, (4 * half + k) * P:(4 * half + k + 1) * P])
                        last.then_inc(mergedT_ps.sem, 1)
                mT_hi.wait(pe, 4, L)
                mT_lo.wait(pe, 4, L)
                for h in range(4):
                    deep_unit(base + OUT_PROJ + h, xT_hi, xT_lo, 2 * h, SUMS, h == 0, h == 3)

            def dense():
                open_sums(range(4, 8))
                for h in range(2):
                    wide_unit(DENSE0 + h, xT_hi, xT_lo, 4 * h, [0, 1])

                def turn(i):
                    pe.wait_ge(dn_ready, i)
                    for k in range(4):
                        for t in range(2):
                            last = transpose(ps[:, 2 + t, k * P:k * P + P], dn_act[:, t, k * P:k * P + P])
                    last.then_inc(dnT_ps, 1)

                with pe.Fori(0, 6) as i:
                    for h in range(2):
                        wide_unit(DENSE0 + 2 + h, xT_hi, xT_lo, 4 * h, [2, 3], i)
                    pe.wait_ge(dn_silu, i + 1)
                    wide_unit(DENSE0 + 4, xT_hi, xT_lo, 0, [0, 1], i)
                    turn(i + 1)
                    wide_unit(DENSE0 + 5, xT_hi, xT_lo, 4, [0, 1], i)
                    pe.wait_ge(dnT_hi_ready, i + 1)
                    pe.wait_ge(dnT_lo_ready, i + 1)
                    for h in range(2):
                        deep_unit(DENSE0 + 6 + h, dnT_hi, dnT_lo, 2 * h, SUMS, False, False, i)
                for h in range(2):
                    wide_unit(DENSE0 + 38 + h, xT_hi, xT_lo, 4 * h, [2, 3])
                turn(FCH)
                pe.wait_ge(dnT_hi_ready, FCH)
                pe.wait_ge(dnT_lo_ready, FCH)
                for h in range(2):
                    deep_unit(DENSE0 + 40 + h, dnT_hi, dnT_lo, 2 * h, SUMS, False, h == 1)

            def route():
                pe.wait_ge(router_lo, 1)
                for t in range(2):
                    tok = slice(t * P, t * P + P)
                    for k in range(KT):
                        last = three(ps[:, 6, t * NEXP:(t + 1) * NEXP], xT_hi[:, k, tok], xT_lo[:, k, tok],
                                     rt_hi[:, k, :], rt_lo[:, k, :], start=(k == 0), stop=(k == KT - 1))
                last.then_inc(logits_ps, 1)
                pe.wait_ge(chosen_ready, 1)
                mm(ps[:, 7, 0:8], const("before"), chosen[:, 0, :], start=True, stop=True)
                mm(ps[:, 7, 8:16], const("ones"), chosen[:, 0, :], start=True, stop=False)
                mm(ps[:, 7, 8:16], const("before"), chosen[:, 1, :], start=False, stop=True)
                mm(ps[:, 7, 16:24], const("ones"), chosen[:, 0, :], start=True, stop=False)
                mm(ps[:, 7, 16:24], const("ones"), chosen[:, 1, :], start=False, stop=True).then_inc(places_ps, 1)

            def gather(n):
                pe.wait_ge(put_in_ready, n)
                for k in range(KT):
                    o = ps[:, 5 + k // 4, (k % 4) * P:(k % 4) * P + P]
                    for t in range(2):
                        mm(o, tok_hi[:, t, k * P:k * P + P], put_in[:, t, :], start=(t == 0), stop=False)
                        last = mm(o, tok_lo[:, t, k * P:k * P + P], put_in[:, t, :], start=False, stop=(t == 1))
                last.then_inc(gathered_ps, 1)

            def experts(base, done):
                gather(done + 1)
                pe.wait_ge(ex_lo_ready, 2 * done + 2)
                for h in range(2):
                    wide_unit(base + h, ex_hi, ex_lo, 4 * h, [0])

                def expert(e, last_one):
                    r = e * FCH
                    f = r + done * FCH
                    for h in range(2):
                        wide_unit(base + 2 + h, ex_hi, ex_lo, 4 * h, [1], r)
                    pe.wait_ge(ex_added, e * 2 + 2 * done)
                    for t in range(2):
                        transpose(ps[:, 7, t * P:t * P + P], put_in[:, t, :].bitcast(F32))
                    for t in range(2):
                        last = mm(ps[:, 7, SEQ:SEQ + 1], put_in[:, t, :].bitcast(F32),
                                  share[:, t, bass.ds(e, 1)], start=(t == 0), stop=(t == 1))
                    last.then_inc(put_back_ps, 1)
                    open_sums([2, 3])

                    def turn(n):
                        pe.wait_ge(ex_ready, n)
                        for k in range(4):
                            last = transpose(ps[:, 4, k * P:k * P + P], ex_act[:, k * P:k * P + P])
                        last.then_inc(exT_ps, 1)

                    with pe.Fori(0, 6) as i:
                        v = r + i
                        pe.wait_ge(ex_silu, f + i + 1)
                        for h in range(2):
                            wide_unit(base + 4 + h, ex_hi, ex_lo, 4 * h, [0], v)
                        turn(f + i + 1)
                        for h in range(2):
                            wide_unit(base + 6 + h, ex_hi, ex_lo, 4 * h, [1], v)
                        pe.wait_ge(exT_lo_ready, f + i + 1)
                        for h in range(2):
                            deep_unit(base + 8 + h, exT_hi, exT_lo, 2 * h, EX_SUMS, False, False, v)
                    if not last_one:
                        gather(e + (done + 2))
                    turn(f + FCH)
                    pe.wait_ge(exT_lo_ready, f + FCH)
                    for h in range(2):
                        deep_unit(base + 40 + h, exT_hi, exT_lo, 2 * h, EX_SUMS, False, h == 1, r)
                    if not last_one:
                        pe.wait_ge(ex_lo_ready, e * 2 + (2 * done + 4))
                        for h in range(2):
                            wide_unit(base + FFN_UNITS + h, ex_hi, ex_lo, 4 * h, [0], r)
                    pe.wait_ge(ey_lo_ready, e + (done + 1))
                    pe.wait_ge(put_back_ready, e + (done + 1))
                    for t in range(2):
                        for half in range(2):
                            o, cols = ps[:, 4 + 2 * t + half, :], slice(half * 512, half * 512 + 512)
                            mm(o, put_back[:, t * P:t * P + P], ey_hi[:, cols], start=True, stop=False)
                            last = mm(o, put_back[:, t * P:t * P + P], ey_lo[:, cols], start=False, stop=True)
                        last.then_inc(back_ps, 1)

                with pe.Fori(0, NEXP - 1) as e:
                    expert(e, False)
                expert(NEXP - 1, True)

            pe.wait_ge(consts_in, 16 * 9)
            pe.wait_ge(zeros_set, 1)
            pe.wait_ge(masks_cast, 1)
            transpose(ps[:, 7, 0:40], chan_rows[:, :]).then_inc(chan_ps, 1)
            norm(0)
            mixer(0)
            norm(1)
            dense()
            norm(2)
            mixer(1)
            norm(3)
            route()
            pe.wait_ge(tok_lo_ready, 1)
            experts(MOE0, 0)
            pe.wait_ge(routed, 1)
            flag = pe.value_load(crowded[0:1, 0:1], min_val=0, max_val=1)
            with pe.If(flag > 0):
                for _ in range(3):
                    mm(ps[:, 0, :], zeros[:, 0:P], zeros[:], start=True, stop=True).then_inc(unit_used, 1)
                experts(CROWD0, NEXP)
            norm(4, transposed=False)

        @block.scalar
        def _(act):
            act.dma_start(cst[:], consts).then_inc(consts_in, 16)
            act.dma_start(norm_w[0:2, :], mix_norm_w).then_inc(consts_in, 16)
            act.dma_start(norm_w[2:4, :], ffn_norm_w).then_inc(consts_in, 16)
            act.dma_start(norm_w[4:5, :], final_norm_w.rearrange("(a d) -> a d", a=1)).then_inc(consts_in, 16)
            act.dma_start(chan_rows[0:8, :], ret_norm_w.rearrange("l (c p) -> (l c) p", p=P)).then_inc(consts_in, 16)
            act.dma_start(chan_rows[8:32, :], conv_w.rearrange("l j (c p) -> (l j c) p", p=P)).then_inc(consts_in, 16)
            act.dma_start(chan_rows[32:40, :], conv_b.rearrange("l (c p) -> (l c) p", p=P)).then_inc(consts_in, 16)
            act.dma_start(probs[:, 0, :], masks).then_inc(consts_in, 16)
            act.dma_start(router[:], moe_router[0].rearrange("(k p) e -> p k e", p=P)).then_inc(consts_in, 16)
            chain = Chain(scalar_chain, act)
            run = nc.scalar.activation

            def norm(q, before):
                for t in range(2):
                    before(t)
                    chain(run(wide[:, t, :], res[:, t, :], ACT.Square, accum_out=stat[:, t:t + 1]))
                    run(stat[:, 2 + t:3 + t], stat[:, t:t + 1], ACT.Sqrt, scale=1.0 / D, bias=EPS)\
                        .then_inc(root_ready, 1)
                if q < 4:
                    for t in range(2):
                        act.wait_ge(normed_ps, 2 * q + t + 1)
                        for half in range(2):
                            run(xT_hi[:, 4 * half:4 * half + 4, t * P:t * P + P],
                                ps[:, 2 + 2 * t + half, :].rearrange("p (k t) -> p k t", k=4), ACT.Copy)\
                                .then_inc(xT_hi_ready, 1)

            def added(n):
                return lambda t: act.wait_ge(res_added, n + t + 1)

            def mixer(L):
                base = MIX0[L]

                def exps(g):
                    max_ready.wait(act, g + 1, L)
                    for j in range(4):
                        run(probs[:, j, 0:SEQ], ps[:, 5 + j // 2, (j % 2) * SEQ:(j % 2) * SEQ + SEQ], ACT.Exp,
                            scale=HEAD ** -0.5, bias=stat[:, 16 + j:17 + j], accum_out=stat[:, 24 + j:25 + j])
                    for j in range(4):
                        last = run(probs[:, j, SEQ:SEQ + P], ps[:, 7, j * P:j * P + P], ACT.Exp,
                                   scale=HEAD ** -0.5, bias=stat[:, 20 + j:21 + j],
                                   accum_out=stat[:, 28 + j:29 + j])
                    last.then_inc(exp_done.sem, 1)

                def turn_probs(g):
                    probsT_ps.wait(act, g + 1, L)
                    run(probsT[:, :, 0:SEQ], ps[:, 5:7, :].rearrange("p b (j q) -> p (b j) q", j=2), ACT.Copy)\
                        .then_inc(probsT_ready0.sem, 1)

                def turn_attention(g):
                    attn_ps.wait(act, g + 1, L)
                    run(yA_hi[:, 2 * g:2 * g + 2, :], ps[:, 4, :].rearrange("p (c t) -> p c t", c=2), ACT.Copy)\
                        .then_inc(attn_hi.sem, 1)

                def sigmoid(c, half):
                    run(gates[:, :, half * 512:half * 512 + 512], ps[:, 2 * (c % 2):2 * (c % 2) + 2, :],
                        ACT.Sigmoid).then_inc(gate_ready.sem, 1)

                for m in range(3, MIX_UNITS):
                    if m == 39:
                        for b in range(4):
                            mergedT_ps.wait(act, b + 1, L)
                            run(xT_hi[:, 4 * (b % 2):4 * (b % 2) + 4, (b // 2) * P:(b // 2) * P + P],
                                ps[:, b, :].rearrange("p (k t) -> p k t", k=4), ACT.Copy).then_inc(mT_hi.sem, 1)
                    act.wait_ge(unit_used, base + m - 2)
                    if m == 8:
                        run(v_attn[:], ps[:, 0:2, :], ACT.Copy).then_inc(v_copied.sem, 1)
                        qkT_ps.wait(act, 1, L)
                        run(qT[:].rearrange("p c t -> p (c t)"), ps[:, 4:6, :].rearrange("p b n -> p (b n)"),
                            ACT.Copy).then_inc(qT_ready.sem, 1)
                    if m == 10:
                        exps(0)
                    if m == 12:
                        run(v_ret[:], ps[:, 0:2, :], ACT.Copy).then_inc(v_copied.sem, 1)
                        turn_probs(0)
                    if m == 14:
                        run(conv_c.rearrange("p c t -> p (c t)"), ps[:, 2:4, :].rearrange("p b n -> p (b n)"),
                            ACT.Copy).then_inc(conv_c_copied.sem, 1)
                        turn_attention(0)
                        exps(1)
                    if m == 16:
                        turn_probs(1)
                    if m == 18:
                        turn_attention(1)
                        ret_qkT_ps.wait(act, 1, L)
                        run(rqT[:].rearrange("p c t -> p (c t)"), ps[:, 5, :], ACT.Copy).then_inc(rqT_ready.sem, 1)
                        conv_y_ready.wait(act, 1, L)
                        run(yC_hi[:], conv, ACT.Copy).then_inc(conv_hi.sem, 1)
                    if m == 20:
                        run(ret_gate[:], ps[:, 0:2, :], ACT.Silu).then_inc(ret_gate_ready.sem, 1)
                    if m == 22:
                        ret_o_ps.wait(act, 1, L)
                        run(squares, ps[:, 5:7, :].rearrange("p b n -> p (b n)"), ACT.Square)\
                            .then_inc(ret_sq_done.sem, 1)
                        sigmoid(9, 0)
                    if m == 23:
                        ret_ss_ready.wait(act, 1, L)
                        run(stat[:, 40:48], stat[:, 32:40], ACT.Sqrt, scale=1.0 / P, bias=EPS)\
                            .then_inc(ret_root.sem, 1)
                    if m == 24:
                        sigmoid(10, 1)
                    if m == 26:
                        ret_yT_ps.wait(act, 1, L)
                        for c in range(BT):
                            last = run(yA_hi[:, c, :], ps[:, c // 2, (c % 2) * SEQ:(c % 2) * SEQ + SEQ], ACT.Copy,
                                       scale=chan[:, L * BT + c:L * BT + c + 1])
                        last.then_inc(ret_hi.sem, 1)
                    if m == 28:
                        merged.wait(act, 1, L)
                        sigmoid(11, 0)
                    if m == 30:
                        sigmoid(12, 1)
                    if m == 34:
                        merged.wait(act, 2, L)
                        sigmoid(13, 0)
                    if m == 36:
                        sigmoid(14, 1)
                    split_hi(act, base + m)
                for m in range(3):
                    split_hi(act, base + MIX_UNITS + m)

            def dense():
                def silu(n):
                    run(dn_sil[:], ps[:, 0:2, :], ACT.Silu).then_inc(dn_silu, 1)

                def turn(i):
                    act.wait_ge(dnT_ps, i)
                    run(dnT_hi[:].rearrange("p k (t n) -> p t k n", t=2),
                        ps[:, 2:4, :].rearrange("p t (k n) -> p t k n", k=4), ACT.Copy).then_inc(dnT_hi_ready, 1)

                split_hi(act, DENSE0 + 3)
                act.wait_ge(unit_used, DENSE0 + 2)
                silu(0)
                split_hi(act, DENSE0 + 4)
                with act.Fori(0, 6) as i:
                    split_hi(act, DENSE0 + 5, i)
                    split_hi(act, DENSE0 + 6, i)
                    turn(i + 1)
                    split_hi(act, DENSE0 + 7, i)
                    act.wait_ge(unit_used, i * RAW + (DENSE0 + 6))
                    silu(i + 1)
                    for j in (8, 9, 10):
                        split_hi(act, DENSE0 + j, i)
                split_hi(act, DENSE0 + 41)
                split_hi(act, DENSE0 + 42)
                turn(FCH)
                split_hi(act, DENSE0 + 43)
                split_hi(act, DENSE0 + 44)

            def experts(base, done):
                def take_gathered(n):
                    act.wait_ge(gathered_ps, n)
                    for half in range(2):
                        run(ex_hi[:, 4 * half:4 * half + 4, :],
                            ps[:, 5 + half, :].rearrange("p (k t) -> p k t", k=4), ACT.Copy).then_inc(ex_hi_ready, 1)

                def expert(e, last_one):
                    r = e * FCH
                    f = r + done * FCH

                    def silu(n, unit):
                        act.wait_ge(unit_used, unit)
                        act.wait_ge(ex_ready, n)
                        run(ex_sil[:], ps[:, 0, :], ACT.Silu).then_inc(ex_silu, 1)

                    def turn(n):
                        act.wait_ge(exT_ps, n)
                        run(exT_hi[:], ps[:, 4, :].rearrange("p (k t) -> p k t", k=4), ACT.Copy)\
                            .then_inc(exT_hi_ready, 1)

                    split_hi(act, base + 3, r)
                    silu(f, r * RAW + (base + 2))
                    for j in (4, 5, 6):
                        split_hi(act, base + j, r)
                    act.wait_ge(put_back_ps, e + (done + 1))
                    run(put_back[:], ps[:, 7, 0:SEQ], ACT.Copy).then_inc(put_back_ready, 1)
                    with act.Fori(0, 6) as i:
                        v = r + i
                        split_hi(act, base + 7, v)
                        turn(f + i + 1)
                        silu(f + i + 1, v * RAW + (base + 6))
                        for j in (8, 9, 10, 11, 12):
                            split_hi(act, base + j, v)
                    if not last_one:
                        take_gathered(e + (done + 2))
                    turn(f + FCH)
                    split_hi(act, base + 43, r)
                    act.wait_ge(unit_used, r * RAW + (base + FFN_UNITS))
                    act.wait_ge(slot_w_ready, e + (done + 1))
                    run(ey_hi[:], ps[:, 2:4, :].rearrange("p b n -> p (b n)"), ACT.Copy, scale=slot_w[:, 0:1])\
                        .then_inc(ey_hi_ready, 1)
                    split_hi(act, base + 44, r)

                if done:
                    for j in range(3):
                        split_hi(act, base + j)
                take_gathered(done + 1)
                with act.Fori(0, NEXP - 1) as e:
                    expert(e, False)
                expert(NEXP - 1, True)

            for m in range(3):
                split_hi(act, m)
            act.wait_ge(consts_in, 16 * 9)
            run(msk[:], probs[:, 0, :], ACT.Copy).then_inc(masks_cast, 1)
            norm(0, lambda t: act.wait_ge(x_in, 16))
            mixer(0)
            norm(1, added(0))
            dense()
            norm(2, added(2))
            mixer(1)
            norm(3, added(4))
            run(rt_hi[:], router[:], ACT.Copy).then_inc(router_hi, 1)
            act.wait_ge(normed, 8)
            run(tok_hi[:], wide[:], ACT.Copy).then_inc(tok_hi_ready, 1)
            act.wait_ge(gap_ready, 1)
            run(prob[:, 2:4], prob[:, 0:2], ACT.Exp).then_inc(gap_exp, 1)
            experts(MOE0, 0)
            act.wait_ge(routed, 1)
            flag = act.value_load(crowded[0:1, 0:1], min_val=0, max_val=1)
            with act.If(flag > 0):
                experts(CROWD0, NEXP)
            norm(4, lambda t: act.wait_ge(res_final, 1))

        @block.vector
        def _(dve):
            chain = Chain(vector_chain, dve)
            v = nc.vector

            def rsqrt(o, root, sum_sq, scale, tmp):
                chain(v.reciprocal(o, root))
                chain(v.tensor_scalar(tmp, sum_sq, -0.5 * scale, -0.5 * EPS, ALU.mult, ALU.add))
                chain(v.tensor_tensor(tmp, tmp, o, ALU.mult))
                chain(v.tensor_tensor(tmp, tmp, o, ALU.mult))
                chain(v.scalar_tensor_tensor(o, tmp, 1.5, o, ALU.add, ALU.mult))

            def norm(q):
                for t in range(2):
                    dve.wait_ge(root_ready, 2 * q + t + 1)
                    rsqrt(stat[:, 4 + t:5 + t], stat[:, 2 + t:3 + t], stat[:, t:t + 1], 1.0 / D,
                          stat[:, 6 + t:7 + t])
                    dve.wait_ge(norm_w_ps, q + 1)
                    v.scalar_tensor_tensor(wide[:, t, :], res[:, t, :], stat[:, 4 + t:5 + t],
                                           ps[:, 0:2, :].rearrange("p b n -> p (b n)"), ALU.mult, ALU.mult)\
                        .then_inc(normed if q < 4 else out_ready, 1)
                if q < 4:
                    for t in range(2):
                        for half in range(2):
                            dve.wait_ge(xT_hi_ready, 4 * q + 2 * t + half + 1)
                            part = (slice(None), slice(4 * half, 4 * half + 4), slice(t * P, t * P + P))
                            v.tensor_tensor(xT_lo[part],
                                            ps[:, 2 + 2 * t + half, :].rearrange("p (k t) -> p k t", k=4),
                                            xT_hi[part].bitcast(F32), ALU.subtract).then_inc(xT_lo_ready, 1)

            def add_residual():
                for t in range(2):
                    v.tensor_tensor(res[:, t, :], res[:, t, :],
                                    ps[:, 4 + 2 * t:6 + 2 * t, :].rearrange("p b n -> p (b n)"), ALU.add)\
                        .then_inc(res_added, 1)

            def mixer(L):
                base = MIX0[L]

                def rope(k, dst, bank):
                    if k or L:
                        rope_done.wait(dve, k, L)
                    for t in range(2):
                        heads = ps[:, bank + t, :].rearrange("p (h d) -> p h d", h=8)
                        cos = const("cos")[:, t * HEAD:t * HEAD + HEAD]
                        sin = const("sin")[:, t * HEAD:t * HEAD + HEAD]
                        o = dst(t).rearrange("p (h d) -> p h d", h=8)
                        tmp = rope_tmp.rearrange("p (h d) -> p h d", h=8)
                        half = HEAD // 2
                        v.tensor_tensor(o, heads, cos.unsqueeze(1).to_broadcast([P, 8, HEAD]), ALU.mult)
                        v.tensor_tensor(tmp[:, :, 0:half], heads[:, :, half:HEAD],
                                        sin[:, 0:half].unsqueeze(1).to_broadcast([P, 8, half]), ALU.mult)
                        chain(v.tensor_tensor(tmp[:, :, half:HEAD], heads[:, :, 0:half],
                                              sin[:, half:HEAD].unsqueeze(1).to_broadcast([P, 8, half]), ALU.mult))
                        last = v.tensor_tensor(dst(t), dst(t), rope_tmp, ALU.add)
                        if t == 0:
                            chain(last)
                    last.then_inc(rope_done.sem, 1)

                def row_max(g):
                    scores_ps.wait(dve, g + 1, L)
                    v.tensor_reduce(stat[:, 8:12], ps[:, 5:7, :].rearrange("p b (j q) -> p (b j) q", j=2),
                                    AX_X, ALU.max)
                    chain(v.tensor_reduce(stat[:, 12:16], ps[:, 7, :].rearrange("p (j q) -> p j q", j=4),
                                          AX_X, ALU.max))
                    v.tensor_scalar(stat[:, 16:24], stat[:, 8:16], -HEAD ** -0.5, None, ALU.mult)\
                        .then_inc(max_ready.sem, 1)

                def normalise(g):
                    exp_done.wait(dve, g + 1, L)
                    chain(v.reciprocal(stat[:, 24:32], stat[:, 24:32]))
                    v.tensor_tensor(probs[:, :, 0:SEQ], probs[:, :, 0:SEQ],
                                    stat[:, 24:28].unsqueeze(2).to_broadcast([P, 4, SEQ]), ALU.mult)
                    v.tensor_tensor(probs[:, :, SEQ:SEQ + P], probs[:, :, SEQ:SEQ + P],
                                    stat[:, 28:32].unsqueeze(2).to_broadcast([P, 4, P]), ALU.mult)\
                        .then_inc(probs_ready.sem, 1)

                def turn_probs(g):
                    probsT_ps.wait(dve, g + 1, L)
                    v.tensor_copy(probsT[:, :, SEQ:SEQ + P], ps[:, 7, :].rearrange("p (j q) -> p j q", j=4))\
                        .then_inc(probsT_ready1.sem, 1)

                def turn_attention(g):
                    attn_hi.wait(dve, g + 1, L)
                    v.tensor_tensor(yA_lo[:, 2 * g:2 * g + 2, :], ps[:, 4, :].rearrange("p (c t) -> p c t", c=2),
                                    yA_hi[:, 2 * g:2 * g + 2, :].bitcast(F32), ALU.subtract)\
                        .then_inc(attn_lo.sem, 1)

                def merge(b):
                    gate_ready.wait(dve, 2 * b + 2, L)
                    flat = ps[:, 4:8, :].rearrange("p b n -> p (b n)")
                    g = gates[:].rearrange("p t d -> p (t d)")
                    m = wide[:].rearrange("p t d -> p (t d)")
                    if b == 0:
                        v.tensor_tensor(m, flat, g, ALU.mult).then_inc(merged.sem, 1)
                    else:
                        chain(v.tensor_tensor(g, flat, g, ALU.mult))
                        v.tensor_tensor(m, m, g, ALU.add).then_inc(merged.sem, 1)

                for m in range(3, MIX_UNITS):
                    if m == 39:
                        for b in range(4):
                            mT_hi.wait(dve, b + 1, L)
                            part = (slice(None), slice(4 * (b % 2), 4 * (b % 2) + 4), slice((b // 2) * P, (b // 2) * P + P))
                            v.tensor_tensor(xT_lo[part], ps[:, b, :].rearrange("p (k t) -> p k t", k=4),
                                            xT_hi[part].bitcast(F32), ALU.subtract).then_inc(mT_lo.sem, 1)
                    dve.wait_ge(unit_used, base + m - 2)
                    if m == 4:
                        rope(0, lambda t: wide[:, t, 0:512], 0)
                    if m == 6:
                        rope(1, lambda t: wide[:, t, 512:1024], 2)
                    if m == 8:
                        qkT_ps.wait(dve, 1, L)
                        v.tensor_copy(kT[:].rearrange("p c t -> p (c t)"),
                                      ps[:, 6:8, :].rearrange("p b n -> p (b n)")).then_inc(kT_ready.sem, 1)
                    if m == 10:
                        row_max(0)
                        rope(2, lambda t: ret_qk[:, t, :], 2)
                    if m == 11:
                        normalise(0)
                    if m == 12:
                        turn_probs(0)
                    if m == 14:
                        row_max(1)
                        turn_attention(0)
                    if m == 15:
                        normalise(1)
                    if m == 16:
                        conv_c_copied.wait(dve, 1, L)
                        chain(v.tensor_tensor(uT[:, :, 2:SEQ + 2], conv_c,
                                              ps[:, 0:2, :].rearrange("p b (c t) -> p (b c) t", c=2), ALU.mult))
                        turn_probs(1)
                        w = lambda j, c: chan[:, 8 + L * 12 + j * 4 + c:9 + L * 12 + j * 4 + c]
                        for c in range(BT):
                            last = v.tensor_scalar(conv[:, c, :], uT[:, c, 2:SEQ + 2], w(2, c),
                                                   chan[:, 32 + L * 4 + c:33 + L * 4 + c], ALU.mult, ALU.add)
                        chain(last)
                        for c in range(BT):
                            last = v.scalar_tensor_tensor(conv[:, c, :], uT[:, c, 1:SEQ + 1], w(1, c),
                                                          conv[:, c, :], ALU.mult, ALU.add)
                        chain(last)
                        for c in range(BT):
                            last = v.scalar_tensor_tensor(conv[:, c, :], uT[:, c, 0:SEQ], w(0, c),
                                                          conv[:, c, :], ALU.mult, ALU.add)
                        last.then_inc(conv_u_ready.sem, 1)
                    if m == 18:
                        conv_u_ready.wait(dve, 1, L)
                        v.tensor_tensor(conv, conv, ps[:, 2:4, :].rearrange("p b (c t) -> p (b c) t", c=2),
                                        ALU.mult).then_inc(conv_y_ready.sem, 1)
                        turn_attention(1)
                        v.tensor_tensor(kzeta[:].rearrange("p (h d) -> p h d", h=RET_HEADS),
                                        ret_qk[:, 0, SEQ:2 * SEQ].rearrange("p (h d) -> p h d", h=RET_HEADS),
                                        const("zeta").unsqueeze(2).to_broadcast([P, RET_HEADS, HEAD]), ALU.mult)
                        ret_qkT_ps.wait(dve, 1, L)
                        v.tensor_copy(rkT[:].rearrange("p c t -> p (c t)"), ps[:, 6, :])
                        rqT_ready.wait(dve, 1, L)
                        v.tensor_tensor(rqxT[:], rqT[:, :, P:SEQ], const("xi").rearrange("p (c t) -> p c t", c=2),
                                        ALU.mult).then_inc(rkT_ready.sem, 1)
                        conv_hi.wait(dve, 1, L)
                        v.tensor_tensor(yC_lo[:], conv, yC_hi[:].bitcast(F32), ALU.subtract)\
                            .then_inc(conv_lo.sem, 1)
                    if m == 20:
                        ret_scores_ps.wait(dve, 1, L)
                        v.tensor_copy(state[:], ps[:, 7, 0:2 * P])
                        v.tensor_tensor(decayed.rearrange("p (t n) -> p t n", t=2), ps[:, 5:7, :],
                                        const("decay").unsqueeze(1).to_broadcast([P, 2, 512]), ALU.mult)\
                            .then_inc(decayed_ready.sem, 1)
                    if m == 22:
                        ret_sq_done.wait(dve, 1, L)
                        v.tensor_reduce(stat[:, 32:40], squares.rearrange("p (h d) -> p h d", d=P), AX_X, ALU.add)\
                            .then_inc(ret_ss_ready.sem, 1)
                    if m == 23:
                        ret_root.wait(dve, 1, L)
                        rsqrt(stat[:, 48:56], stat[:, 40:48], stat[:, 32:40], 1.0 / P, stat[:, 56:64])
                        ret_gate_ready.wait(dve, 1, L)
                        chain(v.tensor_tensor(ret_o[:].rearrange("p t (h d) -> p (t h) d", d=P),
                                              ps[:, 5:7, :].rearrange("p t (h d) -> p (t h) d", d=P),
                                              stat[:, 48:56].unsqueeze(2).to_broadcast([P, 8, P]), ALU.mult))
                        v.tensor_tensor(ret_o[:], ret_o[:], ret_gate[:], ALU.mult).then_inc(ret_y_ready.sem, 1)
                    if m == 26:
                        merge(0)
                        ret_hi.wait(dve, 1, L)
                        for c in range(BT):
                            last = v.scalar_tensor_tensor(
                                yA_lo[:, c, :], ps[:, c // 2, (c % 2) * SEQ:(c % 2) * SEQ + SEQ],
                                chan[:, L * BT + c:L * BT + c + 1], yA_hi[:, c, :].bitcast(F32),
                                ALU.mult, ALU.subtract)
                        last.then_inc(ret_lo.sem, 1)
                    if m == 32:
                        merge(1)
                    if m == 38:
                        merge(2)
                    split_lo(dve, base + m)
                for m in range(2):
                    split_lo(dve, base + MIX_UNITS + m)
                dve.wait_ge(unit_used, base + MIX_UNITS)
                add_residual()
                split_lo(dve, base + MIX_UNITS + 2)

            def dense():
                def activate(i):
                    dve.wait_ge(dn_silu, i)
                    v.tensor_tensor(dn_act[:], dn_sil[:], ps[:, 2:4, :], ALU.mult).then_inc(dn_ready, 1)

                def turn(i):
                    dve.wait_ge(dnT_hi_ready, i)
                    for t in range(2):
                        tok = slice(t * P, t * P + P)
                        last = v.tensor_tensor(dnT_lo[:, :, tok],
                                               ps[:, 2 + t, :].rearrange("p (k n) -> p k n", k=4),
                                               dnT_hi[:, :, tok].bitcast(F32), ALU.subtract)
                    last.then_inc(dnT_lo_ready, 1)

                split_lo(dve, DENSE0 + 3)
                split_lo(dve, DENSE0 + 4)
                with dve.Fori(0, 6) as i:
                    split_lo(dve, DENSE0 + 5, i)
                    dve.wait_ge(unit_used, i * RAW + (DENSE0 + 4))
                    activate(i + 1)
                    split_lo(dve, DENSE0 + 6, i)
                    turn(i + 1)
                    for j in (7, 8, 9, 10):
                        split_lo(dve, DENSE0 + j, i)
                split_lo(dve, DENSE0 + 41)
                dve.wait_ge(unit_used, DENSE0 + 40)
                activate(FCH)
                split_lo(dve, DENSE0 + 42)
                turn(FCH)
                split_lo(dve, DENSE0 + 43)
                dve.wait_ge(unit_used, DENSE0 + FFN_UNITS)
                add_residual()
                split_lo(dve, DENSE0 + 44)

            def route():
                dve.wait_ge(router_hi, 1)
                v.tensor_tensor(rt_lo[:], router[:], rt_hi[:].bitcast(F32), ALU.subtract).then_inc(router_lo, 1)
                dve.wait_ge(tok_hi_ready, 1)
                v.tensor_tensor(tok_lo[:], wide[:], tok_hi[:].bitcast(F32), ALU.subtract).then_inc(tok_lo_ready, 1)
                dve.wait_ge(logits_ps, 1)
                chain(v.tensor_copy(logits[:].rearrange("p t e -> p (t e)"), ps[:, 6, 0:2 * NEXP]))
                for t in range(2):
                    chain(v.max(top[:, t, :], logits[:, t, :]))
                    chain(v.max_index(top_at[:, t, :], top[:, t, :], logits[:, t, :]))
                chain(v.tensor_copy(top_f[:], top_at[:]))
                v.tensor_tensor(prob[:, 0:2], top[:, :, 1], top[:, :, 0], ALU.subtract).then_inc(gap_ready, 1)
                eight = const("iota")[:, 0:NEXP]
                for t in range(2):
                    v.tensor_scalar(first[:, t, :], eight, top_f[:, t, 0:1], None, ALU.is_equal)
                    chain(v.tensor_scalar(second[:, t, :], eight, top_f[:, t, 1:2], None, ALU.is_equal))
                v.tensor_tensor(chosen[:], first[:], second[:], ALU.add).then_inc(chosen_ready, 1)
                dve.wait_ge(gap_exp, 1)
                chain(v.tensor_scalar(prob[:, 4:6], prob[:, 2:4], 1.0, None, ALU.add))
                chain(v.reciprocal(prob[:, 4:6], prob[:, 4:6]))
                chain(v.tensor_tensor(prob[:, 6:8], prob[:, 2:4], prob[:, 4:6], ALU.mult))
                for t in range(2):
                    chain(v.tensor_scalar(share[:, t, :], first[:, t, :], prob[:, 4 + t:5 + t], None, ALU.mult))
                    chain(v.scalar_tensor_tensor(share[:, t, :], second[:, t, :], prob[:, 6 + t:7 + t],
                                                 share[:, t, :], ALU.mult, ALU.add))
                dve.wait_ge(chosen_ready, 1)
                dve.wait_ge(places_ps, 1)
                mine = slot_of[:]
                chain(v.scalar_tensor_tensor(mine, ps[:, 7, 0:16].rearrange("p (t e) -> p t e", t=2), 1.0,
                                             chosen[:], ALU.add, ALU.mult))
                chain(v.tensor_scalar(mine, mine, -1.0, None, ALU.add))
                chain(v.tensor_reduce(stat[:, 8:9], ps[:, 7, 16:24], AX_X, ALU.max))
                v.tensor_scalar(crowded[:], stat[:, 8:9], float(P), None, ALU.is_gt).then_inc(routed, 1)

            def one_hot(e):
                for t in range(2):
                    last = v.tensor_scalar(put_in[:, t, :], const("iota"), slot_of[:, t, bass.ds(e, 1)], None,
                                           ALU.is_equal)
                last.then_inc(put_in_ready, 1)

            def experts(base, done):
                def take_gathered(n):
                    for half in range(2):
                        dve.wait_ge(ex_hi_ready, n + half + 1)
                        v.tensor_tensor(ex_lo[:, 4 * half:4 * half + 4, :],
                                        ps[:, 5 + half, :].rearrange("p (k t) -> p k t", k=4),
                                        ex_hi[:, 4 * half:4 * half + 4, :].bitcast(F32), ALU.subtract)\
                            .then_inc(ex_lo_ready, 1)

                def expert(e, last_one):
                    r = e * FCH
                    f = r + done * FCH

                    def activate(n, unit):
                        dve.wait_ge(unit_used, unit)
                        dve.wait_ge(ex_silu, n)
                        v.tensor_tensor(ex_act[:], ex_sil[:], ps[:, 1, :], ALU.mult).then_inc(ex_ready, 1)

                    def turn(n):
                        dve.wait_ge(exT_hi_ready, n)
                        v.tensor_tensor(exT_lo[:], ps[:, 4, :].rearrange("p (k t) -> p k t", k=4),
                                        exT_hi[:].bitcast(F32), ALU.subtract).then_inc(exT_lo_ready, 1)

                    split_lo(dve, base + 4, r)
                    split_lo(dve, base + 5, r)
                    activate(f + 1, r * RAW + (base + 4))
                    split_lo(dve, base + 6, r)
                    dve.wait_ge(put_back_ready, e + (done + 1))
                    v.tensor_copy(slot_w[:], ps[:, 7, SEQ:SEQ + 1]).then_inc(slot_w_ready, 1)
                    if not last_one:
                        one_hot(e + 1)
                    with dve.Fori(0, 6) as i:
                        w = r + i
                        split_lo(dve, base + 7, w)
                        turn(f + i + 1)
                        split_lo(dve, base + 8, w)
                        split_lo(dve, base + 9, w)
                        activate(f + i + 2, w * RAW + (base + 8))
                        split_lo(dve, base + 10, w)
                        split_lo(dve, base + 11, w)
                        split_lo(dve, base + 12, w)
                    if not last_one:
                        take_gathered(e * 2 + (2 * done + 2))
                    turn(f + FCH)
                    split_lo(dve, base + 43, r)
                    dve.wait_ge(ey_hi_ready, e + (done + 1))
                    v.scalar_tensor_tensor(ey_lo[:], ps[:, 2:4, :].rearrange("p b n -> p (b n)"), slot_w[:, 0:1],
                                           ey_hi[:].bitcast(F32), ALU.mult, ALU.subtract).then_inc(ey_lo_ready, 1)
                    if not last_one:
                        split_lo(dve, base + 44, r)
                        split_lo(dve, base + 45, r)
                    for t in range(2):
                        dve.wait_ge(back_ps, e * 2 + (2 * done + t + 1))
                        v.tensor_tensor(res[:, t, :], res[:, t, :],
                                        ps[:, 4 + 2 * t:6 + 2 * t, :].rearrange("p b n -> p (b n)"), ALU.add)\
                            .then_inc(ex_added, 1)
                    if last_one:
                        split_lo(dve, base + 44, r)

                one_hot(0)
                if done:
                    for j in range(3):
                        split_lo(dve, base + j)
                take_gathered(2 * done)
                split_lo(dve, base + 3)
                with dve.Fori(0, NEXP - 1) as e:
                    expert(e, False)
                expert(NEXP - 1, True)

            dve.wait_ge(consts_in, 16 * 9)
            dve.wait_ge(pads_set, 1)
            dve.wait_ge(chan_ps, 1)
            chain(v.tensor_copy(chan[:], ps[:, 7, 0:40]))
            for m in range(3):
                split_lo(dve, m)
            norm(0)
            mixer(0)
            norm(1)
            dense()
            norm(2)
            mixer(1)
            norm(3)
            route()
            experts(MOE0, 0)
            dve.wait_ge(ex_added, 2 * NEXP)
            flag = dve.value_load(crowded[0:1, 0:1], min_val=0, max_val=1)
            with dve.If(flag > 0):
                v.tensor_scalar(slot_of[:], slot_of[:], -float(P), None, ALU.add).then_inc(slots_moved, 1)
                dve.wait_ge(slots_moved, 1)
                experts(CROWD0, NEXP)
                dve.wait_ge(ex_added, 4 * NEXP)
                v.memset(stat[:, 8:9], 0.0).then_inc(res_final, 1)
            with dve.Else():
                v.memset(stat[:, 8:9], 0.0).then_inc(res_final, 1)
            norm(4)


_INS = ["x", "mix_norm_w", "w_in", "conv_w", "conv_b", "ret_norm_w", "w_br_attn", "w_br_conv", "w_br_ret",
        "w_out", "ffn_norm_w", "dense_w_gate", "dense_w_up", "dense_w_down", "moe_router", "moe_w_gate",
        "moe_w_up", "moe_w_down", "final_norm_w"]


def kernel(**inputs):
    import numpy as _np
    import concourse.bacc as _bacc
    from concourse import mybir as _mybir
    from concourse.bass_utils import run_bass_kernel_spmd as _run

    nc = _bacc.Bacc("TRN2", target_bir_lowering=False, num_devices=1)
    consts, masks = shape_constants()
    arrays, args = {}, []
    for name, a in [(n, inputs[n]) for n in _INS] + [("consts", consts), ("masks", masks)]:
        a = _np.ascontiguousarray(a)
        arrays[f"in_{name}_dram"] = a
        args.append(nc.dram_tensor(f"in_{name}_dram", a.shape, _mybir.dt.from_np(a.dtype), kind="ExternalInput").ap())
    args.append(nc.dram_tensor("out_0_dram", (1, SEQ, D), F32, kind="ExternalOutput").ap())
    hybrid_trunk_kernel(nc, *args)
    r = _run(nc, [arrays], core_ids=[0])
    return r.results[0]["out_0_dram"]
```

```python
from contextlib import ExitStack

import numpy as np

import concourse.bass as bass
from concourse import mybir

F32 = mybir.dt.float32
F32R = mybir.dt.float32r
BF16 = mybir.dt.bfloat16
I32 = mybir.dt.int32
U32 = mybir.dt.uint32
ALU = mybir.AluOpType
ACT = mybir.ActivationFunctionType
AX_X = mybir.AxisListType.X

P = 128
DEPTH = 2
SEQ = 256
D = 1024
KT = D // P
HEAD = 64
EPS = 1e-6
ATTN_HEADS = 8
RET_HEADS = 4
BR_W = 512
BT = BR_W // P
FF = 3584
FCH = FF // 512
NEXP = 8

UNIT = 2048
RAW = 6
SPLIT = 3
MIX_UNITS = 40
FFN_UNITS = 6 * FCH
CHUNKS = (0, 1, 2, 6, 7, 4, 5, 3, 8, 9, 10, 11, 12, 13, 14)
BR_ATTN, BR_CONV, BR_RET, OUT_PROJ = 22, 28, 32, 36

CONST_PARTS = (("ident", 128), ("cos", 128), ("sin", 128), ("decay", 512), ("xi", 256), ("zeta", 4),
               ("iota", 128), ("before", 128), ("ones", 128), ("pick", 640))
CONST_AT = {}
CONST_W = 0
for _name, _w in CONST_PARTS:
    CONST_AT[_name] = (CONST_W, CONST_W + _w)
    CONST_W += _w


def shape_constants():
    c = np.zeros((P, CONST_W), np.float32)

    def put(name, a):
        lo, hi = CONST_AT[name]
        c[:a.shape[0], lo:hi] = a

    inv_freq = (1.0 / (np.float32(10000.0) ** (np.arange(0, HEAD, 2, dtype=np.float32) / HEAD))).astype(np.float32)
    ang = np.arange(SEQ, dtype=np.float32)[:, None] * inv_freq[None, :]
    cos, sin = np.cos(ang), np.sin(ang)
    tokens = lambda a: a.reshape(2, P, HEAD).transpose(1, 0, 2).reshape(P, 2 * HEAD)
    put("cos", tokens(np.concatenate([cos, cos], 1)))
    put("sin", tokens(np.concatenate([-sin, sin], 1)))
    log_g = np.log1p(-np.exp2(-5.0 - np.arange(RET_HEADS, dtype=np.float32))).astype(np.float32)
    n = np.arange(P, dtype=np.float32)
    diff = n[None, :] - n[:, None]
    scale = np.float32(HEAD ** -0.5)
    decay = np.where(diff[None] >= 0, np.exp(np.maximum(diff, 0)[None] * log_g[:, None, None]), 0) * scale
    put("decay", decay.transpose(1, 0, 2).reshape(P, RET_HEADS * P))
    xi = np.exp((n + 1)[None, :] * log_g[:, None])
    put("xi", np.repeat(xi.reshape(2, 2, P), HEAD, axis=1).reshape(2, P, P).transpose(1, 0, 2).reshape(P, 2 * P))
    put("zeta", (np.exp((P - 1 - n)[None, :] * log_g[:, None]) * scale).T)
    put("ident", np.eye(P))
    put("iota", np.tile(n, (P, 1)))
    put("before", np.triu(np.ones((P, P)), 1))
    put("ones", np.ones((P, P)))
    put("pick", np.kron(np.eye(5), np.ones((1, P))))
    masks = np.zeros((P, 3 * P), np.float32)
    masks[:, :P] = np.eye(P)
    masks[:, 2 * P:] = np.triu(np.full((P, P), -1e30), 1)
    return c, masks


class Signal:

    def __init__(self, sem, per_layer=0):
        self.sem, self.per_layer = sem, per_layer

    def wait(self, eng, k, layer=0):
        eng.wait_ge(self.sem, layer * self.per_layer + k)


class Chain:

    def __init__(self, sem, eng):
        self.sem, self.eng, self.n = sem, eng, 0

    def __call__(self, ins):
        self.n += 1
        ins.then_inc(self.sem, 1)
        self.eng.wait_ge(self.sem, self.n)


def hybrid_trunk_kernel(nc, x, mix_norm_w, w_in, conv_w, conv_b, ret_norm_w, w_br_attn, w_br_conv,
                        w_br_ret, w_out, ffn_norm_w, dense_w_gate, dense_w_up, dense_w_down,
                        moe_router, moe_w_gate, moe_w_up, moe_w_down, final_norm_w,
                        consts, masks, out):
    ctx = ExitStack()
    with ctx:
        at = [(nc.sbuf_base + 31) // 32 * 32]

        def place(name, shape, dt):
            size = int(np.prod(shape[1:])) * (2 if dt == BF16 else 4)
            t = nc.alloc_sbuf_tensor_at(name, shape, dt, offset=at[0])
            at[0] += (size + 31) // 32 * 32
            return t

        raw = place("raw", [P, RAW, UNIT], F32)
        w_hi = place("w_hi", [P, SPLIT, UNIT], F32R)
        w_lo = place("w_lo", [P, SPLIT, UNIT], F32R)
        res = place("res", [P, 2, D], F32)
        wide = place("wide", [P, 2, D], F32)
        cst = place("cst", [P, CONST_W], F32)
        msk = place("msk", [P, 3 * P], BF16)
        zeros = place("zeros", [P, 512], BF16)
        norm_w = place("norm_w", [5, D], F32)
        chan_rows = place("chan_rows", [40, P], F32)
        chan = place("chan", [P, 40], F32)
        stat = place("stat", [P, 64], F32)
        spare = place("spare", [P, 9], F32)
        router = place("router", [P, KT, NEXP], F32)
        rt = place("rt", [P, KT, 2 * NEXP], F32R)
        region = at[0]
        xT_hi = place("xT_hi", [P, KT, SEQ], F32R)
        xT_lo = place("xT_lo", [P, KT, SEQ], F32R)
        after_xT = at[0]
        ret_qk = place("ret_qk", [P, 2, 512], F32)
        gates_at = at[0]
        qT = place("qT", [P, BT, SEQ], F32)
        kT = place("kT", [P, BT, SEQ], F32)
        v_at = at[0]
        v_attn = place("v_attn", [P, 2, BR_W], F32)
        probs = place("probs", [P, 4, 384], F32)
        probsT = place("probsT", [P, 4, 384], F32)
        yA_hi = place("yA_hi", [P, BT, SEQ], F32R)
        yA_lo = place("yA_lo", [P, BT, SEQ], F32R)
        yC_hi = place("yC_hi", [P, BT, SEQ], F32R)
        yC_lo = place("yC_lo", [P, BT, SEQ], F32R)
        uT = place("uT", [P, BT, SEQ + 2], F32)
        rqT = place("rqT", [P, 2, SEQ], F32)
        rkT = place("rkT", [P, 2, SEQ], F32)
        rqxT = place("rqxT", [P, 2, P], F32)
        kzeta = place("kzeta", [P, 4 * HEAD], F32)
        state = place("state", [P, 2 * P], F32)
        v_ret = place("v_ret", [P, 2, BR_W], F32)
        ret_gate = place("ret_gate", [P, 2, BR_W], F32)
        assert at[0] <= nc.sbuf_usable_end, at[0]
        gates = nc.alloc_sbuf_tensor_at("gates", [P, 2, D], F32, offset=gates_at)
        ret_o = nc.alloc_sbuf_tensor_at("ret_o", [P, 2, BR_W], F32, offset=v_at)
        rope_tmp = probsT[:].rearrange("p a b -> p (a b)")[:, 0:512]
        decayed = probsT[:].rearrange("p a b -> p (a b)")[:, 0:1024]
        squares = probs[:].rearrange("p a b -> p (a b)")[:, 0:1024]
        conv = wide[:, 0, :].rearrange("p (c t) -> p c t", c=BT)
        conv_c = wide[:, 1, :].rearrange("p (c t) -> p c t", c=BT)
        at[0] = after_xT
        dn_act = place("dn_act", [P, 2, 512], F32)
        dn_sil = place("dn_sil", [P, 2, 512], F32)
        dnT_hi = place("dnT_hi", [P, 4, SEQ], F32R)
        dnT_lo = place("dnT_lo", [P, 4, SEQ], F32R)
        at[0] = after_xT
        tok_hi = place("tok_hi", [P, 2, D], F32R)
        tok_lo = place("tok_lo", [P, 2, D], F32R)
        ex_hi = place("ex_hi", [P, KT, P], F32R)
        ex_lo = place("ex_lo", [P, KT, P], F32R)
        put_in = place("put_in", [P, 2, P], F32R)
        put_back = place("put_back", [P, SEQ], F32R)
        ex_act = place("ex_act", [P, 512], F32)
        ex_sil = place("ex_sil", [P, 512], F32)
        exT_hi = place("exT_hi", [P, 4, P], F32R)
        exT_lo = place("exT_lo", [P, 4, P], F32R)
        ey_hi = place("ey_hi", [P, D], F32R)
        ey_lo = place("ey_lo", [P, D], F32R)
        logits = place("logits", [P, 2, NEXP], F32)
        top = place("top", [P, 2, NEXP], F32)
        top_at = place("top_at", [P, 2, NEXP], U32)
        top_f = place("top_f", [P, 2, NEXP], F32)
        first = place("first", [P, 2, NEXP], F32)
        second = place("second", [P, 2, NEXP], F32)
        chosen = place("chosen", [P, 2, NEXP], F32)
        share = place("share", [P, 2, NEXP], F32)
        slot_of = place("slot_of", [P, 2, NEXP], F32)
        prob = place("prob", [P, 8], F32)
        slot_w = place("slot_w", [P, 1], F32)
        crowded = place("crowded", [P, 1], I32)
        assert at[0] <= nc.sbuf_usable_end, at[0]

        ps = ctx.enter_context(nc.psum_tensor("ps", [P, 8, 512], F32))

        def const(name, rows=P):
            lo, hi = CONST_AT[name]
            return cst[0:rows, lo:hi]

        ident = const("ident")

        def sem(name):
            return ctx.enter_context(nc.semaphore(name))

        def signal(name, per_layer=0):
            return Signal(sem(name), per_layer)

        x_in = [sem("x_in0"), sem("x_in1")]
        first_norm_w_in = sem("first_norm_w_in")
        norm_w_in = sem("norm_w_in")
        consts_in = sem("consts_in")
        params_in = sem("params_in")
        landed = [sem(f"landed{i}") for i in range(RAW)]
        hi_ready = sem("hi_ready")
        lo_ready = sem("lo_ready")
        unit_used = sem("unit_used")
        spare_set = sem("spare_set")
        zeros_set = sem("zeros_set")
        pads_set = sem("pads_set")
        masks_cast = sem("masks_cast")
        chan_ps = sem("chan_ps")
        chan_set = sem("chan_set")
        tensor_chain = sem("tensor_chain")
        scalar_chain = sem("scalar_chain")
        vector_chain = sem("vector_chain")
        sq_summed = sem("sq_summed")
        root_ready = sem("root_ready")
        norm_w_ps = sem("norm_w_ps")
        normed = sem("normed")
        normed_ps = sem("normed_ps")
        xT_hi_ready = sem("xT_hi_ready")
        xT_lo_ready = sem("xT_lo_ready")
        tile0_summed = sem("tile0_summed")
        res_added = sem("res_added")
        rope_done = signal("rope_done", 3)
        v_copied = signal("v_copied", 2)
        qkT_ps = signal("qkT_ps", 1)
        qT_ready = signal("qT_ready", 1)
        kT_ready = signal("kT_ready", 1)
        scores_ps = signal("scores_ps", 2)
        max_ready = signal("max_ready", 2)
        exp_done = signal("exp_done", 2)
        probs_ready = signal("probs_ready", 2)
        probsT_ps = signal("probsT_ps", 2)
        probsT_ready0 = signal("probsT_ready0", 2)
        probsT_ready1 = signal("probsT_ready1", 2)
        attn_ps = signal("attn_ps", 2)
        attn_hi = signal("attn_hi", 2)
        attn_lo = signal("attn_lo", 2)
        conv_c_copied = signal("conv_c_copied", 1)
        conv_u_ready = signal("conv_u_ready", 1)
        conv_y_ready = signal("conv_y_ready", 1)
        conv_hi = signal("conv_hi", 1)
        conv_lo = signal("conv_lo", 1)
        ret_qkT_ps = signal("ret_qkT_ps", 1)
        rqT_ready = signal("rqT_ready", 1)
        rkT_ready = signal("rkT_ready", 1)
        ret_scores_ps = signal("ret_scores_ps", 1)
        decayed_ready = signal("decayed_ready", 1)
        ret_o_ps = signal("ret_o_ps", 1)
        ret_sq_done = signal("ret_sq_done", 1)
        ret_ss_ready = signal("ret_ss_ready", 1)
        ret_root = signal("ret_root", 1)
        ret_gate_ready = signal("ret_gate_ready", 1)
        ret_y_ready = signal("ret_y_ready", 1)
        ret_yT_ps = signal("ret_yT_ps", 1)
        ret_hi = signal("ret_hi", 1)
        ret_lo = signal("ret_lo", 1)
        gate_ready = signal("gate_ready", 6)
        merged = signal("merged", 6)
        mergedT_ps = signal("mergedT_ps", 4)
        mT_hi = signal("mT_hi", 4)
        mT_lo = signal("mT_lo", 4)
        dn_silu = sem("dn_silu")
        dn_ready = sem("dn_ready")
        dnT_ps = sem("dnT_ps")
        dnT_hi_ready = sem("dnT_hi_ready")
        dnT_lo_ready = sem("dnT_lo_ready")
        ex_silu = sem("ex_silu")
        ex_ready = sem("ex_ready")
        exT_ps = sem("exT_ps")
        exT_hi_ready = sem("exT_hi_ready")
        exT_lo_ready = sem("exT_lo_ready")
        tok_hi_ready = sem("tok_hi_ready")
        tok_lo_ready = sem("tok_lo_ready")
        router_hi = sem("router_hi")
        router_lo = sem("router_lo")
        logits_ps = sem("logits_ps")
        gap_ready = sem("gap_ready")
        gap_exp = sem("gap_exp")
        chosen_ready = sem("chosen_ready")
        places_ps = sem("places_ps")
        totals_ps = sem("totals_ps")
        routed = sem("routed")
        put_in_ready = sem("put_in_ready")
        put_back_ps = sem("put_back_ps")
        put_back_ready = sem("put_back_ready")
        slot_w_ready = sem("slot_w_ready")
        gathered_ps = sem("gathered_ps")
        ex_hi_ready = sem("ex_hi_ready")
        ex_lo_ready = sem("ex_lo_ready")
        ey_hi_ready = sem("ey_hi_ready")
        ey_lo_ready = sem("ey_lo_ready")
        back_ps = sem("back_ps")
        ex_added = sem("ex_added")
        slots_moved = sem("slots_moved")
        res_final = sem("res_final")
        out_ready = sem("out_ready")
        out_stored = sem("out_stored")

        MIX0 = (0, MIX_UNITS + FFN_UNITS)
        DENSE0 = MIX_UNITS
        MOE0 = 2 * MIX_UNITS + FFN_UNITS
        CROWD0 = MOE0 + NEXP * FFN_UNITS

        def wait_split(eng, j, r):
            eng.wait_ge(lo_ready, r * RAW + (j + 1))

        def split_hi(act, j, r=0):
            act.wait_ge(landed[j % RAW], r * 16 + (j // RAW + 1) * 16)
            if j >= SPLIT:
                act.wait_ge(unit_used, r * RAW + (j - SPLIT + 1))
            nc.scalar.activation(w_hi[:, j % SPLIT, :], raw[:, j % RAW, :], ACT.Copy).then_inc(hi_ready, 1)

        def split_lo(dve, j, r=0):
            dve.wait_ge(hi_ready, r * RAW + (j + 1))
            if j >= SPLIT:
                dve.wait_ge(unit_used, r * RAW + (j - SPLIT + 1))
            nc.vector.tensor_tensor(w_lo[:, j % SPLIT, :], raw[:, j % RAW, :],
                                    w_hi[:, j % SPLIT, :].bitcast(F32), ALU.subtract).then_inc(lo_ready, 1)

        block = ctx.enter_context(nc.Block())

        @block.sync
        def _(sp):
            for t in range(2):
                sp.dma_start(res[:, t, :], x[0, t * P:(t + 1) * P, :]).then_inc(x_in[t], 16)
            pick = CONST_AT["pick"][0]
            sp.dma_start(cst[:, 0:pick], consts[:, 0:pick]).then_inc(consts_in, 16)

            def load(j, src, r=0):
                if j >= RAW:
                    sp.wait_ge(lo_ready, r * RAW + (j - RAW + 1))
                shape = src.shape
                dst = raw[:, j % RAW, :].rearrange("p (k n) -> p k n", n=shape[-1])
                sp.dma_start(dst, src).then_inc(landed[j % RAW], 16)

            def wide_unit(w, k_half, col):
                return w[bass.ds(k_half, 512), bass.ds(col, 512)].rearrange("(k p) n -> p k n", p=P)

            def deep_unit(w, row):
                return w[bass.ds(row, 2 * P), :].rearrange("(k p) n -> p k n", p=P)

            def load_mixer(layer):
                n = MIX0[layer]
                for c, chunk in enumerate(CHUNKS):
                    if layer == 0 and c == 1:
                        sp.dma_start(chan_rows[0:8, :], ret_norm_w.rearrange("l (c p) -> (l c) p", p=P)).then_inc(params_in, 16)
                        sp.dma_start(chan_rows[8:32, :], conv_w.rearrange("l j (c p) -> (l j c) p", p=P))\
                                .then_inc(params_in, 16)
                        sp.dma_start(chan_rows[32:40, :], conv_b.rearrange("l (c p) -> (l c) p", p=P)).then_inc(params_in, 16)
                        sp.dma_start(probs[:, 0, :], masks).then_inc(params_in, 16)
                        sp.dma_start(router[:], moe_router[0].rearrange("(k p) e -> p k e", p=P)).then_inc(params_in, 16)
                    for half in range(2):
                        load(n, wide_unit(w_in[layer], half * 512, chunk * 512))
                        n += 1
                    if c in (10, 12, 13):
                        w = {10: w_br_attn, 12: w_br_conv, 13: w_br_ret}[c]
                        for h in range(2):
                            load(n, deep_unit(w[layer], h * 2 * P))
                            n += 1
                for h in range(4):
                    load(n, deep_unit(w_out[layer], h * 2 * P))
                    n += 1

            load_mixer(0)
            gate, up, down = dense_w_gate[0], dense_w_up[0], dense_w_down[0]
            for h in range(2):
                load(DENSE0 + h, wide_unit(gate, h * 512, 0))
            with sp.Fori(0, 6) as i:
                for h in range(2):
                    load(DENSE0 + 2 + h, wide_unit(up, h * 512, i * 512), i)
                for h in range(2):
                    load(DENSE0 + 4 + h, wide_unit(gate, h * 512, i * 512 + 512), i)
                for h in range(2):
                    load(DENSE0 + 6 + h, deep_unit(down, i * 512 + h * 2 * P), i)
            for h in range(2):
                load(DENSE0 + 38 + h, wide_unit(up, h * 512, (FCH - 1) * 512))
            for h in range(2):
                load(DENSE0 + 40 + h, deep_unit(down, (FCH - 1) * 512 + h * 2 * P))
            load_mixer(1)

            gate = moe_w_gate[0].rearrange("e k f -> (e k) f")
            up = moe_w_up[0].rearrange("e k f -> (e k) f")
            down = moe_w_down[0].rearrange("e f d -> (e f) d")

            def load_experts(base):
                with sp.Fori(0, NEXP) as e:
                    for h in range(2):
                        load(base + h, wide_unit(gate, e * D + h * 512, 0), e * FCH)
                    for h in range(2):
                        load(base + 2 + h, wide_unit(up, e * D + h * 512, 0), e * FCH)
                    with sp.Fori(0, 6) as i:
                        r = e * FCH + i
                        for h in range(2):
                            load(base + 4 + h, wide_unit(gate, e * D + h * 512, i * 512 + 512), r)
                        for h in range(2):
                            load(base + 6 + h, wide_unit(up, e * D + h * 512, i * 512 + 512), r)
                        for h in range(2):
                            load(base + 8 + h, deep_unit(down, e * FF + i * 512 + h * 2 * P), r)
                    for h in range(2):
                        load(base + 40 + h, deep_unit(down, e * FF + ((FCH - 1) * 512 + h * 2 * P)), e * FCH)

            load_experts(MOE0)
            sp.wait_ge(routed, 1)
            flag = sp.value_load(crowded[0:1, 0:1], min_val=0, max_val=1)
            with sp.If(flag > 0):
                load_experts(CROWD0)
            for t in range(2):
                sp.wait_ge(out_ready, t + 1)
                sp.dma_start(out[0, t * P:(t + 1) * P, :], wide[:, t, :]).then_inc(out_stored, 16)
            sp.wait_ge(out_stored, 32)

        @block.gpsimd
        def _(pool):
            nc.gpsimd.memset(spare[:, 8:9], 1.0).then_inc(spare_set, 1)
            nc.gpsimd.memset(zeros[:], 0.0).then_inc(zeros_set, 1)
            nc.gpsimd.memset(uT[:, :, 0:2], 0.0).then_inc(pads_set, 1)

        @block.tensor
        def _(pe):
            mm = nc.tensor.matmul
            chain = Chain(tensor_chain, pe)

            def three(o, a_hi, a_lo, b_hi, b_lo, start, stop):
                mm(o, a_hi, b_hi, start=start, stop=False, skip_group_check=True)
                mm(o, a_hi, b_lo, start=False, stop=False, skip_group_check=True)
                return mm(o, a_lo, b_hi, start=False, stop=stop, skip_group_check=True)

            def wide_unit(j, x_hi, x_lo, kt0, banks, r=0):
                wait_split(pe, j, r)
                s = j % SPLIT
                for k in range(4):
                    cols = slice(k * 512, k * 512 + 512)
                    for t, bank in enumerate(banks):
                        tok = slice(t * P, t * P + P)
                        last = three(ps[:, bank, :], x_hi[:, kt0 + k, tok], x_lo[:, kt0 + k, tok],
                                     w_hi[:, s, cols], w_lo[:, s, cols],
                                     start=(kt0 == 0 and k == 0), stop=(kt0 == 4 and k == 3))
                last.then_inc(unit_used, 1)

            def deep_unit(j, x_hi, x_lo, kt0, banks, start, stop, r=0):
                wait_split(pe, j, r)
                s = j % SPLIT
                for k in range(2):
                    for t, pair in enumerate(banks):
                        tok = slice(t * P, t * P + P)
                        for half, bank in enumerate(pair):
                            cols = slice(k * 1024 + half * 512, k * 1024 + half * 512 + 512)
                            last = three(ps[:, bank, :], x_hi[:, kt0 + k, tok],
                                         x_lo[:, kt0 + k, tok], w_hi[:, s, cols], w_lo[:, s, cols],
                                         start=(start and k == 0), stop=(stop and k == 1))
                last.then_inc(unit_used, 1)

            def channel_unit(j, kt0, bank0):
                wait_split(pe, j, 0)
                s = j % SPLIT
                for k in range(4):
                    for cb in range(4):
                        cols = slice(k * 512 + cb * P, k * 512 + cb * P + P)
                        o = ps[:, bank0 + cb // 2, (cb % 2) * SEQ:(cb % 2) * SEQ + SEQ]
                        last = three(o, w_hi[:, s, cols], w_lo[:, s, cols], xT_hi[:, kt0 + k, :],
                                     xT_lo[:, kt0 + k, :], start=(kt0 == 0 and k == 0 and cb % 2 == 0),
                                     stop=(kt0 == 4 and k == 3))
                last.then_inc(unit_used, 1)

            SUMS, EX_SUMS = ((4, 5), (6, 7)), ((2, 3),)
            BRANCH = ((4, 6), (5, 7))

            def transpose(o, i):
                return nc.tensor.transpose(o, i, ident[0:i.shape[0], 0:i.shape[0]])

            def open_sums(banks):
                for b in banks:
                    mm(ps[:, b, :], zeros[:, 0:P], zeros[:], start=True, stop=False, skip_group_check=True)

            def deep_pair(j, x_hi, x_lo, kt0, banks, r=0):
                wait_split(pe, j + 1, r)
                for t, pair in enumerate(banks):
                    tok = slice(t * P, t * P + P)
                    for u in range(2):
                        s = (j + u) % SPLIT
                        for k in range(2):
                            for half, bank in enumerate(pair):
                                cols = slice(k * 1024 + half * 512, k * 1024 + half * 512 + 512)
                                last = three(ps[:, bank, :], x_hi[:, kt0 + 2 * u + k, tok],
                                             x_lo[:, kt0 + 2 * u + k, tok], w_hi[:, s, cols], w_lo[:, s, cols],
                                             start=False, stop=(u == 1 and k == 1))
                        if t == 1:
                            last.then_inc(unit_used, 1)
                    if t == 0:
                        last.then_inc(tile0_summed, 1)

            def norm_weights(q, banks):
                row = (0, 2, 1, 3, 4)[q]
                rows = 5 if q else 2
                for half, bank in enumerate(banks):
                    last = mm(ps[:, bank, :], const("pick", rows)[:, row * P:row * P + P],
                              norm_w[0:rows, half * 512:half * 512 + 512], start=True, stop=True)
                last.then_inc(norm_w_ps, 1)

            def turn_normed(q, t):
                pe.wait_ge(normed, 2 * q + t + 1)
                for k in range(KT):
                    last = transpose(ps[:, 2 + 2 * t + k // 4, (k % 4) * P:(k % 4) * P + P],
                                     wide[:, t, k * P:k * P + P])
                last.then_inc(normed_ps, 1)

            def first_pair(q, j, banks):
                def half_products(u, t):
                    s, tok = (j + u) % SPLIT, slice(t * P, t * P + P)
                    for k in range(4):
                        cols = slice(k * 512, k * 512 + 512)
                        last = three(ps[:, banks[t], :], xT_hi[:, 4 * u + k, tok], xT_lo[:, 4 * u + k, tok],
                                     w_hi[:, s, cols], w_lo[:, s, cols], start=(u == 0 and k == 0),
                                     stop=(u == 1 and k == 3))
                    return last

                turn_normed(q, 0)
                if q:
                    pe.wait_ge(res_added, 2 * q)
                else:
                    turn_normed(q, 1)
                wait_split(pe, j, 0)
                pe.wait_ge(xT_lo_ready, 4 * q + 2)
                half_products(0, 0)
                if q:
                    turn_normed(q, 1)
                wait_split(pe, j + 1, 0)
                half_products(1, 0)
                pe.wait_ge(xT_lo_ready, 4 * q + 4)
                half_products(0, 1).then_inc(unit_used, 1)
                half_products(1, 1).then_inc(unit_used, 1)

            def mixer(L):
                base = MIX0[L]

                def attention_scores(g):
                    for odd in range(2):
                        for j in (odd, odd + 2):
                            hp, r = (4 * g + j) // 2, HEAD * odd
                            o = ps[:, 5 + j // 2, odd * SEQ:odd * SEQ + SEQ]
                            mm(o, msk[:, 0:P], msk[:, P:3 * P], start=True, stop=False)
                            mm(o, qT[r:r + HEAD, hp, P:SEQ], kT[r:r + HEAD, hp, :], start=False, stop=True)
                            o = ps[:, 7, j * P:j * P + P]
                            mm(o, msk[:, 0:P], msk[:, 2 * P:3 * P], start=True, stop=False)
                            last = mm(o, qT[r:r + HEAD, hp, 0:P], kT[r:r + HEAD, hp, 0:P], start=False, stop=True)
                        if odd == 0:
                            chain(last)
                    last.then_inc(scores_ps.sem, 1)

                def transpose_probs(g):
                    probs_ready.wait(pe, g + 1, L)
                    for j in range(4):
                        b, c = 5 + j // 2, (j % 2) * SEQ
                        transpose(ps[:, b, c:c + P], probs[:, j, 2 * P:3 * P])
                        transpose(ps[:, b, c + P:c + 2 * P], probs[:, j, 0:P])
                        last = transpose(ps[:, 7, j * P:j * P + P], probs[:, j, P:2 * P])
                    last.then_inc(probsT_ps.sem, 1)

                def attention_values(g):
                    probsT_ready0.wait(pe, g + 1, L)
                    probsT_ready1.wait(pe, g + 1, L)
                    if g == 1:
                        attn_hi.wait(pe, 1, L)
                        attn_lo.wait(pe, 1, L)
                    for j in range(4):
                        h, r, c = 4 * g + j, HEAD * (j % 2), (j // 2) * SEQ
                        mm(ps[r:r + HEAD, 4, c:c + SEQ], v_attn[:, 0, h * HEAD:h * HEAD + HEAD],
                           probsT[:, j, 0:SEQ], start=True, stop=True)
                        last = mm(ps[r:r + HEAD, 4, c + P:c + SEQ], v_attn[:, 1, h * HEAD:h * HEAD + HEAD],
                                  probsT[:, j, SEQ:SEQ + P], start=False, stop=True, skip_group_check=True)
                    last.then_inc(attn_ps.sem, 1)

                def chunk(c, n):
                    for half in range(2):
                        wide_unit(n + half, xT_hi, xT_lo, 4 * half, [2 * (c % 2), 2 * (c % 2) + 1])

                n = base
                first_pair(2 * L, n, [6, 7])
                chunk(1, n + 2)
                if L == 0:
                    pe.wait_ge(params_in, 16 * 5)
                    transpose(ps[:, 4, 0:40], chan_rows[:, :]).then_inc(chan_ps, 1)
                chunk(2, n + 4)
                rope_done.wait(pe, 2, L)
                for c in range(4):
                    for t in range(2):
                        col = (c % 2) * SEQ + t * P
                        transpose(ps[:, 4 + c // 2, col:col + P], wide[:, t, c * P:c * P + P])
                        last = transpose(ps[:, 6 + c // 2, col:col + P], wide[:, t, 512 + c * P:512 + c * P + P])
                last.then_inc(qkT_ps.sem, 1)
                chunk(3, n + 6)
                qT_ready.wait(pe, 1, L)
                kT_ready.wait(pe, 1, L)
                if L == 0:
                    pe.wait_ge(masks_cast, 1)
                attention_scores(0)
                v_copied.wait(pe, 1, L)
                chunk(4, n + 8)
                rope_done.wait(pe, 3, L)
                channel_unit(n + 10, 0, 2)
                transpose_probs(0)
                channel_unit(n + 11, 4, 2)
                attention_values(0)
                attention_scores(1)
                v_copied.wait(pe, 2, L)
                for half in range(2):
                    channel_unit(n + 12 + half, 4 * half, 0)
                conv_c_copied.wait(pe, 1, L)
                channel_unit(n + 14, 0, 2)
                transpose_probs(1)
                channel_unit(n + 15, 4, 2)
                attention_values(1)
                for c in range(2):
                    for t in range(2):
                        col = c * SEQ + t * P
                        transpose(ps[:, 5, col:col + P], ret_qk[:, t, c * P:c * P + P])
                        last = transpose(ps[:, 6, col:col + P], ret_qk[:, t, SEQ + c * P:SEQ + c * P + P])
                last.then_inc(ret_qkT_ps.sem, 1)
                conv_u_ready.wait(pe, 1, L)
                chunk(8, n + 16)
                rqT_ready.wait(pe, 1, L)
                rkT_ready.wait(pe, 1, L)
                for odd in range(2):
                    for h in (odd, odd + 2):
                        hp, r = h // 2, HEAD * odd
                        for t in range(2):
                            tok = slice(t * P, t * P + P)
                            mm(ps[:, 5 + t, h * P:h * P + P], rkT[r:r + HEAD, hp, tok], rqT[r:r + HEAD, hp, tok],
                               start=True, stop=True)
                        last = mm(ps[r:r + HEAD, 7, hp * P:hp * P + P], kzeta[:, h * HEAD:h * HEAD + HEAD],
                                  v_ret[:, 0, h * P:h * P + P], start=True, stop=True)
                    if odd == 0:
                        chain(last)
                last.then_inc(ret_scores_ps.sem, 1)
                conv_y_ready.wait(pe, 1, L)
                chunk(9, n + 18)
                decayed_ready.wait(pe, 1, L)
                for odd in range(2):
                    for h in (odd, odd + 2):
                        hp, r, cols = h // 2, HEAD * odd, slice(h * P, h * P + P)
                        for t in range(2):
                            mm(ps[:, 5 + t, cols], decayed[:, t * 512 + h * P:t * 512 + h * P + P],
                               v_ret[:, t, cols], start=True, stop=(t == 0))
                        last = mm(ps[:, 6, cols], rqxT[r:r + HEAD, hp, :], state[r:r + HEAD, hp * P:hp * P + P],
                                  start=False, stop=True)
                    if odd == 0:
                        chain(last)
                last.then_inc(ret_o_ps.sem, 1)
                ret_gate_ready.wait(pe, 1, L)
                chunk(10, n + 20)
                ret_y_ready.wait(pe, 1, L)
                attn_hi.wait(pe, 2, L)
                attn_lo.wait(pe, 2, L)
                for h in range(2):
                    deep_unit(base + BR_ATTN + h, yA_hi, yA_lo, 2 * h, BRANCH, h == 0, h == 1)
                gate_ready.wait(pe, 2, L)
                for c in range(BT):
                    for t in range(2):
                        col = (c % 2) * SEQ + t * P
                        last = transpose(ps[:, c // 2, col:col + P], ret_o[:, t, c * P:c * P + P])
                last.then_inc(ret_yT_ps.sem, 1)
                chunk(11, n + 24)
                ret_hi.wait(pe, 1, L)
                ret_lo.wait(pe, 1, L)
                chunk(12, n + 26)
                merged.wait(pe, 2, L)
                conv_hi.wait(pe, 1, L)
                conv_lo.wait(pe, 1, L)
                for h in range(2):
                    deep_unit(base + BR_CONV + h, yC_hi, yC_lo, 2 * h, BRANCH, h == 0, h == 1)
                gate_ready.wait(pe, 3, L)
                chunk(13, n + 30)
                merged.wait(pe, 4, L)
                for h in range(2):
                    deep_unit(base + BR_RET + h, yA_hi, yA_lo, 2 * h, BRANCH, h == 0, h == 1)
                gate_ready.wait(pe, 4, L)

                def turn_merged(half, bank0):
                    merged.wait(pe, 5 + half, L)
                    gate_ready.wait(pe, 5 + half, L)
                    for t in range(2):
                        for k in range(4):
                            last = transpose(ps[:, bank0 + t, k * P:k * P + P],
                                             wide[:, t, (4 * half + k) * P:(4 * half + k + 1) * P])
                        last.then_inc(mergedT_ps.sem, 1)

                wide_unit(n + 34, xT_hi, xT_lo, 0, [0, 1])
                turn_merged(0, 2)
                wide_unit(n + 35, xT_hi, xT_lo, 4, [0, 1])
                mT_hi.wait(pe, 2, L)
                mT_lo.wait(pe, 2, L)
                sums = ((2, 3), (4, 5))
                deep_unit(base + OUT_PROJ, xT_hi, xT_lo, 0, sums, True, False)
                turn_merged(1, 0)
                deep_unit(base + OUT_PROJ + 1, xT_hi, xT_lo, 2, sums, False, False)
                mT_hi.wait(pe, 4, L)
                mT_lo.wait(pe, 4, L)
                norm_weights(2 * L + 1, [6, 7])
                deep_pair(base + OUT_PROJ + 2, xT_hi, xT_lo, 4, sums)

            def dense():
                first_pair(1, DENSE0, [0, 1])
                open_sums(range(4, 8))

                def turn(i):
                    pe.wait_ge(dn_ready, i)
                    for k in range(4):
                        for t in range(2):
                            last = transpose(ps[:, 2 + t, k * P:k * P + P], dn_act[:, t, k * P:k * P + P])
                    last.then_inc(dnT_ps, 1)

                with pe.Fori(0, 6) as i:
                    for h in range(2):
                        wide_unit(DENSE0 + 2 + h, xT_hi, xT_lo, 4 * h, [2, 3], i)
                    pe.wait_ge(dn_silu, i + 1)
                    wide_unit(DENSE0 + 4, xT_hi, xT_lo, 0, [0, 1], i)
                    turn(i + 1)
                    wide_unit(DENSE0 + 5, xT_hi, xT_lo, 4, [0, 1], i)
                    pe.wait_ge(dnT_hi_ready, i + 1)
                    pe.wait_ge(dnT_lo_ready, i + 1)
                    for h in range(2):
                        deep_unit(DENSE0 + 6 + h, dnT_hi, dnT_lo, 2 * h, SUMS, False, False, i)
                for h in range(2):
                    wide_unit(DENSE0 + 38 + h, xT_hi, xT_lo, 4 * h, [2, 3])
                turn(FCH)
                norm_weights(2, [0, 1])
                pe.wait_ge(dnT_hi_ready, FCH)
                pe.wait_ge(dnT_lo_ready, FCH)
                deep_pair(DENSE0 + 40, dnT_hi, dnT_lo, 0, SUMS)

            def route():
                pe.wait_ge(router_lo, 1)
                turn_normed(3, 0)
                pe.wait_ge(res_added, 6)
                for t in range(2):
                    pe.wait_ge(xT_lo_ready, 14 + 2 * t)
                    tok = slice(t * P, t * P + P)
                    for k in range(KT):
                        mm(ps[:, 0, 2 * t * NEXP:2 * (t + 1) * NEXP], xT_hi[:, k, tok],
                           rt[:, k, :], start=(k == 0), stop=False, skip_group_check=True)
                        last = mm(ps[:, 0, 2 * t * NEXP:(2 * t + 1) * NEXP], xT_lo[:, k, tok],
                                  rt[:, k, 0:NEXP], start=False, stop=(k == KT - 1), skip_group_check=True)
                    if t == 0:
                        turn_normed(3, 1)
                last.then_inc(logits_ps, 1)
                pe.wait_ge(chosen_ready, 1)
                mm(ps[:, 7, 0:8], const("before"), chosen[:, 0, :], start=True, stop=True)
                mm(ps[:, 7, 8:16], const("ones"), chosen[:, 0, :], start=True, stop=False)
                mm(ps[:, 7, 8:16], const("before"), chosen[:, 1, :], start=False, stop=True).then_inc(places_ps, 1)
                mm(ps[:, 4, 0:8], const("ones"), chosen[:, 0, :], start=True, stop=False)
                mm(ps[:, 4, 0:8], const("ones"), chosen[:, 1, :], start=False, stop=True).then_inc(totals_ps, 1)

            def gather(n):
                pe.wait_ge(put_in_ready, n)
                for k in range(KT):
                    o = ps[:, 5 + k // 4, (k % 4) * P:(k % 4) * P + P]
                    for t in range(2):
                        mm(o, tok_hi[:, t, k * P:k * P + P], put_in[:, t, :], start=(t == 0), stop=False)
                        last = mm(o, tok_lo[:, t, k * P:k * P + P], put_in[:, t, :], start=False, stop=(t == 1))
                    if k % 4 == 3:
                        last.then_inc(gathered_ps, 1)

            def experts(base, done):
                gather(done + 1)
                for h in range(2):
                    pe.wait_ge(ex_lo_ready, 2 * done + h + 1)
                    wide_unit(base + h, ex_hi, ex_lo, 4 * h, [0])

                def expert(e, last_one):
                    r = e * FCH
                    f = r + done * FCH
                    for h in range(2):
                        wide_unit(base + 2 + h, ex_hi, ex_lo, 4 * h, [1], r)
                    pe.wait_ge(ex_added, e * 2 + 2 * done)
                    for t in range(2):
                        transpose(ps[:, 7, t * P:t * P + P], put_in[:, t, :].bitcast(F32))
                    for t in range(2):
                        last = mm(ps[:, 7, SEQ:SEQ + 1], put_in[:, t, :].bitcast(F32),
                                  share[:, t, bass.ds(e, 1)], start=(t == 0), stop=(t == 1))
                    last.then_inc(put_back_ps, 1)
                    open_sums([2, 3])

                    def turn(n):
                        pe.wait_ge(ex_ready, n)
                        for k in range(4):
                            last = transpose(ps[:, 4, k * P:k * P + P], ex_act[:, k * P:k * P + P])
                        last.then_inc(exT_ps, 1)

                    with pe.Fori(0, 6) as i:
                        v = r + i
                        pe.wait_ge(ex_silu, f + i + 1)
                        for h in range(2):
                            wide_unit(base + 4 + h, ex_hi, ex_lo, 4 * h, [0], v)
                        turn(f + i + 1)
                        for h in range(2):
                            wide_unit(base + 6 + h, ex_hi, ex_lo, 4 * h, [1], v)
                        pe.wait_ge(exT_lo_ready, f + i + 1)
                        for h in range(2):
                            deep_unit(base + 8 + h, exT_hi, exT_lo, 2 * h, EX_SUMS, False, False, v)
                    turn(f + FCH)
                    if not last_one:
                        gather(e + (done + 2))
                    pe.wait_ge(exT_lo_ready, f + FCH)
                    for h in range(2):
                        deep_unit(base + 40 + h, exT_hi, exT_lo, 2 * h, EX_SUMS, False, h == 1, r)
                    if not last_one:
                        pe.wait_ge(ex_lo_ready, e * 2 + (2 * done + 4))
                        for h in range(2):
                            wide_unit(base + FFN_UNITS + h, ex_hi, ex_lo, 4 * h, [0], r)
                    pe.wait_ge(ey_lo_ready, e + (done + 1))
                    pe.wait_ge(put_back_ready, e + (done + 1))
                    for t in range(2):
                        for half in range(2):
                            o, cols = ps[:, 4 + 2 * t + half, :], slice(half * 512, half * 512 + 512)
                            mm(o, put_back[:, t * P:t * P + P], ey_hi[:, cols], start=True, stop=False)
                            last = mm(o, put_back[:, t * P:t * P + P], ey_lo[:, cols], start=False, stop=True)
                        last.then_inc(back_ps, 1)

                with pe.Fori(0, NEXP - 1) as e:
                    expert(e, False)
                expert(NEXP - 1, True)

            pe.wait_ge(first_norm_w_in, 16 * 2)
            norm_weights(0, [0, 1])
            pe.wait_ge(norm_w_in, 16 * 2)
            pe.wait_ge(consts_in, 16)
            pe.wait_ge(zeros_set, 1)
            mixer(0)
            dense()
            mixer(1)
            route()
            pe.wait_ge(tok_lo_ready, 2)
            experts(MOE0, 0)
            pe.wait_ge(routed, 1)
            flag = pe.value_load(crowded[0:1, 0:1], min_val=0, max_val=1)
            with pe.If(flag > 0):
                experts(CROWD0, NEXP)
            norm_weights(4, [0, 1])

        @block.scalar
        def _(act):
            lo, hi = CONST_AT["pick"]
            act.dma_start(cst[0:5, lo:hi], consts[0:5, lo:hi]).then_inc(first_norm_w_in, 16)
            act.dma_start(norm_w[0:2, :], mix_norm_w).then_inc(first_norm_w_in, 16)
            act.dma_start(norm_w[2:4, :], ffn_norm_w).then_inc(norm_w_in, 16)
            act.dma_start(norm_w[4:5, :], final_norm_w.rearrange("(a d) -> a d", a=1)).then_inc(norm_w_in, 16)
            chain = Chain(scalar_chain, act)
            run = nc.scalar.activation

            def root(t):
                chain(run(wide[:, t, :], res[:, t, :], ACT.Square, accum_out=stat[:, t:t + 1]))
                run(stat[:, 2 + t:3 + t], stat[:, t:t + 1], ACT.Sqrt, scale=1.0 / D, bias=EPS)\
                    .then_inc(root_ready, 1)

            def ready_root(n):
                run(spare[:, n:n + 1], spare[:, 8:9], ACT.Sqrt)

            def turn_normed(q, t):
                act.wait_ge(normed_ps, 2 * q + t + 1)
                for half in range(2):
                    run(xT_hi[:, 4 * half:4 * half + 4, t * P:t * P + P],
                        ps[:, 2 + 2 * t + half, :].rearrange("p (k t) -> p k t", k=4), ACT.Copy)\
                        .then_inc(xT_hi_ready, 1)

            def cross(q, n):
                split_hi(act, n)
                ready_root(q)
                act.wait_ge(res_added, 2 * q - 1)
                root(0)
                split_hi(act, n + 1)
                turn_normed(q, 0)
                act.wait_ge(res_added, 2 * q)
                root(1)
                turn_normed(q, 1)
                if q < 3:
                    split_hi(act, n + 2)

            def mixer(L):
                base = MIX0[L]

                def exps(g):
                    max_ready.wait(act, g + 1, L)
                    for j in range(4):
                        run(probs[:, j, 0:SEQ], ps[:, 5 + j // 2, (j % 2) * SEQ:(j % 2) * SEQ + SEQ], ACT.Exp,
                            scale=HEAD ** -0.5, bias=stat[:, 16 + j:17 + j], accum_out=stat[:, 24 + j:25 + j])
                    for j in range(4):
                        last = run(probs[:, j, SEQ:SEQ + P], ps[:, 7, j * P:j * P + P], ACT.Exp,
                                   scale=HEAD ** -0.5, bias=stat[:, 20 + j:21 + j],
                                   accum_out=stat[:, 28 + j:29 + j])
                    last.then_inc(exp_done.sem, 1)

                def turn_probs(g):
                    probsT_ps.wait(act, g + 1, L)
                    run(probsT[:, :, 0:SEQ], ps[:, 5:7, :].rearrange("p b (j q) -> p (b j) q", j=2), ACT.Copy)\
                        .then_inc(probsT_ready0.sem, 1)

                def turn_attention(g):
                    attn_ps.wait(act, g + 1, L)
                    run(yA_hi[:, 2 * g:2 * g + 2, :], ps[:, 4, :].rearrange("p (c t) -> p c t", c=2), ACT.Copy)\
                        .then_inc(attn_hi.sem, 1)

                def sigmoid(c, half):
                    run(gates[:, :, half * 512:half * 512 + 512], ps[:, 2 * (c % 2):2 * (c % 2) + 2, :],
                        ACT.Sigmoid).then_inc(gate_ready.sem, 1)

                def turn_merged(half, bank0):
                    for t in range(2):
                        mergedT_ps.wait(act, 2 * half + t + 1, L)
                        run(xT_hi[:, 4 * half:4 * half + 4, t * P:t * P + P],
                            ps[:, bank0 + t, :].rearrange("p (k t) -> p k t", k=4), ACT.Copy).then_inc(mT_hi.sem, 1)

                for m in range(3, MIX_UNITS):
                    act.wait_ge(unit_used, base + m - 2)
                    if m == 4 and L == 0:
                        act.wait_ge(params_in, 16 * 5)
                        run(msk[:], probs[:, 0, :], ACT.Copy).then_inc(masks_cast, 1)
                    if m == 8:
                        run(v_attn[:], ps[:, 0:2, :], ACT.Copy).then_inc(v_copied.sem, 1)
                        qkT_ps.wait(act, 1, L)
                        run(qT[:].rearrange("p c t -> p (c t)"), ps[:, 4:6, :].rearrange("p b n -> p (b n)"),
                            ACT.Copy).then_inc(qT_ready.sem, 1)
                    if m == 10:
                        exps(0)
                    if m == 12:
                        run(v_ret[:], ps[:, 0:2, :], ACT.Copy).then_inc(v_copied.sem, 1)
                    if m == 13:
                        turn_probs(0)
                    if m == 14:
                        run(conv_c.rearrange("p c t -> p (c t)"), ps[:, 2:4, :].rearrange("p b n -> p (b n)"),
                            ACT.Copy).then_inc(conv_c_copied.sem, 1)
                        turn_attention(0)
                        exps(1)
                    if m == 17:
                        turn_probs(1)
                    if m == 18:
                        turn_attention(1)
                        ret_qkT_ps.wait(act, 1, L)
                        run(rqT[:].rearrange("p c t -> p (c t)"), ps[:, 5, :], ACT.Copy).then_inc(rqT_ready.sem, 1)
                        conv_y_ready.wait(act, 1, L)
                        run(yC_hi[:], conv, ACT.Copy).then_inc(conv_hi.sem, 1)
                    if m == 20:
                        run(ret_gate[:], ps[:, 0:2, :], ACT.Silu).then_inc(ret_gate_ready.sem, 1)
                    if m == 22:
                        ret_o_ps.wait(act, 1, L)
                        run(squares, ps[:, 5:7, :].rearrange("p b n -> p (b n)"), ACT.Square)\
                            .then_inc(ret_sq_done.sem, 1)
                        sigmoid(9, 0)
                    if m == 23:
                        ret_ss_ready.wait(act, 1, L)
                        run(stat[:, 40:48], stat[:, 32:40], ACT.Sqrt, scale=1.0 / P, bias=EPS)\
                            .then_inc(ret_root.sem, 1)
                    if m == 24:
                        sigmoid(10, 1)
                    if m == 26:
                        ret_yT_ps.wait(act, 1, L)
                        for c in range(BT):
                            last = run(yA_hi[:, c, :], ps[:, c // 2, (c % 2) * SEQ:(c % 2) * SEQ + SEQ], ACT.Copy,
                                       scale=chan[:, L * BT + c:L * BT + c + 1])
                        last.then_inc(ret_hi.sem, 1)
                    if m == 28:
                        merged.wait(act, 1, L)
                        sigmoid(11, 0)
                    if m == 30:
                        merged.wait(act, 2, L)
                        sigmoid(12, 1)
                    if m == 34:
                        merged.wait(act, 3, L)
                        sigmoid(13, 0)
                    if m == 37:
                        turn_merged(0, 2)
                    if m == 38:
                        merged.wait(act, 4, L)
                        sigmoid(14, 1)
                    if m == 39:
                        turn_merged(1, 0)
                    split_hi(act, base + m)

            def dense():
                def silu(n):
                    run(dn_sil[:], ps[:, 0:2, :], ACT.Silu).then_inc(dn_silu, 1)

                def turn(i):
                    act.wait_ge(dnT_ps, i)
                    run(dnT_hi[:].rearrange("p k (t n) -> p t k n", t=2),
                        ps[:, 2:4, :].rearrange("p t (k n) -> p t k n", k=4), ACT.Copy).then_inc(dnT_hi_ready, 1)

                split_hi(act, DENSE0 + 3)
                act.wait_ge(unit_used, DENSE0 + 2)
                silu(0)
                split_hi(act, DENSE0 + 4)
                with act.Fori(0, 6) as i:
                    split_hi(act, DENSE0 + 5, i)
                    split_hi(act, DENSE0 + 6, i)
                    turn(i + 1)
                    split_hi(act, DENSE0 + 7, i)
                    act.wait_ge(unit_used, i * RAW + (DENSE0 + 6))
                    silu(i + 1)
                    for j in (8, 9, 10):
                        split_hi(act, DENSE0 + j, i)
                split_hi(act, DENSE0 + 41)
                turn(FCH)

            def experts(base, done):
                def take_gathered(n):
                    for half in range(2):
                        act.wait_ge(gathered_ps, n + half)
                        run(ex_hi[:, 4 * half:4 * half + 4, :],
                            ps[:, 5 + half, :].rearrange("p (k t) -> p k t", k=4), ACT.Copy).then_inc(ex_hi_ready, 1)

                def expert(e, last_one):
                    r = e * FCH
                    f = r + done * FCH

                    def silu(n, unit):
                        act.wait_ge(unit_used, unit)
                        act.wait_ge(ex_ready, n)
                        run(ex_sil[:], ps[:, 0, :], ACT.Silu).then_inc(ex_silu, 1)

                    def turn(n):
                        act.wait_ge(exT_ps, n)
                        run(exT_hi[:], ps[:, 4, :].rearrange("p (k t) -> p k t", k=4), ACT.Copy)\
                            .then_inc(exT_hi_ready, 1)

                    split_hi(act, base + 3, r)
                    silu(f, r * RAW + (base + 2))
                    for j in (4, 5):
                        split_hi(act, base + j, r)
                    act.wait_ge(put_back_ps, e + (done + 1))
                    run(put_back[:], ps[:, 7, 0:SEQ], ACT.Copy).then_inc(put_back_ready, 1)
                    with act.Fori(0, 6) as i:
                        v = r + i
                        split_hi(act, base + 6, v)
                        split_hi(act, base + 7, v)
                        turn(f + i + 1)
                        silu(f + i + 1, v * RAW + (base + 6))
                        for j in (8, 9, 10, 11):
                            split_hi(act, base + j, v)
                    turn(f + FCH)
                    if not last_one:
                        split_hi(act, base + 42, r)
                        take_gathered(e * 2 + (2 * done + 3))
                        split_hi(act, base + 43, r)
                    else:
                        ready_root(4 + done // NEXP)
                    act.wait_ge(unit_used, r * RAW + (base + FFN_UNITS))
                    act.wait_ge(slot_w_ready, e + (done + 1))
                    run(ey_hi[:], ps[:, 2:4, :].rearrange("p b n -> p (b n)"), ACT.Copy, scale=slot_w[:, 0:1])\
                        .then_inc(ey_hi_ready, 1)
                    if not last_one:
                        split_hi(act, base + 44, r)

                if done:
                    for j in range(3):
                        split_hi(act, base + j)
                take_gathered(2 * done + 1)
                with act.Fori(0, NEXP - 1) as e:
                    expert(e, False)
                expert(NEXP - 1, True)

            act.wait_ge(spare_set, 1)
            ready_root(0)
            for t in range(2):
                act.wait_ge(x_in[t], 16)
                root(t)
            turn_normed(0, 0)
            split_hi(act, 0)
            turn_normed(0, 1)
            split_hi(act, 1)
            split_hi(act, 2)
            mixer(0)
            cross(1, DENSE0)
            dense()
            cross(2, MIX0[1])
            mixer(1)
            run(rt[:, :, 0:NEXP], router[:], ACT.Copy).then_inc(router_hi, 1)
            cross(3, MOE0)
            for t in range(2):
                act.wait_ge(normed, 7 + t)
                run(tok_hi[:, t, :], wide[:, t, :], ACT.Copy).then_inc(tok_hi_ready, 1)
            act.wait_ge(gap_ready, 1)
            run(prob[:, 2:4], prob[:, 0:2], ACT.Exp).then_inc(gap_exp, 1)
            split_hi(act, MOE0 + 2)
            experts(MOE0, 0)
            act.wait_ge(routed, 1)
            flag = act.value_load(crowded[0:1, 0:1], min_val=0, max_val=1)
            with act.If(flag > 0):
                experts(CROWD0, NEXP)
            for t in range(2):
                act.wait_ge(res_final, t + 1)
                root(t)

        @block.vector
        def _(dve):
            chain = Chain(vector_chain, dve)
            v = nc.vector

            def rsqrt(o, root, sum_sq, scale, tmp):
                chain(v.reciprocal(o, root))
                chain(v.tensor_scalar(tmp, sum_sq, -0.5 * scale, -0.5 * EPS, ALU.mult, ALU.add))
                chain(v.tensor_tensor(tmp, tmp, o, ALU.mult))
                chain(v.tensor_tensor(tmp, tmp, o, ALU.mult))
                chain(v.scalar_tensor_tensor(o, tmp, 1.5, o, ALU.add, ALU.mult))

            def normalise_tile(q, t, weights):
                dve.wait_ge(root_ready, 2 * q + t + 1)
                rsqrt(stat[:, 4 + t:5 + t], stat[:, 2 + t:3 + t], stat[:, t:t + 1], 1.0 / D, stat[:, 6 + t:7 + t])
                dve.wait_ge(norm_w_ps, q + 1)
                two = lambda a: a.rearrange("p (b n) -> p b n", b=2)
                v.scalar_tensor_tensor(two(wide[:, t, :]), two(res[:, t, :]), stat[:, 4 + t:5 + t], weights,
                                       ALU.mult, ALU.mult).then_inc(normed if q < 4 else out_ready, 1)

            def turn_normed(q, t):
                for half in range(2):
                    dve.wait_ge(xT_hi_ready, 4 * q + 2 * t + half + 1)
                    part = (slice(None), slice(4 * half, 4 * half + 4), slice(t * P, t * P + P))
                    v.tensor_tensor(xT_lo[part],
                                    ps[:, 2 + 2 * t + half, :].rearrange("p (k t) -> p k t", k=4),
                                    xT_hi[part].bitcast(F32), ALU.subtract).then_inc(xT_lo_ready, 1)

            def cross(q, n, sums, weights):
                def add_residual(t):
                    two = res[:, t, :].rearrange("p (b n) -> p b n", b=2)
                    v.tensor_tensor(two, two, sums[t], ALU.add).then_inc(res_added, 1)

                split_lo(dve, n)
                dve.wait_ge(tile0_summed, q)
                add_residual(0)
                normalise_tile(q, 0, weights)
                dve.wait_ge(unit_used, n)
                add_residual(1)
                turn_normed(q, 0)
                if q < 3:
                    split_lo(dve, n + 1)
                normalise_tile(q, 1, weights)
                turn_normed(q, 1)
                if q < 3:
                    split_lo(dve, n + 2)

            def mixer(L):
                base = MIX0[L]

                def rope(k, dst, bank):
                    if k or L:
                        rope_done.wait(dve, k, L)
                    for t in range(2):
                        heads = ps[:, bank + t, :].rearrange("p (h d) -> p h d", h=8)
                        cos = const("cos")[:, t * HEAD:t * HEAD + HEAD]
                        sin = const("sin")[:, t * HEAD:t * HEAD + HEAD]
                        o = dst(t).rearrange("p (h d) -> p h d", h=8)
                        tmp = rope_tmp.rearrange("p (h d) -> p h d", h=8)
                        half = HEAD // 2
                        v.tensor_tensor(o, heads, cos.unsqueeze(1).to_broadcast([P, 8, HEAD]), ALU.mult)
                        v.tensor_tensor(tmp[:, :, 0:half], heads[:, :, half:HEAD],
                                        sin[:, 0:half].unsqueeze(1).to_broadcast([P, 8, half]), ALU.mult)
                        chain(v.tensor_tensor(tmp[:, :, half:HEAD], heads[:, :, 0:half],
                                              sin[:, half:HEAD].unsqueeze(1).to_broadcast([P, 8, half]), ALU.mult))
                        last = v.tensor_tensor(dst(t), dst(t), rope_tmp, ALU.add)
                        if t == 0:
                            chain(last)
                    last.then_inc(rope_done.sem, 1)

                def row_max(g):
                    scores_ps.wait(dve, g + 1, L)
                    v.tensor_reduce(stat[:, 8:12], ps[:, 5:7, :].rearrange("p b (j q) -> p (b j) q", j=2),
                                    AX_X, ALU.max)
                    chain(v.tensor_reduce(stat[:, 12:16], ps[:, 7, :].rearrange("p (j q) -> p j q", j=4),
                                          AX_X, ALU.max))
                    v.tensor_scalar(stat[:, 16:24], stat[:, 8:16], -HEAD ** -0.5, None, ALU.mult)\
                        .then_inc(max_ready.sem, 1)

                def normalise(g):
                    exp_done.wait(dve, g + 1, L)
                    chain(v.reciprocal(stat[:, 24:32], stat[:, 24:32]))
                    v.tensor_tensor(probs[:, :, 0:SEQ], probs[:, :, 0:SEQ],
                                    stat[:, 24:28].unsqueeze(2).to_broadcast([P, 4, SEQ]), ALU.mult)
                    v.tensor_tensor(probs[:, :, SEQ:SEQ + P], probs[:, :, SEQ:SEQ + P],
                                    stat[:, 28:32].unsqueeze(2).to_broadcast([P, 4, P]), ALU.mult)\
                        .then_inc(probs_ready.sem, 1)

                def turn_probs(g):
                    probsT_ps.wait(dve, g + 1, L)
                    v.tensor_copy(probsT[:, :, SEQ:SEQ + P], ps[:, 7, :].rearrange("p (j q) -> p j q", j=4))\
                        .then_inc(probsT_ready1.sem, 1)

                def turn_attention(g):
                    attn_hi.wait(dve, g + 1, L)
                    v.tensor_tensor(yA_lo[:, 2 * g:2 * g + 2, :], ps[:, 4, :].rearrange("p (c t) -> p c t", c=2),
                                    yA_hi[:, 2 * g:2 * g + 2, :].bitcast(F32), ALU.subtract)\
                        .then_inc(attn_lo.sem, 1)

                def merge(b, half):
                    gate_ready.wait(dve, 2 * b + half + 1, L)
                    y = ps[:, 4 + 2 * half:6 + 2 * half, :]
                    g = gates[:, :, half * 512:half * 512 + 512]
                    m = wide[:, :, half * 512:half * 512 + 512]
                    if b == 0:
                        v.tensor_tensor(m, y, g, ALU.mult).then_inc(merged.sem, 1)
                    else:
                        chain(v.tensor_tensor(g, y, g, ALU.mult))
                        v.tensor_tensor(m, m, g, ALU.add).then_inc(merged.sem, 1)

                def turn_merged(half, bank0):
                    for t in range(2):
                        mT_hi.wait(dve, 2 * half + t + 1, L)
                        part = (slice(None), slice(4 * half, 4 * half + 4), slice(t * P, t * P + P))
                        v.tensor_tensor(xT_lo[part], ps[:, bank0 + t, :].rearrange("p (k t) -> p k t", k=4),
                                        xT_hi[part].bitcast(F32), ALU.subtract).then_inc(mT_lo.sem, 1)

                for m in range(3, MIX_UNITS):
                    dve.wait_ge(unit_used, base + m - 2)
                    if m == 4:
                        rope(0, lambda t: wide[:, t, 0:512], 6)
                    if m == 6:
                        if L == 0:
                            dve.wait_ge(chan_ps, 1)
                            v.tensor_copy(chan[:], ps[:, 4, 0:40])
                        rope(1, lambda t: wide[:, t, 512:1024], 2)
                    if m == 8:
                        qkT_ps.wait(dve, 1, L)
                        v.tensor_copy(kT[:].rearrange("p c t -> p (c t)"),
                                      ps[:, 6:8, :].rearrange("p b n -> p (b n)")).then_inc(kT_ready.sem, 1)
                    if m == 10:
                        row_max(0)
                        rope(2, lambda t: ret_qk[:, t, :], 2)
                    if m == 11:
                        normalise(0)
                    if m == 13:
                        turn_probs(0)
                    if m == 14:
                        row_max(1)
                        turn_attention(0)
                    if m == 15:
                        normalise(1)
                    if m == 16:
                        conv_c_copied.wait(dve, 1, L)
                        chain(v.tensor_tensor(uT[:, :, 2:SEQ + 2], conv_c,
                                              ps[:, 0:2, :].rearrange("p b (c t) -> p (b c) t", c=2), ALU.mult))
                        w = lambda j, c: chan[:, 8 + L * 12 + j * 4 + c:9 + L * 12 + j * 4 + c]
                        for c in range(BT):
                            last = v.tensor_scalar(conv[:, c, :], uT[:, c, 2:SEQ + 2], w(2, c),
                                                   chan[:, 32 + L * 4 + c:33 + L * 4 + c], ALU.mult, ALU.add)
                        chain(last)
                        for c in range(BT):
                            last = v.scalar_tensor_tensor(conv[:, c, :], uT[:, c, 1:SEQ + 1], w(1, c),
                                                          conv[:, c, :], ALU.mult, ALU.add)
                        chain(last)
                        for c in range(BT):
                            last = v.scalar_tensor_tensor(conv[:, c, :], uT[:, c, 0:SEQ], w(0, c),
                                                          conv[:, c, :], ALU.mult, ALU.add)
                        last.then_inc(conv_u_ready.sem, 1)
                    if m == 17:
                        turn_probs(1)
                    if m == 18:
                        conv_u_ready.wait(dve, 1, L)
                        v.tensor_tensor(conv, conv, ps[:, 2:4, :].rearrange("p b (c t) -> p (b c) t", c=2),
                                        ALU.mult).then_inc(conv_y_ready.sem, 1)
                        turn_attention(1)
                        v.tensor_tensor(kzeta[:].rearrange("p (h d) -> p h d", h=RET_HEADS),
                                        ret_qk[:, 0, SEQ:2 * SEQ].rearrange("p (h d) -> p h d", h=RET_HEADS),
                                        const("zeta").unsqueeze(2).to_broadcast([P, RET_HEADS, HEAD]), ALU.mult)
                        ret_qkT_ps.wait(dve, 1, L)
                        v.tensor_copy(rkT[:].rearrange("p c t -> p (c t)"), ps[:, 6, :])
                        rqT_ready.wait(dve, 1, L)
                        v.tensor_tensor(rqxT[:], rqT[:, :, P:SEQ], const("xi").rearrange("p (c t) -> p c t", c=2),
                                        ALU.mult).then_inc(rkT_ready.sem, 1)
                        conv_hi.wait(dve, 1, L)
                        v.tensor_tensor(yC_lo[:], conv, yC_hi[:].bitcast(F32), ALU.subtract)\
                            .then_inc(conv_lo.sem, 1)
                    if m == 20:
                        ret_scores_ps.wait(dve, 1, L)
                        v.tensor_copy(state[:], ps[:, 7, 0:2 * P])
                        v.tensor_tensor(decayed.rearrange("p (t n) -> p t n", t=2), ps[:, 5:7, :],
                                        const("decay").unsqueeze(1).to_broadcast([P, 2, 512]), ALU.mult)\
                            .then_inc(decayed_ready.sem, 1)
                    if m == 22:
                        ret_sq_done.wait(dve, 1, L)
                        v.tensor_reduce(stat[:, 32:40], squares.rearrange("p (h d) -> p h d", d=P), AX_X, ALU.add)\
                            .then_inc(ret_ss_ready.sem, 1)
                    if m == 23:
                        ret_root.wait(dve, 1, L)
                        rsqrt(stat[:, 48:56], stat[:, 40:48], stat[:, 32:40], 1.0 / P, stat[:, 56:64])
                        ret_gate_ready.wait(dve, 1, L)
                        chain(v.tensor_tensor(ret_o[:].rearrange("p t (h d) -> p (t h) d", d=P),
                                              ps[:, 5:7, :].rearrange("p t (h d) -> p (t h) d", d=P),
                                              stat[:, 48:56].unsqueeze(2).to_broadcast([P, 8, P]), ALU.mult))
                        v.tensor_tensor(ret_o[:], ret_o[:], ret_gate[:], ALU.mult).then_inc(ret_y_ready.sem, 1)
                    if m == 26:
                        merge(0, 0)
                        merge(0, 1)
                        ret_hi.wait(dve, 1, L)
                        for c in range(BT):
                            last = v.scalar_tensor_tensor(
                                yA_lo[:, c, :], ps[:, c // 2, (c % 2) * SEQ:(c % 2) * SEQ + SEQ],
                                chan[:, L * BT + c:L * BT + c + 1], yA_hi[:, c, :].bitcast(F32),
                                ALU.mult, ALU.subtract)
                        last.then_inc(ret_lo.sem, 1)
                    if m == 32:
                        merge(1, 0)
                        merge(1, 1)
                    if m == 36:
                        merge(2, 0)
                    if m == 37:
                        turn_merged(0, 2)
                    if m == 38:
                        merge(2, 1)
                    if m == 39:
                        turn_merged(1, 0)
                    split_lo(dve, base + m)

            def dense():
                def activate(i):
                    dve.wait_ge(dn_silu, i)
                    v.tensor_tensor(dn_act[:], dn_sil[:], ps[:, 2:4, :], ALU.mult).then_inc(dn_ready, 1)

                def turn(i):
                    dve.wait_ge(dnT_hi_ready, i)
                    for t in range(2):
                        tok = slice(t * P, t * P + P)
                        last = v.tensor_tensor(dnT_lo[:, :, tok],
                                               ps[:, 2 + t, :].rearrange("p (k n) -> p k n", k=4),
                                               dnT_hi[:, :, tok].bitcast(F32), ALU.subtract)
                    last.then_inc(dnT_lo_ready, 1)

                split_lo(dve, DENSE0 + 3)
                split_lo(dve, DENSE0 + 4)
                with dve.Fori(0, 6) as i:
                    split_lo(dve, DENSE0 + 5, i)
                    dve.wait_ge(unit_used, i * RAW + (DENSE0 + 4))
                    activate(i + 1)
                    split_lo(dve, DENSE0 + 6, i)
                    turn(i + 1)
                    for j in (7, 8, 9, 10):
                        split_lo(dve, DENSE0 + j, i)
                split_lo(dve, DENSE0 + 41)
                dve.wait_ge(unit_used, DENSE0 + 40)
                activate(FCH)
                turn(FCH)

            def one_hot(e):
                for t in range(2):
                    last = v.tensor_scalar(put_in[:, t, :], const("iota"), slot_of[:, t, bass.ds(e, 1)], None,
                                           ALU.is_equal)
                last.then_inc(put_in_ready, 1)

            def route():
                split_lo(dve, MOE0 + 1)
                for t in range(2):
                    dve.wait_ge(tok_hi_ready, t + 1)
                    v.tensor_tensor(tok_lo[:, t, :], wide[:, t, :], tok_hi[:, t, :].bitcast(F32), ALU.subtract)\
                        .then_inc(tok_lo_ready, 1)
                dve.wait_ge(logits_ps, 1)
                parts = ps[:, 0, 0:4 * NEXP].rearrange("p (t h e) -> p t h e", t=2, h=2)
                chain(v.tensor_copy(logits[:], parts[:, :, 0, :]))
                chain(v.tensor_tensor(logits[:], logits[:], parts[:, :, 1, :], ALU.add))
                for t in range(2):
                    chain(v.max(top[:, t, :], logits[:, t, :]))
                    chain(v.max_index(top_at[:, t, :], top[:, t, :], logits[:, t, :]))
                chain(v.tensor_copy(top_f[:], top_at[:]))
                v.tensor_tensor(prob[:, 0:2], top[:, :, 1], top[:, :, 0], ALU.subtract).then_inc(gap_ready, 1)
                eight = const("iota")[:, 0:NEXP]
                for t in range(2):
                    v.tensor_scalar(first[:, t, :], eight, top_f[:, t, 0:1], None, ALU.is_equal)
                    chain(v.tensor_scalar(second[:, t, :], eight, top_f[:, t, 1:2], None, ALU.is_equal))
                v.tensor_tensor(chosen[:], first[:], second[:], ALU.add).then_inc(chosen_ready, 1)
                dve.wait_ge(gap_exp, 1)
                chain(v.tensor_scalar(prob[:, 4:6], prob[:, 2:4], 1.0, None, ALU.add))
                chain(v.reciprocal(prob[:, 4:6], prob[:, 4:6]))
                chain(v.tensor_tensor(prob[:, 6:8], prob[:, 2:4], prob[:, 4:6], ALU.mult))
                for t in range(2):
                    chain(v.tensor_scalar(share[:, t, :], first[:, t, :], prob[:, 4 + t:5 + t], None, ALU.mult))
                    chain(v.scalar_tensor_tensor(share[:, t, :], second[:, t, :], prob[:, 6 + t:7 + t],
                                                 share[:, t, :], ALU.mult, ALU.add))
                dve.wait_ge(chosen_ready, 1)
                dve.wait_ge(places_ps, 1)
                mine = slot_of[:]
                chain(v.scalar_tensor_tensor(mine, ps[:, 7, 0:16].rearrange("p (t e) -> p t e", t=2), 1.0,
                                             chosen[:], ALU.add, ALU.mult))
                chain(v.tensor_scalar(mine, mine, -1.0, None, ALU.add))
                one_hot(0)
                dve.wait_ge(totals_ps, 1)
                chain(v.tensor_reduce(stat[:, 8:9], ps[:, 4, 0:8], AX_X, ALU.max))
                v.tensor_scalar(crowded[:], stat[:, 8:9], float(P), None, ALU.is_gt).then_inc(routed, 1)
                split_lo(dve, MOE0 + 2)

            def experts(base, done):
                def take_gathered(n):
                    for half in range(2):
                        dve.wait_ge(ex_hi_ready, n + half + 1)
                        v.tensor_tensor(ex_lo[:, 4 * half:4 * half + 4, :],
                                        ps[:, 5 + half, :].rearrange("p (k t) -> p k t", k=4),
                                        ex_hi[:, 4 * half:4 * half + 4, :].bitcast(F32), ALU.subtract)\
                            .then_inc(ex_lo_ready, 1)

                def expert(e, last_one):
                    r = e * FCH
                    f = r + done * FCH

                    def activate(n, unit):
                        dve.wait_ge(unit_used, unit)
                        dve.wait_ge(ex_silu, n)
                        v.tensor_tensor(ex_act[:], ex_sil[:], ps[:, 1, :], ALU.mult).then_inc(ex_ready, 1)

                    def turn(n):
                        dve.wait_ge(exT_hi_ready, n)
                        v.tensor_tensor(exT_lo[:], ps[:, 4, :].rearrange("p (k t) -> p k t", k=4),
                                        exT_hi[:].bitcast(F32), ALU.subtract).then_inc(exT_lo_ready, 1)

                    split_lo(dve, base + 4, r)
                    split_lo(dve, base + 5, r)
                    activate(f + 1, r * RAW + (base + 4))
                    dve.wait_ge(put_back_ready, e + (done + 1))
                    v.tensor_copy(slot_w[:], ps[:, 7, SEQ:SEQ + 1]).then_inc(slot_w_ready, 1)
                    if not last_one:
                        one_hot(e + 1)
                    with dve.Fori(0, 6) as i:
                        w = r + i
                        split_lo(dve, base + 6, w)
                        split_lo(dve, base + 7, w)
                        turn(f + i + 1)
                        split_lo(dve, base + 8, w)
                        split_lo(dve, base + 9, w)
                        activate(f + i + 2, w * RAW + (base + 8))
                        split_lo(dve, base + 10, w)
                        split_lo(dve, base + 11, w)
                    turn(f + FCH)
                    if not last_one:
                        split_lo(dve, base + 42, r)
                        take_gathered(e * 2 + (2 * done + 2))
                        split_lo(dve, base + 43, r)
                    dve.wait_ge(ey_hi_ready, e + (done + 1))
                    v.scalar_tensor_tensor(ey_lo[:], ps[:, 2:4, :].rearrange("p b n -> p (b n)"), slot_w[:, 0:1],
                                           ey_hi[:].bitcast(F32), ALU.mult, ALU.subtract).then_inc(ey_lo_ready, 1)
                    if not last_one:
                        split_lo(dve, base + 44, r)
                        split_lo(dve, base + 45, r)
                    for t in range(2):
                        dve.wait_ge(back_ps, e * 2 + (2 * done + t + 1))
                        v.tensor_tensor(res[:, t, :], res[:, t, :],
                                        ps[:, 4 + 2 * t:6 + 2 * t, :].rearrange("p b n -> p (b n)"), ALU.add)\
                            .then_inc(ex_added, 1)

                if done:
                    one_hot(0)
                    for j in range(3):
                        split_lo(dve, base + j)
                take_gathered(2 * done)
                split_lo(dve, base + 3)
                with dve.Fori(0, NEXP - 1) as e:
                    expert(e, False)
                expert(NEXP - 1, True)

            low_weights = ps[:, 0:2, :]
            for t in range(2):
                dve.wait_ge(x_in[t], 16)
                normalise_tile(0, t, low_weights)
            turn_normed(0, 0)
            split_lo(dve, 0)
            turn_normed(0, 1)
            split_lo(dve, 1)
            split_lo(dve, 2)
            dve.wait_ge(consts_in, 16)
            dve.wait_ge(pads_set, 1)
            out_proj_sums = (ps[:, 2:4, :], ps[:, 4:6, :])
            down_sums = (ps[:, 4:6, :], ps[:, 6:8, :])
            mixer(0)
            cross(1, DENSE0, out_proj_sums, ps[:, 6:8, :])
            dense()
            cross(2, MIX0[1], down_sums, low_weights)
            mixer(1)
            dve.wait_ge(router_hi, 1)
            v.tensor_tensor(rt[:, :, NEXP:2 * NEXP], router[:], rt[:, :, 0:NEXP].bitcast(F32), ALU.subtract)\
                .then_inc(router_lo, 1)
            cross(3, MOE0, out_proj_sums, ps[:, 6:8, :])
            route()
            dve.wait_ge(routed, 1)
            flag = dve.value_load(crowded[0:1, 0:1], min_val=0, max_val=1)
            experts(MOE0, 0)

            def finish(n):
                for t in range(2):
                    dve.wait_ge(ex_added, n - 1 + t)
                    v.memset(stat[:, 8 + t:9 + t], 0.0).then_inc(res_final, 1)

            with dve.If(flag > 0):
                dve.wait_ge(ex_added, 2 * NEXP)
                v.tensor_scalar(slot_of[:], slot_of[:], -float(P), None, ALU.add).then_inc(slots_moved, 1)
                dve.wait_ge(slots_moved, 1)
                experts(CROWD0, NEXP)
                finish(4 * NEXP)
            with dve.Else():
                finish(2 * NEXP)
            for t in range(2):
                normalise_tile(4, t, low_weights)


_INS = ["x", "mix_norm_w", "w_in", "conv_w", "conv_b", "ret_norm_w", "w_br_attn", "w_br_conv", "w_br_ret",
        "w_out", "ffn_norm_w", "dense_w_gate", "dense_w_up", "dense_w_down", "moe_router", "moe_w_gate",
        "moe_w_up", "moe_w_down", "final_norm_w"]


def kernel(**inputs):
    import numpy as _np
    import concourse.bacc as _bacc
    from concourse import mybir as _mybir
    from concourse.bass_utils import run_bass_kernel_spmd as _run

    nc = _bacc.Bacc("TRN2", target_bir_lowering=False, num_devices=1)
    consts, masks = shape_constants()
    arrays, args = {}, []
    for name, a in [(n, inputs[n]) for n in _INS] + [("consts", consts), ("masks", masks)]:
        a = _np.ascontiguousarray(a)
        arrays[f"in_{name}_dram"] = a
        args.append(nc.dram_tensor(f"in_{name}_dram", a.shape, _mybir.dt.from_np(a.dtype), kind="ExternalInput").ap())
    args.append(nc.dram_tensor("out_0_dram", (1, SEQ, D), F32, kind="ExternalOutput").ap())
    hybrid_trunk_kernel(nc, *args)
    r = _run(nc, [arrays], core_ids=[0])
    return r.results[0]["out_0_dram"]
```

```python
from contextlib import ExitStack

import numpy as np

import concourse.bass as bass
from concourse import mybir

F32 = mybir.dt.float32
F32R = mybir.dt.float32r
BF16 = mybir.dt.bfloat16
I32 = mybir.dt.int32
U32 = mybir.dt.uint32
ALU = mybir.AluOpType
ACT = mybir.ActivationFunctionType
AX_X = mybir.AxisListType.X

P = 128
DEPTH = 2
SEQ = 256
D = 1024
KT = D // P
HEAD = 64
EPS = 1e-6
ATTN_HEADS = 8
RET_HEADS = 4
BR_W = 512
BT = BR_W // P
FF = 3584
FCH = FF // 512
NEXP = 8

UNIT = 2048
RAW = 6
SPLIT = 3
DEEP = 2 * RAW
MIX_UNITS = 40
FFN_UNITS = 6 * FCH
CHUNKS = (0, 1, 2, 6, 7, 4, 5, 3, 8, 9, 10, 11, 12, 13, 14)
BR_ATTN, BR_CONV, BR_RET, OUT_PROJ = 22, 28, 32, 36

CONST_PARTS = (("ident", 128), ("cos", 128), ("sin", 128), ("decay", 512), ("xi", 256), ("zeta", 4),
               ("iota", 128), ("before", 128), ("ones", 128))
CONST_AT = {}
CONST_W = 0
for _name, _w in CONST_PARTS:
    CONST_AT[_name] = (CONST_W, CONST_W + _w)
    CONST_W += _w


def shape_constants():
    c = np.zeros((P, CONST_W), np.float32)

    def put(name, a):
        lo, hi = CONST_AT[name]
        c[:a.shape[0], lo:hi] = a

    inv_freq = (1.0 / (np.float32(10000.0) ** (np.arange(0, HEAD, 2, dtype=np.float32) / HEAD))).astype(np.float32)
    ang = np.arange(SEQ, dtype=np.float32)[:, None] * inv_freq[None, :]
    cos, sin = np.cos(ang), np.sin(ang)
    tokens = lambda a: a.reshape(2, P, HEAD).transpose(1, 0, 2).reshape(P, 2 * HEAD)
    put("cos", tokens(np.concatenate([cos, cos], 1)))
    put("sin", tokens(np.concatenate([-sin, sin], 1)))
    log_g = np.log1p(-np.exp2(-5.0 - np.arange(RET_HEADS, dtype=np.float32))).astype(np.float32)
    n = np.arange(P, dtype=np.float32)
    diff = n[None, :] - n[:, None]
    scale = np.float32(HEAD ** -0.5)
    decay = np.where(diff[None] >= 0, np.exp(np.maximum(diff, 0)[None] * log_g[:, None, None]), 0) * scale
    put("decay", decay.transpose(1, 0, 2).reshape(P, RET_HEADS * P))
    xi = np.exp((n + 1)[None, :] * log_g[:, None])
    put("xi", np.repeat(xi.reshape(2, 2, P), HEAD, axis=1).reshape(2, P, P).transpose(1, 0, 2).reshape(P, 2 * P))
    put("zeta", (np.exp((P - 1 - n)[None, :] * log_g[:, None]) * scale).T)
    put("ident", np.eye(P))
    put("iota", np.tile(n, (P, 1)))
    put("before", np.triu(np.ones((P, P)), 1))
    put("ones", np.ones((P, P)))
    masks = np.zeros((P, 3 * P), np.float32)
    masks[:, :P] = np.eye(P)
    masks[:, 2 * P:] = np.triu(np.full((P, P), -1e30), 1)
    return c, masks


class Signal:

    def __init__(self, sem, per_layer=0):
        self.sem, self.per_layer = sem, per_layer

    def wait(self, eng, k, layer=0):
        eng.wait_ge(self.sem, layer * self.per_layer + k)


class Chain:

    def __init__(self, sem, eng):
        self.sem, self.eng, self.n = sem, eng, 0

    def __call__(self, ins):
        self.n += 1
        ins.then_inc(self.sem, 1)
        self.eng.wait_ge(self.sem, self.n)


def hybrid_trunk_kernel(nc, x, mix_norm_w, w_in, conv_w, conv_b, ret_norm_w, w_br_attn, w_br_conv,
                        w_br_ret, w_out, ffn_norm_w, dense_w_gate, dense_w_up, dense_w_down,
                        moe_router, moe_w_gate, moe_w_up, moe_w_down, final_norm_w,
                        consts, masks, out):
    ctx = ExitStack()
    with ctx:
        at = [(nc.sbuf_base + 31) // 32 * 32]

        def place(name, shape, dt):
            size = int(np.prod(shape[1:])) * (2 if dt == BF16 else 4)
            t = nc.alloc_sbuf_tensor_at(name, shape, dt, offset=at[0])
            at[0] += (size + 31) // 32 * 32
            return t

        raw = place("raw", [P, RAW, UNIT], F32)
        w_hi = place("w_hi", [P, SPLIT, UNIT], F32R)
        w_lo = place("w_lo", [P, SPLIT, UNIT], F32R)
        res = place("res", [P, 2, D], F32)
        wide_at = at[0]
        wide = place("wide", [P, 2, D], F32)
        cst_at = at[0]
        cst = place("cst", [P, CONST_W], F32)
        msk = place("msk", [P, 3 * P], BF16)
        zeros = place("zeros", [P, 512], BF16)
        norm_w = place("norm_w", [P, D], F32)
        chan = place("chan", [P, 40], F32)
        stat = place("stat", [P, 64], F32)
        spare = place("spare", [P, 9], F32)
        router = place("router", [P, KT, NEXP], F32)
        rt = place("rt", [P, KT, 2 * NEXP], F32R)
        region = at[0]
        xT_hi = place("xT_hi", [P, KT, SEQ], F32R)
        xT_lo = place("xT_lo", [P, KT, SEQ], F32R)
        after_xT = at[0]
        ret_qk = place("ret_qk", [P, 2, 512], F32)
        gates_at = at[0]
        qT = place("qT", [P, BT, SEQ], F32)
        kT = place("kT", [P, BT, SEQ], F32)
        v_at = at[0]
        v_attn = place("v_attn", [P, 2, BR_W], F32)
        probs = place("probs", [P, 4, 384], F32)
        probsT = place("probsT", [P, 4, 384], F32)
        yA_hi = place("yA_hi", [P, BT, SEQ], F32R)
        yA_lo = place("yA_lo", [P, BT, SEQ], F32R)
        yC_hi = place("yC_hi", [P, BT, SEQ], F32R)
        yC_lo = place("yC_lo", [P, BT, SEQ], F32R)
        uT = place("uT", [P, BT, SEQ + 2], F32)
        rqT = place("rqT", [P, 2, SEQ], F32)
        rkT = place("rkT", [P, 2, SEQ], F32)
        rqxT = place("rqxT", [P, 2, P], F32)
        kzeta = place("kzeta", [P, 4 * HEAD], F32)
        state = place("state", [P, 2 * P], F32)
        v_ret = place("v_ret", [P, 2, BR_W], F32)
        ret_gate = place("ret_gate", [P, 2, BR_W], F32)
        assert at[0] <= nc.sbuf_usable_end, at[0]
        chan_rows = nc.alloc_sbuf_tensor_at("chan_rows", [40, P], F32, offset=at[0] - BR_W * 8)
        gates = nc.alloc_sbuf_tensor_at("gates", [P, 2, D], F32, offset=gates_at)
        ret_o = nc.alloc_sbuf_tensor_at("ret_o", [P, 2, BR_W], F32, offset=v_at)
        rope_tmp = probsT[:].rearrange("p a b -> p (a b)")[:, 0:512]
        decayed = probsT[:].rearrange("p a b -> p (a b)")[:, 0:1024]
        squares = probs[:].rearrange("p a b -> p (a b)")[:, 0:1024]
        conv = wide[:, 0, :].rearrange("p (c t) -> p c t", c=BT)
        conv_c = wide[:, 1, :].rearrange("p (c t) -> p c t", c=BT)
        at[0] = after_xT
        dn_act = place("dn_act", [P, 2, 512], F32)
        dn_sil = place("dn_sil", [P, 2, 512], F32)
        dnT_hi = place("dnT_hi", [P, 4, SEQ], F32R)
        dnT_lo = place("dnT_lo", [P, 4, SEQ], F32R)
        at[0] = after_xT
        tok_hi = place("tok_hi", [P, 2, D], F32R)
        tok_lo = place("tok_lo", [P, 2, D], F32R)
        deep = place("deep", [P, RAW, UNIT], F32)
        assert at[0] <= nc.sbuf_usable_end, at[0]
        at[0] = region
        ex_hi = place("ex_hi", [P, KT, P], F32R)
        ex_lo = place("ex_lo", [P, KT, P], F32R)
        ex_act = place("ex_act", [P, 512], F32)
        ex_sil = place("ex_sil", [P, 512], F32)
        exT_hi = place("exT_hi", [P, 4, P], F32R)
        exT_lo = place("exT_lo", [P, 4, P], F32R)
        assert at[0] <= after_xT, at[0]
        at[0] = wide_at
        ey_hi = place("ey_hi", [P, D], F32R)
        ey_lo = place("ey_lo", [P, D], F32R)
        assert at[0] <= cst_at, at[0]
        at[0] = cst_at + CONST_AT["cos"][0] * 4
        put_in = place("put_in", [P, 2, P], F32R)
        put_back = place("put_back", [P, SEQ], F32R)
        logits = place("logits", [P, 2, NEXP], F32)
        top = place("top", [P, 2, NEXP], F32)
        top_at = place("top_at", [P, 2, NEXP], U32)
        top_f = place("top_f", [P, 2, NEXP], F32)
        first = place("first", [P, 2, NEXP], F32)
        second = place("second", [P, 2, NEXP], F32)
        chosen = place("chosen", [P, 2, NEXP], F32)
        share = place("share", [P, 2, NEXP], F32)
        slot_of = place("slot_of", [P, 2, NEXP], F32)
        prob = place("prob", [P, 8], F32)
        slot_w = place("slot_w", [P, 1], F32)
        crowded = place("crowded", [P, 1], I32)
        assert at[0] <= cst_at + CONST_AT["xi"][1] * 4, at[0]

        ps = ctx.enter_context(nc.psum_tensor("ps", [P, 8, 512], F32))

        def const(name, rows=P):
            lo, hi = CONST_AT[name]
            return cst[0:rows, lo:hi]

        ident = const("ident")

        def sem(name):
            return ctx.enter_context(nc.semaphore(name))

        def signal(name, per_layer=0):
            return Signal(sem(name), per_layer)

        x_in = [sem("x_in0"), sem("x_in1")]
        norm_w_in = sem("norm_w_in")
        consts_in = sem("consts_in")
        params_in = sem("params_in")
        landed = [sem(f"landed{i}") for i in range(RAW)]
        deep_landed = [sem(f"deep_landed{i}") for i in range(RAW)]
        hi_ready = sem("hi_ready")
        lo_ready = sem("lo_ready")
        unit_used = sem("unit_used")
        spare_set = sem("spare_set")
        zeros_set = sem("zeros_set")
        pads_set = sem("pads_set")
        masks_cast = sem("masks_cast")
        chan_ps = sem("chan_ps")
        tensor_chain = sem("tensor_chain")
        scalar_chain = sem("scalar_chain")
        vector_chain = sem("vector_chain")
        root_ready = sem("root_ready")
        normed = sem("normed")
        normed_ps = sem("normed_ps")
        xT_hi_ready = sem("xT_hi_ready")
        xT_lo_ready = sem("xT_lo_ready")
        res_added = sem("res_added")
        tile0_summed = sem("tile0_summed")
        rope_done = signal("rope_done", 3)
        v_copied = signal("v_copied", 2)
        qkT_ps = signal("qkT_ps", 1)
        qT_ready = signal("qT_ready", 1)
        kT_ready = signal("kT_ready", 1)
        scores_ps = signal("scores_ps", 2)
        max_ready = signal("max_ready", 2)
        exp_done = signal("exp_done", 2)
        probs_ready = signal("probs_ready", 2)
        probsT_ps = signal("probsT_ps", 2)
        probsT_ready0 = signal("probsT_ready0", 2)
        probsT_ready1 = signal("probsT_ready1", 2)
        attn_ps = signal("attn_ps", 2)
        attn_hi = signal("attn_hi", 2)
        attn_lo = signal("attn_lo", 2)
        conv_c_copied = signal("conv_c_copied", 1)
        conv_u_ready = signal("conv_u_ready", 1)
        conv_y_ready = signal("conv_y_ready", 1)
        conv_hi = signal("conv_hi", 1)
        conv_lo = signal("conv_lo", 1)
        ret_qkT_ps = signal("ret_qkT_ps", 1)
        rqT_ready = signal("rqT_ready", 1)
        rkT_ready = signal("rkT_ready", 1)
        ret_scores_ps = signal("ret_scores_ps", 1)
        decayed_ready = signal("decayed_ready", 1)
        ret_o_ps = signal("ret_o_ps", 1)
        ret_sq_done = signal("ret_sq_done", 1)
        ret_ss_ready = signal("ret_ss_ready", 1)
        ret_root = signal("ret_root", 1)
        ret_gate_ready = signal("ret_gate_ready", 1)
        ret_y_ready = signal("ret_y_ready", 1)
        ret_yT_ps = signal("ret_yT_ps", 1)
        ret_hi = signal("ret_hi", 1)
        ret_lo = signal("ret_lo", 1)
        gate_ready = signal("gate_ready", 6)
        merged = signal("merged", 6)
        mergedT_ps = signal("mergedT_ps", 4)
        mT_hi = signal("mT_hi", 4)
        mT_lo = signal("mT_lo", 4)
        dn_silu = sem("dn_silu")
        hidden_ready = sem("hidden_ready")
        dnT_ps = sem("dnT_ps")
        dnT_hi_ready = sem("dnT_hi_ready")
        dnT_lo_ready = sem("dnT_lo_ready")
        ex_silu = sem("ex_silu")
        exT_ps = sem("exT_ps")
        exT_hi_ready = sem("exT_hi_ready")
        exT_lo_ready = sem("exT_lo_ready")
        tok_hi_ready = sem("tok_hi_ready")
        tok_lo_ready = sem("tok_lo_ready")
        router_hi = sem("router_hi")
        router_lo = sem("router_lo")
        logits_ps = sem("logits_ps")
        gap_ready = sem("gap_ready")
        gap_exp = sem("gap_exp")
        chosen_ready = sem("chosen_ready")
        places_ps = sem("places_ps")
        totals_ps = sem("totals_ps")
        routed = sem("routed")
        put_in_ready = sem("put_in_ready")
        put_back_ps = sem("put_back_ps")
        put_back_ready = sem("put_back_ready")
        slot_w_ready = sem("slot_w_ready")
        gathered_ps = sem("gathered_ps")
        ex_hi_ready = sem("ex_hi_ready")
        ex_lo_ready = sem("ex_lo_ready")
        ey_hi_ready = sem("ey_hi_ready")
        ey_lo_ready = sem("ey_lo_ready")
        back_ps = sem("back_ps")
        slots_moved = sem("slots_moved")
        out_ready = sem("out_ready")
        out_stored = sem("out_stored")

        MIX0 = (0, MIX_UNITS + FFN_UNITS)
        DENSE0 = MIX_UNITS
        MOE0 = 2 * MIX_UNITS + FFN_UNITS
        CROWD0 = MOE0 + NEXP * FFN_UNITS

        def wait_split(eng, j, r):
            eng.wait_ge(lo_ready, r * RAW + (j + 1))

        def turn_of(j):
            return RAW if j < MOE0 else DEEP

        def source(j):
            turns, k = divmod(j - MOE0, DEEP)
            if j < MOE0:
                return raw[:, j % RAW, :], landed[j % RAW], j // RAW + 1
            if k < RAW:
                return deep[:, k, :], deep_landed[k], turns + 1
            return raw[:, j % RAW, :], landed[j % RAW], (MOE0 + k - DEEP) // RAW + 2 + turns

        def split_hi(act, j, r=0):
            unit, arrived, count = source(j)
            act.wait_ge(arrived, r * 16 + count * 16)
            if j >= SPLIT:
                act.wait_ge(unit_used, r * turn_of(j) + (j - SPLIT + 1))
            nc.scalar.activation(w_hi[:, j % SPLIT, :], unit, ACT.Copy).then_inc(hi_ready, 1)

        def split_lo(dve, j, r=0):
            dve.wait_ge(hi_ready, r * turn_of(j) + (j + 1))
            if j >= SPLIT:
                dve.wait_ge(unit_used, r * turn_of(j) + (j - SPLIT + 1))
            nc.vector.tensor_tensor(w_lo[:, j % SPLIT, :], source(j)[0],
                                    w_hi[:, j % SPLIT, :].bitcast(F32), ALU.subtract).then_inc(lo_ready, 1)

        block = ctx.enter_context(nc.Block())

        @block.sync
        def _(sp):
            for t in range(2):
                sp.dma_start(res[:, t, :], x[0, t * P:(t + 1) * P, :]).then_inc(x_in[t], 16)
            sp.dma_start(cst[:], consts).then_inc(consts_in, 16)

            def load(j, src, r=0):
                unit, arrived, _ = source(j)
                if j >= RAW:
                    sp.wait_ge(lo_ready, r * turn_of(j) + (j - turn_of(j) + 1))
                sp.dma_start(unit.rearrange("p (k n) -> p k n", n=src.shape[-1]), src).then_inc(arrived, 16)

            def wide_unit(w, k_half, col):
                return w[bass.ds(k_half, 512), bass.ds(col, 512)].rearrange("(k p) n -> p k n", p=P)

            def deep_unit(w, row):
                return w[bass.ds(row, 2 * P), :].rearrange("(k p) n -> p k n", p=P)

            def load_mixer(layer):
                n = MIX0[layer]
                for c, chunk in enumerate(CHUNKS):
                    if layer == 0 and c == 1:
                        rows = lambda a, pattern: a.rearrange(pattern, p=P)
                        for dst, src in ((chan_rows[0:8, :], rows(ret_norm_w, "l (c p) -> (l c) p")),
                                         (chan_rows[8:32, :], rows(conv_w, "l j (c p) -> (l j c) p")),
                                         (chan_rows[32:40, :], rows(conv_b, "l (c p) -> (l c) p")),
                                         (probs[:, 0, :], masks),
                                         (router[:], rows(moe_router[0], "(k p) e -> p k e"))):
                            sp.dma_start(dst, src).then_inc(params_in, 16)
                    for half in range(2):
                        load(n, wide_unit(w_in[layer], half * 512, chunk * 512))
                        n += 1
                    if c in (10, 12, 13):
                        w = {10: w_br_attn, 12: w_br_conv, 13: w_br_ret}[c]
                        for h in range(2):
                            load(n, deep_unit(w[layer], h * 2 * P))
                            n += 1
                for h in range(4):
                    load(n, deep_unit(w_out[layer], h * 2 * P))
                    n += 1

            load_mixer(0)
            gate, up, down = dense_w_gate[0], dense_w_up[0], dense_w_down[0]
            for h in range(2):
                load(DENSE0 + h, wide_unit(gate, h * 512, 0))
            with sp.Fori(0, 6) as i:
                for h in range(2):
                    load(DENSE0 + 2 + h, wide_unit(up, h * 512, i * 512), i)
                for h in range(2):
                    load(DENSE0 + 4 + h, wide_unit(gate, h * 512, i * 512 + 512), i)
                for h in range(2):
                    load(DENSE0 + 6 + h, deep_unit(down, i * 512 + h * 2 * P), i)
            for h in range(2):
                load(DENSE0 + 38 + h, wide_unit(up, h * 512, (FCH - 1) * 512))
            for h in range(2):
                load(DENSE0 + 40 + h, deep_unit(down, (FCH - 1) * 512 + h * 2 * P))
            load_mixer(1)

            gate = moe_w_gate[0].rearrange("e k f -> (e k) f")
            up = moe_w_up[0].rearrange("e k f -> (e k) f")
            down = moe_w_down[0].rearrange("e f d -> (e f) d")

            def load_experts(base):
                with sp.Fori(0, NEXP // 2) as pair:
                    r = pair * FCH
                    for odd in range(2):
                        e, n = pair * 2 + odd, base + odd * FFN_UNITS
                        for h in range(2):
                            load(n + h, wide_unit(gate, e * D + h * 512, 0), r)
                        for h in range(2):
                            load(n + 2 + h, wide_unit(up, e * D + h * 512, 0), r)
                        with sp.Fori(0, (FCH - 1) // 2) as i:
                            for s in range(2):
                                m, col = n + RAW * s + 4, i * 1024 + s * 512
                                for h in range(2):
                                    load(m + h, wide_unit(gate, e * D + h * 512, col + 512), r + i)
                                for h in range(2):
                                    load(m + 2 + h, wide_unit(up, e * D + h * 512, col + 512), r + i)
                                for h in range(2):
                                    load(m + 4 + h, deep_unit(down, e * FF + (col + h * 2 * P)), r + i)
                        for h in range(2):
                            load(n + 40 + h, deep_unit(down, e * FF + ((FCH - 1) * 512 + h * 2 * P)), r)

            sp.wait_ge(unit_used, MIX0[1] + BR_RET + 2)
            load_experts(MOE0)
            sp.wait_ge(routed, 1)
            flag = sp.value_load(crowded[0:1, 0:1], min_val=0, max_val=1)
            with sp.If(flag > 0):
                load_experts(CROWD0)
            for t in range(2):
                sp.wait_ge(out_ready, t + 1)
                sp.dma_start(out[0, t * P:(t + 1) * P, :], wide[:, t, :]).then_inc(out_stored, 16)
            sp.wait_ge(out_stored, 32)

        @block.gpsimd
        def _(pool):
            nc.gpsimd.memset(spare[:, 8:9], 1.0).then_inc(spare_set, 1)
            nc.gpsimd.memset(zeros[:], 0.0).then_inc(zeros_set, 1)
            nc.gpsimd.memset(uT[:, :, 0:2], 0.0).then_inc(pads_set, 1)

        @block.tensor
        def _(pe):
            mm = nc.tensor.matmul
            chain = Chain(tensor_chain, pe)

            def three(o, a_hi, a_lo, b_hi, b_lo, start, stop):
                mm(o, a_hi, b_hi, start=start, stop=False, skip_group_check=True)
                mm(o, a_hi, b_lo, start=False, stop=False, skip_group_check=True)
                return mm(o, a_lo, b_hi, start=False, stop=stop, skip_group_check=True)

            def wide_unit(j, x_hi, x_lo, kt0, banks, r=0):
                wait_split(pe, j, r)
                s = j % SPLIT
                for k in range(4):
                    cols = slice(k * 512, k * 512 + 512)
                    for t, bank in enumerate(banks):
                        tok = slice(t * P, t * P + P)
                        last = three(ps[:, bank, :], x_hi[:, kt0 + k, tok], x_lo[:, kt0 + k, tok],
                                     w_hi[:, s, cols], w_lo[:, s, cols],
                                     start=(kt0 == 0 and k == 0), stop=(kt0 == 4 and k == 3))
                last.then_inc(unit_used, 1)

            def deep_unit(j, x_hi, x_lo, kt0, banks, start, stop, r=0):
                wait_split(pe, j, r)
                s = j % SPLIT
                for k in range(2):
                    for t, pair in enumerate(banks):
                        tok = slice(t * P, t * P + P)
                        for half, bank in enumerate(pair):
                            cols = slice(k * 1024 + half * 512, k * 1024 + half * 512 + 512)
                            last = three(ps[:, bank, :], x_hi[:, kt0 + k, tok],
                                         x_lo[:, kt0 + k, tok], w_hi[:, s, cols], w_lo[:, s, cols],
                                         start=(start and k == 0), stop=(stop and k == 1))
                last.then_inc(unit_used, 1)

            def channel_unit(j, kt0, bank0):
                wait_split(pe, j, 0)
                s = j % SPLIT
                for k in range(4):
                    for cb in range(4):
                        cols = slice(k * 512 + cb * P, k * 512 + cb * P + P)
                        o = ps[:, bank0 + cb // 2, (cb % 2) * SEQ:(cb % 2) * SEQ + SEQ]
                        last = three(o, w_hi[:, s, cols], w_lo[:, s, cols], xT_hi[:, kt0 + k, :],
                                     xT_lo[:, kt0 + k, :], start=(kt0 == 0 and k == 0 and cb % 2 == 0),
                                     stop=(kt0 == 4 and k == 3))
                last.then_inc(unit_used, 1)

            SUMS, EX_SUMS = ((4, 5), (6, 7)), ((2, 3),)
            BRANCH = ((4, 6), (5, 7))

            def transpose(o, i):
                return nc.tensor.transpose(o, i, ident[0:i.shape[0], 0:i.shape[0]])

            def keep_warm(n):
                for _ in range(n):
                    mm(ps[:, 7, :], zeros[:, 0:P], zeros[:], start=True, stop=True)

            def open_sums(banks):
                for b in banks:
                    mm(ps[:, b, :], zeros[:, 0:P], zeros[:], start=True, stop=False, skip_group_check=True)

            def deep_pair(j, x_hi, x_lo, kt0, banks, r=0):
                wait_split(pe, j + 1, r)
                for t, pair in enumerate(banks):
                    tok = slice(t * P, t * P + P)
                    for u in range(2):
                        s = (j + u) % SPLIT
                        for k in range(2):
                            for half, bank in enumerate(pair):
                                cols = slice(k * 1024 + half * 512, k * 1024 + half * 512 + 512)
                                last = three(ps[:, bank, :], x_hi[:, kt0 + 2 * u + k, tok],
                                             x_lo[:, kt0 + 2 * u + k, tok], w_hi[:, s, cols], w_lo[:, s, cols],
                                             start=False, stop=(u == 1 and k == 1))
                        if t == 1:
                            last.then_inc(unit_used, 1)
                    if t == 0:
                        last.then_inc(tile0_summed, 1)

            def turn_normed(q, t):
                pe.wait_ge(normed, 2 * q + t + 1)
                for k in range(KT):
                    last = transpose(ps[:, 2 + 2 * t + k // 4, (k % 4) * P:(k % 4) * P + P],
                                     wide[:, t, k * P:k * P + P])
                last.then_inc(normed_ps, 1)

            def first_pair(q, j, banks):
                def half_products(u, t):
                    s, tok = (j + u) % SPLIT, slice(t * P, t * P + P)
                    for k in range(4):
                        cols = slice(k * 512, k * 512 + 512)
                        last = three(ps[:, banks[t], :], xT_hi[:, 4 * u + k, tok], xT_lo[:, 4 * u + k, tok],
                                     w_hi[:, s, cols], w_lo[:, s, cols], start=(u == 0 and k == 0),
                                     stop=(u == 1 and k == 3))
                    return last

                turn_normed(q, 0)
                if q:
                    pe.wait_ge(res_added, 2 * q)
                else:
                    turn_normed(q, 1)
                wait_split(pe, j, 0)
                pe.wait_ge(xT_lo_ready, 4 * q + 2)
                half_products(0, 0)
                if q:
                    turn_normed(q, 1)
                wait_split(pe, j + 1, 0)
                half_products(1, 0)
                pe.wait_ge(xT_lo_ready, 4 * q + 4)
                half_products(0, 1).then_inc(unit_used, 1)
                half_products(1, 1).then_inc(unit_used, 1)

            def mixer(L):
                base = MIX0[L]

                def attention_scores(g):
                    for odd in range(2):
                        for j in (odd, odd + 2):
                            hp, r = (4 * g + j) // 2, HEAD * odd
                            o = ps[:, 5 + j // 2, odd * SEQ:odd * SEQ + SEQ]
                            mm(o, msk[:, 0:P], msk[:, P:3 * P], start=True, stop=False)
                            mm(o, qT[r:r + HEAD, hp, P:SEQ], kT[r:r + HEAD, hp, :], start=False, stop=True)
                            o = ps[:, 7, j * P:j * P + P]
                            mm(o, msk[:, 0:P], msk[:, 2 * P:3 * P], start=True, stop=False)
                            last = mm(o, qT[r:r + HEAD, hp, 0:P], kT[r:r + HEAD, hp, 0:P], start=False, stop=True)
                        if odd == 0:
                            chain(last)
                    last.then_inc(scores_ps.sem, 1)

                def transpose_probs(g):
                    probs_ready.wait(pe, g + 1, L)
                    for j in range(4):
                        b, c = 5 + j // 2, (j % 2) * SEQ
                        transpose(ps[:, b, c:c + P], probs[:, j, 2 * P:3 * P])
                        transpose(ps[:, b, c + P:c + 2 * P], probs[:, j, 0:P])
                        last = transpose(ps[:, 7, j * P:j * P + P], probs[:, j, P:2 * P])
                    last.then_inc(probsT_ps.sem, 1)

                def attention_values(g):
                    probsT_ready0.wait(pe, g + 1, L)
                    probsT_ready1.wait(pe, g + 1, L)
                    if g == 1:
                        attn_hi.wait(pe, 1, L)
                        attn_lo.wait(pe, 1, L)
                    for j in range(4):
                        h, r, c = 4 * g + j, HEAD * (j % 2), (j // 2) * SEQ
                        mm(ps[r:r + HEAD, 4, c:c + SEQ], v_attn[:, 0, h * HEAD:h * HEAD + HEAD],
                           probsT[:, j, 0:SEQ], start=True, stop=True)
                        last = mm(ps[r:r + HEAD, 4, c + P:c + SEQ], v_attn[:, 1, h * HEAD:h * HEAD + HEAD],
                                  probsT[:, j, SEQ:SEQ + P], start=False, stop=True, skip_group_check=True)
                    last.then_inc(attn_ps.sem, 1)

                def chunk(c, n):
                    for half in range(2):
                        wide_unit(n + half, xT_hi, xT_lo, 4 * half, [2 * (c % 2), 2 * (c % 2) + 1])

                n = base
                first_pair(2 * L, n, [6, 7])
                chunk(1, n + 2)
                if L == 0:
                    pe.wait_ge(params_in, 16 * 5)
                    transpose(ps[:, 4, 0:40], chan_rows[:, :]).then_inc(chan_ps, 1)
                chunk(2, n + 4)
                rope_done.wait(pe, 2, L)
                for c in range(4):
                    for t in range(2):
                        col = (c % 2) * SEQ + t * P
                        transpose(ps[:, 4 + c // 2, col:col + P], wide[:, t, c * P:c * P + P])
                        last = transpose(ps[:, 6 + c // 2, col:col + P], wide[:, t, 512 + c * P:512 + c * P + P])
                last.then_inc(qkT_ps.sem, 1)
                chunk(3, n + 6)
                qT_ready.wait(pe, 1, L)
                kT_ready.wait(pe, 1, L)
                if L == 0:
                    pe.wait_ge(masks_cast, 1)
                attention_scores(0)
                v_copied.wait(pe, 1, L)
                chunk(4, n + 8)
                rope_done.wait(pe, 3, L)
                channel_unit(n + 10, 0, 2)
                transpose_probs(0)
                channel_unit(n + 11, 4, 2)
                attention_values(0)
                attention_scores(1)
                v_copied.wait(pe, 2, L)
                for half in range(2):
                    channel_unit(n + 12 + half, 4 * half, 0)
                conv_c_copied.wait(pe, 1, L)
                channel_unit(n + 14, 0, 2)
                transpose_probs(1)
                channel_unit(n + 15, 4, 2)
                attention_values(1)
                for c in range(2):
                    for t in range(2):
                        col = c * SEQ + t * P
                        transpose(ps[:, 5, col:col + P], ret_qk[:, t, c * P:c * P + P])
                        last = transpose(ps[:, 6, col:col + P], ret_qk[:, t, SEQ + c * P:SEQ + c * P + P])
                last.then_inc(ret_qkT_ps.sem, 1)
                conv_u_ready.wait(pe, 1, L)
                chunk(8, n + 16)
                rqT_ready.wait(pe, 1, L)
                rkT_ready.wait(pe, 1, L)
                for odd in range(2):
                    for h in (odd, odd + 2):
                        hp, r = h // 2, HEAD * odd
                        for t in range(2):
                            tok = slice(t * P, t * P + P)
                            mm(ps[:, 5 + t, h * P:h * P + P], rkT[r:r + HEAD, hp, tok], rqT[r:r + HEAD, hp, tok],
                               start=True, stop=True)
                        last = mm(ps[r:r + HEAD, 7, hp * P:hp * P + P], kzeta[:, h * HEAD:h * HEAD + HEAD],
                                  v_ret[:, 0, h * P:h * P + P], start=True, stop=True)
                    if odd == 0:
                        chain(last)
                last.then_inc(ret_scores_ps.sem, 1)
                conv_y_ready.wait(pe, 1, L)
                chunk(9, n + 18)
                decayed_ready.wait(pe, 1, L)
                for odd in range(2):
                    for h in (odd, odd + 2):
                        hp, r, cols = h // 2, HEAD * odd, slice(h * P, h * P + P)
                        for t in range(2):
                            mm(ps[:, 5 + t, cols], decayed[:, t * 512 + h * P:t * 512 + h * P + P],
                               v_ret[:, t, cols], start=True, stop=(t == 0))
                        last = mm(ps[:, 6, cols], rqxT[r:r + HEAD, hp, :], state[r:r + HEAD, hp * P:hp * P + P],
                                  start=False, stop=True)
                    if odd == 0:
                        chain(last)
                last.then_inc(ret_o_ps.sem, 1)
                ret_gate_ready.wait(pe, 1, L)
                chunk(10, n + 20)
                ret_y_ready.wait(pe, 1, L)
                attn_hi.wait(pe, 2, L)
                attn_lo.wait(pe, 2, L)
                for h in range(2):
                    deep_unit(base + BR_ATTN + h, yA_hi, yA_lo, 2 * h, BRANCH, h == 0, h == 1)
                gate_ready.wait(pe, 2, L)
                for c in range(BT):
                    for t in range(2):
                        col = (c % 2) * SEQ + t * P
                        last = transpose(ps[:, c // 2, col:col + P], ret_o[:, t, c * P:c * P + P])
                last.then_inc(ret_yT_ps.sem, 1)
                chunk(11, n + 24)
                ret_hi.wait(pe, 1, L)
                ret_lo.wait(pe, 1, L)
                chunk(12, n + 26)
                merged.wait(pe, 2, L)
                conv_hi.wait(pe, 1, L)
                conv_lo.wait(pe, 1, L)
                for h in range(2):
                    deep_unit(base + BR_CONV + h, yC_hi, yC_lo, 2 * h, BRANCH, h == 0, h == 1)
                gate_ready.wait(pe, 3, L)
                chunk(13, n + 30)
                merged.wait(pe, 4, L)
                for h in range(2):
                    deep_unit(base + BR_RET + h, yA_hi, yA_lo, 2 * h, BRANCH, h == 0, h == 1)
                gate_ready.wait(pe, 4, L)

                def turn_merged(half, bank0):
                    merged.wait(pe, 5 + half, L)
                    gate_ready.wait(pe, 5 + half, L)
                    for t in range(2):
                        for k in range(4):
                            last = transpose(ps[:, bank0 + t, k * P:k * P + P],
                                             wide[:, t, (4 * half + k) * P:(4 * half + k + 1) * P])
                        last.then_inc(mergedT_ps.sem, 1)

                wide_unit(n + 34, xT_hi, xT_lo, 0, [0, 1])
                turn_merged(0, 2)
                wide_unit(n + 35, xT_hi, xT_lo, 4, [0, 1])
                mT_hi.wait(pe, 2, L)
                mT_lo.wait(pe, 2, L)
                sums = ((2, 3), (4, 5))
                deep_unit(base + OUT_PROJ, xT_hi, xT_lo, 0, sums, True, False)
                turn_merged(1, 0)
                deep_unit(base + OUT_PROJ + 1, xT_hi, xT_lo, 2, sums, False, False)
                mT_hi.wait(pe, 4, L)
                mT_lo.wait(pe, 4, L)
                deep_pair(base + OUT_PROJ + 2, xT_hi, xT_lo, 4, sums)

            def dense():
                first_pair(1, DENSE0, [0, 1])
                open_sums(range(4, 8))

                def turn(i):
                    pe.wait_ge(hidden_ready, i)
                    for k in range(4):
                        for t in range(2):
                            last = transpose(ps[:, 2 + t, k * P:k * P + P], dn_act[:, t, k * P:k * P + P])
                    last.then_inc(dnT_ps, 1)

                with pe.Fori(0, 6) as i:
                    for h in range(2):
                        wide_unit(DENSE0 + 2 + h, xT_hi, xT_lo, 4 * h, [2, 3], i)
                    pe.wait_ge(dn_silu, i + 1)
                    wide_unit(DENSE0 + 4, xT_hi, xT_lo, 0, [0, 1], i)
                    turn(i + 1)
                    wide_unit(DENSE0 + 5, xT_hi, xT_lo, 4, [0, 1], i)
                    pe.wait_ge(dnT_hi_ready, i + 1)
                    pe.wait_ge(dnT_lo_ready, i + 1)
                    for h in range(2):
                        deep_unit(DENSE0 + 6 + h, dnT_hi, dnT_lo, 2 * h, SUMS, False, False, i)
                for h in range(2):
                    wide_unit(DENSE0 + 38 + h, xT_hi, xT_lo, 4 * h, [2, 3])
                turn(FCH)
                pe.wait_ge(dnT_hi_ready, FCH)
                pe.wait_ge(dnT_lo_ready, FCH)
                deep_pair(DENSE0 + 40, dnT_hi, dnT_lo, 0, SUMS)

            def route():
                pe.wait_ge(router_lo, 1)
                keep_warm(16)
                for t in range(2):
                    turn_normed(3, t)
                keep_warm(6)
                for t in range(2):
                    pe.wait_ge(xT_lo_ready, 14 + 2 * t)
                    tok = slice(t * P, t * P + P)
                    for k in range(KT):
                        mm(ps[:, 0, 2 * t * NEXP:2 * (t + 1) * NEXP], xT_hi[:, k, tok],
                           rt[:, k, :], start=(k == 0), stop=False, skip_group_check=True)
                        last = mm(ps[:, 0, 2 * t * NEXP:(2 * t + 1) * NEXP], xT_lo[:, k, tok],
                                  rt[:, k, 0:NEXP], start=False, stop=(k == KT - 1), skip_group_check=True)
                last.then_inc(logits_ps, 1)
                keep_warm(14)
                pe.wait_ge(chosen_ready, 1)
                mm(ps[:, 7, 0:8], const("before"), chosen[:, 0, :], start=True, stop=True)
                mm(ps[:, 7, 8:16], const("ones"), chosen[:, 0, :], start=True, stop=False)
                mm(ps[:, 7, 8:16], const("before"), chosen[:, 1, :], start=False, stop=True).then_inc(places_ps, 1)
                mm(ps[:, 4, 0:8], const("ones"), chosen[:, 0, :], start=True, stop=False)
                mm(ps[:, 4, 0:8], const("ones"), chosen[:, 1, :], start=False, stop=True).then_inc(totals_ps, 1)

            def gather(n):
                pe.wait_ge(put_in_ready, n)
                for k in range(KT):
                    o = ps[:, 5 + k // 4, (k % 4) * P:(k % 4) * P + P]
                    for t in range(2):
                        mm(o, tok_hi[:, t, k * P:k * P + P], put_in[:, t, :], start=(t == 0), stop=False)
                        last = mm(o, tok_lo[:, t, k * P:k * P + P], put_in[:, t, :], start=False, stop=(t == 1))
                    if k % 4 == 3:
                        last.then_inc(gathered_ps, 1)

            def experts(base, done):
                gather(done + 1)
                for h in range(2):
                    pe.wait_ge(ex_lo_ready, 2 * done + h + 1)
                    wide_unit(base + h, ex_hi, ex_lo, 4 * h, [0])

                def expert(e, last_one):
                    r = e * FCH
                    f = r + done * FCH
                    for h in range(2):
                        wide_unit(base + 2 + h, ex_hi, ex_lo, 4 * h, [1], r)
                    pe.wait_ge(res_added, e * 2 + (2 * done + 6))
                    for t in range(2):
                        transpose(ps[:, 7, t * P:t * P + P], put_in[:, t, :].bitcast(F32))
                    for t in range(2):
                        last = mm(ps[:, 7, SEQ:SEQ + 1], put_in[:, t, :].bitcast(F32),
                                  share[:, t, bass.ds(e, 1)], start=(t == 0), stop=(t == 1))
                    last.then_inc(put_back_ps, 1)
                    open_sums([2, 3])

                    def turn(n):
                        pe.wait_ge(hidden_ready, n + FCH)
                        for k in range(4):
                            last = transpose(ps[:, 4, k * P:k * P + P], ex_act[:, k * P:k * P + P])
                        last.then_inc(exT_ps, 1)

                    with pe.Fori(0, 6) as i:
                        v = r + i
                        pe.wait_ge(ex_silu, f + i + 1)
                        for h in range(2):
                            wide_unit(base + 4 + h, ex_hi, ex_lo, 4 * h, [0], v)
                        turn(f + i + 1)
                        for h in range(2):
                            wide_unit(base + 6 + h, ex_hi, ex_lo, 4 * h, [1], v)
                        pe.wait_ge(exT_lo_ready, f + i + 1)
                        for h in range(2):
                            deep_unit(base + 8 + h, exT_hi, exT_lo, 2 * h, EX_SUMS, False, False, v)
                    turn(f + FCH)
                    if not last_one:
                        gather(e + (done + 2))
                    pe.wait_ge(exT_lo_ready, f + FCH)
                    for h in range(2):
                        deep_unit(base + 40 + h, exT_hi, exT_lo, 2 * h, EX_SUMS, False, h == 1, r)
                    if not last_one:
                        pe.wait_ge(ex_lo_ready, e * 2 + (2 * done + 4))
                        for h in range(2):
                            wide_unit(base + FFN_UNITS + h, ex_hi, ex_lo, 4 * h, [0], r)
                    pe.wait_ge(ey_lo_ready, e + (done + 1))
                    pe.wait_ge(put_back_ready, e + (done + 1))
                    for t in range(2):
                        for half in range(2):
                            o, cols = ps[:, 4 + 2 * t + half, :], slice(half * 512, half * 512 + 512)
                            mm(o, put_back[:, t * P:t * P + P], ey_hi[:, cols], start=True, stop=False)
                            last = mm(o, put_back[:, t * P:t * P + P], ey_lo[:, cols], start=False, stop=True)
                        last.then_inc(back_ps, 1)

                with pe.Fori(0, NEXP - 1) as e:
                    expert(e, False)
                expert(NEXP - 1, True)

            pe.wait_ge(consts_in, 16)
            pe.wait_ge(zeros_set, 1)
            mixer(0)
            dense()
            mixer(1)
            route()
            pe.wait_ge(tok_lo_ready, 2)
            experts(MOE0, 0)
            pe.wait_ge(routed, 1)
            flag = pe.value_load(crowded[0:1, 0:1], min_val=0, max_val=1)
            with pe.If(flag > 0):
                experts(CROWD0, NEXP)

        @block.scalar
        def _(act):
            weights = (mix_norm_w[0:1, :], ffn_norm_w[0:1, :], mix_norm_w[1:2, :], ffn_norm_w[1:2, :],
                       final_norm_w.rearrange("(a d) -> a d", a=1))

            def load_norm_w(q):
                if q:
                    act.wait_ge(normed, 2 * q)
                act.dma_start(norm_w[:], weights[q].partition_broadcast(P)).then_inc(norm_w_in, 16)

            load_norm_w(0)
            chain = Chain(scalar_chain, act)
            run = nc.scalar.activation

            def root(t, squares_to=wide):
                chain(run(squares_to[:, t, :], res[:, t, :], ACT.Square, accum_out=stat[:, t:t + 1]))
                run(stat[:, 2 + t:3 + t], stat[:, t:t + 1], ACT.Sqrt, scale=1.0 / D, bias=EPS)\
                    .then_inc(root_ready, 1)

            def ready_root(n):
                run(spare[:, n:n + 1], spare[:, 8:9], ACT.Sqrt)

            def turn_normed(q, t):
                act.wait_ge(normed_ps, 2 * q + t + 1)
                for half in range(2):
                    run(xT_hi[:, 4 * half:4 * half + 4, t * P:t * P + P],
                        ps[:, 2 + 2 * t + half, :].rearrange("p (k t) -> p k t", k=4), ACT.Copy)\
                        .then_inc(xT_hi_ready, 1)

            def cross(q, n):
                split_hi(act, n)
                ready_root(q)
                act.wait_ge(res_added, 2 * q - 1)
                root(0)
                split_hi(act, n + 1)
                if q < 3:
                    turn_normed(q, 0)
                act.wait_ge(res_added, 2 * q)
                root(1)
                if q == 3:
                    turn_normed(q, 0)
                turn_normed(q, 1)
                if q < 3:
                    split_hi(act, n + 2)

            def mixer(L):
                base = MIX0[L]

                def exps(g):
                    max_ready.wait(act, g + 1, L)
                    for j in range(4):
                        run(probs[:, j, 0:SEQ], ps[:, 5 + j // 2, (j % 2) * SEQ:(j % 2) * SEQ + SEQ], ACT.Exp,
                            scale=HEAD ** -0.5, bias=stat[:, 16 + j:17 + j], accum_out=stat[:, 24 + j:25 + j])
                    for j in range(4):
                        last = run(probs[:, j, SEQ:SEQ + P], ps[:, 7, j * P:j * P + P], ACT.Exp,
                                   scale=HEAD ** -0.5, bias=stat[:, 20 + j:21 + j],
                                   accum_out=stat[:, 28 + j:29 + j])
                    last.then_inc(exp_done.sem, 1)

                def turn_probs(g):
                    probsT_ps.wait(act, g + 1, L)
                    run(probsT[:, :, 0:SEQ], ps[:, 5:7, :].rearrange("p b (j q) -> p (b j) q", j=2), ACT.Copy)\
                        .then_inc(probsT_ready0.sem, 1)

                def turn_attention(g):
                    attn_ps.wait(act, g + 1, L)
                    run(yA_hi[:, 2 * g:2 * g + 2, :], ps[:, 4, :].rearrange("p (c t) -> p c t", c=2), ACT.Copy)\
                        .then_inc(attn_hi.sem, 1)

                def sigmoid(c, half):
                    run(gates[:, :, half * 512:half * 512 + 512], ps[:, 2 * (c % 2):2 * (c % 2) + 2, :],
                        ACT.Sigmoid).then_inc(gate_ready.sem, 1)

                def turn_merged(half, bank0):
                    for t in range(2):
                        mergedT_ps.wait(act, 2 * half + t + 1, L)
                        run(xT_hi[:, 4 * half:4 * half + 4, t * P:t * P + P],
                            ps[:, bank0 + t, :].rearrange("p (k t) -> p k t", k=4), ACT.Copy).then_inc(mT_hi.sem, 1)

                for m in range(3, MIX_UNITS):
                    act.wait_ge(unit_used, base + m - 2)
                    if m == 6:
                        load_norm_w(2 * L + 1)
                    if m == 4 and L == 0:
                        act.wait_ge(params_in, 16 * 5)
                        run(msk[:], probs[:, 0, :], ACT.Copy).then_inc(masks_cast, 1)
                    if m == 8:
                        run(v_attn[:], ps[:, 0:2, :], ACT.Copy).then_inc(v_copied.sem, 1)
                        qkT_ps.wait(act, 1, L)
                        run(qT[:].rearrange("p c t -> p (c t)"), ps[:, 4:6, :].rearrange("p b n -> p (b n)"),
                            ACT.Copy).then_inc(qT_ready.sem, 1)
                    if m == 10:
                        exps(0)
                    if m == 12:
                        run(v_ret[:], ps[:, 0:2, :], ACT.Copy).then_inc(v_copied.sem, 1)
                    if m == 13:
                        turn_probs(0)
                    if m == 14:
                        run(conv_c.rearrange("p c t -> p (c t)"), ps[:, 2:4, :].rearrange("p b n -> p (b n)"),
                            ACT.Copy).then_inc(conv_c_copied.sem, 1)
                        turn_attention(0)
                        exps(1)
                    if m == 17:
                        turn_probs(1)
                    if m == 18:
                        turn_attention(1)
                        ret_qkT_ps.wait(act, 1, L)
                        run(rqT[:].rearrange("p c t -> p (c t)"), ps[:, 5, :], ACT.Copy).then_inc(rqT_ready.sem, 1)
                        conv_y_ready.wait(act, 1, L)
                        run(yC_hi[:], conv, ACT.Copy).then_inc(conv_hi.sem, 1)
                    if m == 20:
                        run(ret_gate[:], ps[:, 0:2, :], ACT.Silu).then_inc(ret_gate_ready.sem, 1)
                    if m == 22:
                        ret_o_ps.wait(act, 1, L)
                        run(squares, ps[:, 5:7, :].rearrange("p b n -> p (b n)"), ACT.Square)\
                            .then_inc(ret_sq_done.sem, 1)
                        sigmoid(9, 0)
                    if m == 23:
                        ret_ss_ready.wait(act, 1, L)
                        run(stat[:, 40:48], stat[:, 32:40], ACT.Sqrt, scale=1.0 / P, bias=EPS)\
                            .then_inc(ret_root.sem, 1)
                    if m == 24:
                        sigmoid(10, 1)
                    if m == 26:
                        ret_yT_ps.wait(act, 1, L)
                        for c in range(BT):
                            last = run(yA_hi[:, c, :], ps[:, c // 2, (c % 2) * SEQ:(c % 2) * SEQ + SEQ], ACT.Copy,
                                       scale=chan[:, L * BT + c:L * BT + c + 1])
                        last.then_inc(ret_hi.sem, 1)
                    if m == 28:
                        merged.wait(act, 1, L)
                        sigmoid(11, 0)
                    if m == 30:
                        merged.wait(act, 2, L)
                        sigmoid(12, 1)
                    if m == 34:
                        merged.wait(act, 3, L)
                        sigmoid(13, 0)
                    if m == 37:
                        turn_merged(0, 2)
                    if m == 38:
                        merged.wait(act, 4, L)
                        sigmoid(14, 1)
                    if m == 39:
                        turn_merged(1, 0)
                    split_hi(act, base + m)

            def dense():
                def silu(n):
                    run(dn_sil[:], ps[:, 0:2, :], ACT.Silu).then_inc(dn_silu, 1)

                def turn(i):
                    act.wait_ge(dnT_ps, i)
                    run(dnT_hi[:].rearrange("p k (t n) -> p t k n", t=2),
                        ps[:, 2:4, :].rearrange("p t (k n) -> p t k n", k=4), ACT.Copy).then_inc(dnT_hi_ready, 1)

                split_hi(act, DENSE0 + 3)
                act.wait_ge(unit_used, DENSE0 + 2)
                silu(0)
                split_hi(act, DENSE0 + 4)
                load_norm_w(2)
                with act.Fori(0, 6) as i:
                    split_hi(act, DENSE0 + 5, i)
                    split_hi(act, DENSE0 + 6, i)
                    turn(i + 1)
                    split_hi(act, DENSE0 + 7, i)
                    act.wait_ge(unit_used, i * RAW + (DENSE0 + 6))
                    silu(i + 1)
                    for j in (8, 9, 10):
                        split_hi(act, DENSE0 + j, i)
                split_hi(act, DENSE0 + 41)
                turn(FCH)

            def experts(base, done):
                def take_gathered(n):
                    for half in range(2):
                        act.wait_ge(gathered_ps, n + half)
                        run(ex_hi[:, 4 * half:4 * half + 4, :],
                            ps[:, 5 + half, :].rearrange("p (k t) -> p k t", k=4), ACT.Copy).then_inc(ex_hi_ready, 1)

                def expert(pair, odd, last_one=False):
                    e, r, n = pair * 2 + odd, pair * FCH, base + odd * FFN_UNITS
                    f = pair * (2 * FCH) + (odd + done) * FCH

                    def silu(c, unit):
                        act.wait_ge(unit_used, unit)
                        act.wait_ge(hidden_ready, c + FCH)
                        run(ex_sil[:], ps[:, 0, :], ACT.Silu).then_inc(ex_silu, 1)

                    def turn(c):
                        act.wait_ge(exT_ps, c)
                        run(exT_hi[:], ps[:, 4, :].rearrange("p (k t) -> p k t", k=4), ACT.Copy)\
                            .then_inc(exT_hi_ready, 1)

                    silu(f, r * DEEP + (n + 2))
                    for j in (4, 5):
                        split_hi(act, n + j, r)
                    act.wait_ge(put_back_ps, e + (done + 1))
                    run(put_back[:], ps[:, 7, 0:SEQ], ACT.Copy).then_inc(put_back_ready, 1)

                    def step(i, s, splits=(8, 9, 10, 11)):
                        w, m, c = r + i, n + RAW * s, f + i * 2 + s
                        split_hi(act, m + 6, w)
                        split_hi(act, m + 7, w)
                        turn(c + 1)
                        silu(c + 1, w * DEEP + (m + 6))
                        for j in splits:
                            split_hi(act, m + j, w)

                    double_steps = (FCH - 1) // 2
                    with act.Fori(0, double_steps - last_one) as i:
                        step(i, 0)
                        step(i, 1)
                    if last_one:
                        step(double_steps - 1, 0)
                        step(double_steps - 1, 1, (8, 9, 10))
                    turn(f + FCH)
                    if last_one:
                        split_hi(act, n + 41, r)
                    if not last_one:
                        split_hi(act, n + 42, r)
                        take_gathered(e * 2 + (2 * done + 3))
                        split_hi(act, n + 43, r)
                    else:
                        ready_root(4 + done // NEXP)
                    act.wait_ge(unit_used, r * DEEP + (n + FFN_UNITS))
                    act.wait_ge(slot_w_ready, e + (done + 1))
                    run(ey_hi[:], ps[:, 2:4, :].rearrange("p b n -> p (b n)"), ACT.Copy, scale=slot_w[:, 0:1])\
                        .then_inc(ey_hi_ready, 1)
                    if not last_one:
                        split_hi(act, n + 44, r)
                        split_hi(act, n + 45, r)

                if done:
                    for j in range(3):
                        split_hi(act, base + j)
                take_gathered(2 * done + 1)
                split_hi(act, base + 3)
                with act.Fori(0, NEXP // 2 - 1) as pair:
                    expert(pair, 0)
                    expert(pair, 1)
                expert(NEXP // 2 - 1, 0)
                expert(NEXP // 2 - 1, 1, last_one=True)

            act.wait_ge(spare_set, 1)
            ready_root(0)
            for t in range(2):
                act.wait_ge(x_in[t], 16)
                root(t)
            turn_normed(0, 0)
            split_hi(act, 0)
            turn_normed(0, 1)
            split_hi(act, 1)
            split_hi(act, 2)
            mixer(0)
            cross(1, DENSE0)
            dense()
            cross(2, MIX0[1])
            mixer(1)
            run(rt[:, :, 0:NEXP], router[:], ACT.Copy).then_inc(router_hi, 1)
            cross(3, MOE0)
            for t in range(2):
                act.wait_ge(normed, 7 + t)
                run(tok_hi[:, t, :], wide[:, t, :], ACT.Copy).then_inc(tok_hi_ready, 1)
            act.wait_ge(gap_ready, 1)
            run(prob[:, 2:4], prob[:, 0:2], ACT.Exp).then_inc(gap_exp, 1)
            split_hi(act, MOE0 + 2)
            load_norm_w(4)
            experts(MOE0, 0)
            act.wait_ge(routed, 1)
            flag = act.value_load(crowded[0:1, 0:1], min_val=0, max_val=1)
            counted = chain.n

            def final_roots(additions):
                for t in range(2):
                    act.wait_ge(res_added, 5 + additions + t)
                    root(t, squares_to=tok_hi)

            with act.If(flag > 0):
                experts(CROWD0, NEXP)
                final_roots(4 * NEXP)
            chain.n = counted
            with act.Else():
                final_roots(2 * NEXP)

        @block.vector
        def _(dve):
            chain = Chain(vector_chain, dve)
            v = nc.vector

            def rsqrt(o, root, sum_sq, scale, tmp):
                chain(v.reciprocal(o, root))
                chain(v.tensor_scalar(tmp, sum_sq, -0.5 * scale, -0.5 * EPS, ALU.mult, ALU.add))
                chain(v.tensor_tensor(tmp, tmp, o, ALU.mult))
                chain(v.tensor_tensor(tmp, tmp, o, ALU.mult))
                chain(v.scalar_tensor_tensor(o, tmp, 1.5, o, ALU.add, ALU.mult))

            def normalise_tile(q, t):
                dve.wait_ge(root_ready, 2 * q + t + 1)
                rsqrt(stat[:, 4 + t:5 + t], stat[:, 2 + t:3 + t], stat[:, t:t + 1], 1.0 / D, stat[:, 6 + t:7 + t])
                dve.wait_ge(norm_w_in, 16 * (q + 1))
                v.scalar_tensor_tensor(wide[:, t, :], res[:, t, :], stat[:, 4 + t:5 + t], norm_w[:],
                                       ALU.mult, ALU.mult).then_inc(normed if q < 4 else out_ready, 1)

            def turn_normed(q, t):
                for half in range(2):
                    dve.wait_ge(xT_hi_ready, 4 * q + 2 * t + half + 1)
                    part = (slice(None), slice(4 * half, 4 * half + 4), slice(t * P, t * P + P))
                    v.tensor_tensor(xT_lo[part],
                                    ps[:, 2 + 2 * t + half, :].rearrange("p (k t) -> p k t", k=4),
                                    xT_hi[part].bitcast(F32), ALU.subtract).then_inc(xT_lo_ready, 1)

            def cross(q, n, sums):
                def add_residual(t):
                    two = res[:, t, :].rearrange("p (b n) -> p b n", b=2)
                    v.tensor_tensor(two, two, sums[t], ALU.add).then_inc(res_added, 1)

                split_lo(dve, n)
                dve.wait_ge(tile0_summed, q)
                add_residual(0)
                normalise_tile(q, 0)
                dve.wait_ge(unit_used, n)
                add_residual(1)
                if q < 3:
                    turn_normed(q, 0)
                    split_lo(dve, n + 1)
                    normalise_tile(q, 1)
                    turn_normed(q, 1)
                    split_lo(dve, n + 2)
                else:
                    normalise_tile(q, 1)
                    turn_normed(q, 0)
                    turn_normed(q, 1)

            def mixer(L):
                base = MIX0[L]

                def rope(k, dst, bank):
                    if k or L:
                        rope_done.wait(dve, k, L)
                    for t in range(2):
                        heads = ps[:, bank + t, :].rearrange("p (h d) -> p h d", h=8)
                        cos = const("cos")[:, t * HEAD:t * HEAD + HEAD]
                        sin = const("sin")[:, t * HEAD:t * HEAD + HEAD]
                        o = dst(t).rearrange("p (h d) -> p h d", h=8)
                        tmp = rope_tmp.rearrange("p (h d) -> p h d", h=8)
                        half = HEAD // 2
                        v.tensor_tensor(o, heads, cos.unsqueeze(1).to_broadcast([P, 8, HEAD]), ALU.mult)
                        v.tensor_tensor(tmp[:, :, 0:half], heads[:, :, half:HEAD],
                                        sin[:, 0:half].unsqueeze(1).to_broadcast([P, 8, half]), ALU.mult)
                        chain(v.tensor_tensor(tmp[:, :, half:HEAD], heads[:, :, 0:half],
                                              sin[:, half:HEAD].unsqueeze(1).to_broadcast([P, 8, half]), ALU.mult))
                        last = v.tensor_tensor(dst(t), dst(t), rope_tmp, ALU.add)
                        if t == 0:
                            chain(last)
                    last.then_inc(rope_done.sem, 1)

                def row_max(g):
                    scores_ps.wait(dve, g + 1, L)
                    v.tensor_reduce(stat[:, 8:12], ps[:, 5:7, :].rearrange("p b (j q) -> p (b j) q", j=2),
                                    AX_X, ALU.max)
                    chain(v.tensor_reduce(stat[:, 12:16], ps[:, 7, :].rearrange("p (j q) -> p j q", j=4),
                                          AX_X, ALU.max))
                    v.tensor_scalar(stat[:, 16:24], stat[:, 8:16], -HEAD ** -0.5, None, ALU.mult)\
                        .then_inc(max_ready.sem, 1)

                def normalise(g):
                    exp_done.wait(dve, g + 1, L)
                    chain(v.reciprocal(stat[:, 24:32], stat[:, 24:32]))
                    v.tensor_tensor(probs[:, :, 0:SEQ], probs[:, :, 0:SEQ],
                                    stat[:, 24:28].unsqueeze(2).to_broadcast([P, 4, SEQ]), ALU.mult)
                    v.tensor_tensor(probs[:, :, SEQ:SEQ + P], probs[:, :, SEQ:SEQ + P],
                                    stat[:, 28:32].unsqueeze(2).to_broadcast([P, 4, P]), ALU.mult)\
                        .then_inc(probs_ready.sem, 1)

                def turn_probs(g):
                    probsT_ps.wait(dve, g + 1, L)
                    v.tensor_copy(probsT[:, :, SEQ:SEQ + P], ps[:, 7, :].rearrange("p (j q) -> p j q", j=4))\
                        .then_inc(probsT_ready1.sem, 1)

                def turn_attention(g):
                    attn_hi.wait(dve, g + 1, L)
                    v.tensor_tensor(yA_lo[:, 2 * g:2 * g + 2, :], ps[:, 4, :].rearrange("p (c t) -> p c t", c=2),
                                    yA_hi[:, 2 * g:2 * g + 2, :].bitcast(F32), ALU.subtract)\
                        .then_inc(attn_lo.sem, 1)

                def merge(b, half):
                    gate_ready.wait(dve, 2 * b + half + 1, L)
                    y = ps[:, 4 + 2 * half:6 + 2 * half, :]
                    g = gates[:, :, half * 512:half * 512 + 512]
                    m = wide[:, :, half * 512:half * 512 + 512]
                    if b == 0:
                        v.tensor_tensor(m, y, g, ALU.mult).then_inc(merged.sem, 1)
                    else:
                        chain(v.tensor_tensor(g, y, g, ALU.mult))
                        v.tensor_tensor(m, m, g, ALU.add).then_inc(merged.sem, 1)

                def turn_merged(half, bank0):
                    for t in range(2):
                        mT_hi.wait(dve, 2 * half + t + 1, L)
                        part = (slice(None), slice(4 * half, 4 * half + 4), slice(t * P, t * P + P))
                        v.tensor_tensor(xT_lo[part], ps[:, bank0 + t, :].rearrange("p (k t) -> p k t", k=4),
                                        xT_hi[part].bitcast(F32), ALU.subtract).then_inc(mT_lo.sem, 1)

                for m in range(3, MIX_UNITS):
                    dve.wait_ge(unit_used, base + m - 2)
                    if m == 4:
                        rope(0, lambda t: wide[:, t, 0:512], 6)
                    if m == 6:
                        if L == 0:
                            dve.wait_ge(chan_ps, 1)
                            v.tensor_copy(chan[:], ps[:, 4, 0:40])
                        rope(1, lambda t: wide[:, t, 512:1024], 2)
                    if m == 8:
                        qkT_ps.wait(dve, 1, L)
                        v.tensor_copy(kT[:].rearrange("p c t -> p (c t)"),
                                      ps[:, 6:8, :].rearrange("p b n -> p (b n)")).then_inc(kT_ready.sem, 1)
                    if m == 10:
                        row_max(0)
                        rope(2, lambda t: ret_qk[:, t, :], 2)
                    if m == 11:
                        normalise(0)
                    if m == 13:
                        turn_probs(0)
                    if m == 14:
                        row_max(1)
                        turn_attention(0)
                    if m == 15:
                        normalise(1)
                    if m == 16:
                        conv_c_copied.wait(dve, 1, L)
                        chain(v.tensor_tensor(uT[:, :, 2:SEQ + 2], conv_c,
                                              ps[:, 0:2, :].rearrange("p b (c t) -> p (b c) t", c=2), ALU.mult))
                        w = lambda j, c: chan[:, 8 + L * 12 + j * 4 + c:9 + L * 12 + j * 4 + c]
                        for c in range(BT):
                            last = v.tensor_scalar(conv[:, c, :], uT[:, c, 2:SEQ + 2], w(2, c),
                                                   chan[:, 32 + L * 4 + c:33 + L * 4 + c], ALU.mult, ALU.add)
                        chain(last)
                        for c in range(BT):
                            last = v.scalar_tensor_tensor(conv[:, c, :], uT[:, c, 1:SEQ + 1], w(1, c),
                                                          conv[:, c, :], ALU.mult, ALU.add)
                        chain(last)
                        for c in range(BT):
                            last = v.scalar_tensor_tensor(conv[:, c, :], uT[:, c, 0:SEQ], w(0, c),
                                                          conv[:, c, :], ALU.mult, ALU.add)
                        last.then_inc(conv_u_ready.sem, 1)
                    if m == 17:
                        turn_probs(1)
                    if m == 18:
                        conv_u_ready.wait(dve, 1, L)
                        v.tensor_tensor(conv, conv, ps[:, 2:4, :].rearrange("p b (c t) -> p (b c) t", c=2),
                                        ALU.mult).then_inc(conv_y_ready.sem, 1)
                        turn_attention(1)
                        v.tensor_tensor(kzeta[:].rearrange("p (h d) -> p h d", h=RET_HEADS),
                                        ret_qk[:, 0, SEQ:2 * SEQ].rearrange("p (h d) -> p h d", h=RET_HEADS),
                                        const("zeta").unsqueeze(2).to_broadcast([P, RET_HEADS, HEAD]), ALU.mult)
                        ret_qkT_ps.wait(dve, 1, L)
                        v.tensor_copy(rkT[:].rearrange("p c t -> p (c t)"), ps[:, 6, :])
                        rqT_ready.wait(dve, 1, L)
                        v.tensor_tensor(rqxT[:], rqT[:, :, P:SEQ], const("xi").rearrange("p (c t) -> p c t", c=2),
                                        ALU.mult).then_inc(rkT_ready.sem, 1)
                        conv_hi.wait(dve, 1, L)
                        v.tensor_tensor(yC_lo[:], conv, yC_hi[:].bitcast(F32), ALU.subtract)\
                            .then_inc(conv_lo.sem, 1)
                    if m == 20:
                        ret_scores_ps.wait(dve, 1, L)
                        v.tensor_copy(state[:], ps[:, 7, 0:2 * P])
                        v.tensor_tensor(decayed.rearrange("p (t n) -> p t n", t=2), ps[:, 5:7, :],
                                        const("decay").unsqueeze(1).to_broadcast([P, 2, 512]), ALU.mult)\
                            .then_inc(decayed_ready.sem, 1)
                    if m == 22:
                        ret_sq_done.wait(dve, 1, L)
                        v.tensor_reduce(stat[:, 32:40], squares.rearrange("p (h d) -> p h d", d=P), AX_X, ALU.add)\
                            .then_inc(ret_ss_ready.sem, 1)
                    if m == 23:
                        ret_root.wait(dve, 1, L)
                        rsqrt(stat[:, 48:56], stat[:, 40:48], stat[:, 32:40], 1.0 / P, stat[:, 56:64])
                        ret_gate_ready.wait(dve, 1, L)
                        chain(v.tensor_tensor(ret_o[:].rearrange("p t (h d) -> p (t h) d", d=P),
                                              ps[:, 5:7, :].rearrange("p t (h d) -> p (t h) d", d=P),
                                              stat[:, 48:56].unsqueeze(2).to_broadcast([P, 8, P]), ALU.mult))
                        v.tensor_tensor(ret_o[:], ret_o[:], ret_gate[:], ALU.mult).then_inc(ret_y_ready.sem, 1)
                    if m == 26:
                        merge(0, 0)
                        merge(0, 1)
                        ret_hi.wait(dve, 1, L)
                        for c in range(BT):
                            last = v.scalar_tensor_tensor(
                                yA_lo[:, c, :], ps[:, c // 2, (c % 2) * SEQ:(c % 2) * SEQ + SEQ],
                                chan[:, L * BT + c:L * BT + c + 1], yA_hi[:, c, :].bitcast(F32),
                                ALU.mult, ALU.subtract)
                        last.then_inc(ret_lo.sem, 1)
                    if m == 32:
                        merge(1, 0)
                        merge(1, 1)
                    if m == 36:
                        merge(2, 0)
                    if m == 37:
                        turn_merged(0, 2)
                    if m == 38:
                        merge(2, 1)
                    if m == 39:
                        turn_merged(1, 0)
                    split_lo(dve, base + m)

            def dense():
                def activate(i):
                    dve.wait_ge(dn_silu, i)
                    v.tensor_tensor(dn_act[:], dn_sil[:], ps[:, 2:4, :], ALU.mult).then_inc(hidden_ready, 1)

                def turn(i):
                    dve.wait_ge(dnT_hi_ready, i)
                    for t in range(2):
                        tok = slice(t * P, t * P + P)
                        last = v.tensor_tensor(dnT_lo[:, :, tok],
                                               ps[:, 2 + t, :].rearrange("p (k n) -> p k n", k=4),
                                               dnT_hi[:, :, tok].bitcast(F32), ALU.subtract)
                    last.then_inc(dnT_lo_ready, 1)

                split_lo(dve, DENSE0 + 3)
                split_lo(dve, DENSE0 + 4)
                with dve.Fori(0, 6) as i:
                    split_lo(dve, DENSE0 + 5, i)
                    dve.wait_ge(unit_used, i * RAW + (DENSE0 + 4))
                    activate(i + 1)
                    split_lo(dve, DENSE0 + 6, i)
                    turn(i + 1)
                    for j in (7, 8, 9, 10):
                        split_lo(dve, DENSE0 + j, i)
                split_lo(dve, DENSE0 + 41)
                dve.wait_ge(unit_used, DENSE0 + 40)
                activate(FCH)
                turn(FCH)

            def one_hot(e):
                for t in range(2):
                    last = v.tensor_scalar(put_in[:, t, :], const("iota"), slot_of[:, t, bass.ds(e, 1)], None,
                                           ALU.is_equal)
                last.then_inc(put_in_ready, 1)

            def route():
                for t in range(2):
                    dve.wait_ge(tok_hi_ready, t + 1)
                    v.tensor_tensor(tok_lo[:, t, :], wide[:, t, :], tok_hi[:, t, :].bitcast(F32), ALU.subtract)\
                        .then_inc(tok_lo_ready, 1)
                dve.wait_ge(logits_ps, 1)
                parts = ps[:, 0, 0:4 * NEXP].rearrange("p (t h e) -> p t h e", t=2, h=2)
                chain(v.tensor_reduce(logits[:], parts.rearrange("p t h e -> p t e h"), AX_X, ALU.add))
                for t in range(2):
                    chain(v.max(top[:, t, :], logits[:, t, :]))
                    chain(v.max_index(top_at[:, t, :], top[:, t, :], logits[:, t, :]))
                chain(v.tensor_copy(top_f[:], top_at[:]))
                v.tensor_tensor(prob[:, 0:2], top[:, :, 1], top[:, :, 0], ALU.subtract).then_inc(gap_ready, 1)
                eight = const("iota")[:, 0:NEXP]
                for t in range(2):
                    v.tensor_scalar(first[:, t, :], eight, top_f[:, t, 0:1], None, ALU.is_equal)
                    chain(v.tensor_scalar(second[:, t, :], eight, top_f[:, t, 1:2], None, ALU.is_equal))
                v.tensor_tensor(chosen[:], first[:], second[:], ALU.add).then_inc(chosen_ready, 1)
                dve.wait_ge(gap_exp, 1)
                chain(v.tensor_scalar(prob[:, 4:6], prob[:, 2:4], 1.0, None, ALU.add))
                chain(v.reciprocal(prob[:, 4:6], prob[:, 4:6]))
                chain(v.tensor_tensor(prob[:, 6:8], prob[:, 2:4], prob[:, 4:6], ALU.mult))
                for t in range(2):
                    chain(v.tensor_scalar(share[:, t, :], first[:, t, :], prob[:, 4 + t:5 + t], None, ALU.mult))
                    chain(v.scalar_tensor_tensor(share[:, t, :], second[:, t, :], prob[:, 6 + t:7 + t],
                                                 share[:, t, :], ALU.mult, ALU.add))
                dve.wait_ge(chosen_ready, 1)
                dve.wait_ge(places_ps, 1)
                mine = slot_of[:]
                chain(v.scalar_tensor_tensor(mine, ps[:, 7, 0:16].rearrange("p (t e) -> p t e", t=2), 1.0,
                                             chosen[:], ALU.add, ALU.mult))
                chain(v.tensor_scalar(mine, mine, -1.0, None, ALU.add))
                one_hot(0)
                dve.wait_ge(totals_ps, 1)
                chain(v.tensor_reduce(stat[:, 8:9], ps[:, 4, 0:8], AX_X, ALU.max))
                v.tensor_scalar(crowded[:], stat[:, 8:9], float(P), None, ALU.is_gt).then_inc(routed, 1)
                split_lo(dve, MOE0 + 1)

            def experts(base, done):
                def take_gathered(n):
                    for half in range(2):
                        dve.wait_ge(ex_hi_ready, n + half + 1)
                        v.tensor_tensor(ex_lo[:, 4 * half:4 * half + 4, :],
                                        ps[:, 5 + half, :].rearrange("p (k t) -> p k t", k=4),
                                        ex_hi[:, 4 * half:4 * half + 4, :].bitcast(F32), ALU.subtract)\
                            .then_inc(ex_lo_ready, 1)

                def expert(pair, odd, last_one=False):
                    e, r, n = pair * 2 + odd, pair * FCH, base + odd * FFN_UNITS
                    f = pair * (2 * FCH) + (odd + done) * FCH

                    def activate(c, unit):
                        dve.wait_ge(unit_used, unit)
                        dve.wait_ge(ex_silu, c)
                        v.tensor_tensor(ex_act[:], ex_sil[:], ps[:, 1, :], ALU.mult).then_inc(hidden_ready, 1)

                    def turn(c):
                        dve.wait_ge(exT_hi_ready, c)
                        v.tensor_tensor(exT_lo[:], ps[:, 4, :].rearrange("p (k t) -> p k t", k=4),
                                        exT_hi[:].bitcast(F32), ALU.subtract).then_inc(exT_lo_ready, 1)

                    split_lo(dve, n + 4, r)
                    split_lo(dve, n + 5, r)
                    activate(f + 1, r * DEEP + (n + 4))
                    dve.wait_ge(put_back_ready, e + (done + 1))
                    v.tensor_copy(slot_w[:], ps[:, 7, SEQ:SEQ + 1]).then_inc(slot_w_ready, 1)
                    if not last_one:
                        one_hot(e + 1)

                    def step(i, s, splits=(10, 11)):
                        w, m, c = r + i, n + RAW * s, f + i * 2 + s
                        split_lo(dve, m + 6, w)
                        split_lo(dve, m + 7, w)
                        turn(c + 1)
                        split_lo(dve, m + 8, w)
                        split_lo(dve, m + 9, w)
                        activate(c + 2, w * DEEP + (m + 8))
                        for j in splits:
                            split_lo(dve, m + j, w)

                    double_steps = (FCH - 1) // 2
                    with dve.Fori(0, double_steps - last_one) as i:
                        step(i, 0)
                        step(i, 1)
                    if last_one:
                        step(double_steps - 1, 0)
                        step(double_steps - 1, 1, (10,))
                    turn(f + FCH)
                    if last_one:
                        split_lo(dve, n + 41, r)
                    if not last_one:
                        split_lo(dve, n + 42, r)
                        take_gathered(e * 2 + (2 * done + 2))
                        split_lo(dve, n + 43, r)
                    dve.wait_ge(ey_hi_ready, e + (done + 1))
                    v.scalar_tensor_tensor(ey_lo[:], ps[:, 2:4, :].rearrange("p b n -> p (b n)"), slot_w[:, 0:1],
                                           ey_hi[:].bitcast(F32), ALU.mult, ALU.subtract).then_inc(ey_lo_ready, 1)
                    if not last_one:
                        split_lo(dve, n + 44, r)
                        split_lo(dve, n + 45, r)
                    for t in range(2):
                        dve.wait_ge(back_ps, e * 2 + (2 * done + t + 1))
                        v.tensor_tensor(res[:, t, :], res[:, t, :],
                                        ps[:, 4 + 2 * t:6 + 2 * t, :].rearrange("p b n -> p (b n)"), ALU.add)\
                            .then_inc(res_added, 1)

                if done:
                    one_hot(0)
                    for j in range(3):
                        split_lo(dve, base + j)
                take_gathered(2 * done)
                if not done:
                    split_lo(dve, base + 2)
                split_lo(dve, base + 3)
                with dve.Fori(0, NEXP // 2 - 1) as pair:
                    expert(pair, 0)
                    expert(pair, 1)
                expert(NEXP // 2 - 1, 0)
                expert(NEXP // 2 - 1, 1, last_one=True)

            for t in range(2):
                dve.wait_ge(x_in[t], 16)
                normalise_tile(0, t)
            turn_normed(0, 0)
            split_lo(dve, 0)
            turn_normed(0, 1)
            split_lo(dve, 1)
            split_lo(dve, 2)
            dve.wait_ge(consts_in, 16)
            dve.wait_ge(pads_set, 1)
            out_proj_sums = (ps[:, 2:4, :], ps[:, 4:6, :])
            down_sums = (ps[:, 4:6, :], ps[:, 6:8, :])
            mixer(0)
            cross(1, DENSE0, out_proj_sums)
            dense()
            cross(2, MIX0[1], down_sums)
            mixer(1)
            dve.wait_ge(router_hi, 1)
            v.tensor_tensor(rt[:, :, NEXP:2 * NEXP], router[:], rt[:, :, 0:NEXP].bitcast(F32), ALU.subtract)\
                .then_inc(router_lo, 1)
            cross(3, MOE0, out_proj_sums)
            route()
            dve.wait_ge(routed, 1)
            flag = dve.value_load(crowded[0:1, 0:1], min_val=0, max_val=1)
            experts(MOE0, 0)

            with dve.If(flag > 0):
                dve.wait_ge(res_added, 6 + 2 * NEXP)
                v.tensor_scalar(slot_of[:], slot_of[:], -float(P), None, ALU.add).then_inc(slots_moved, 1)
                dve.wait_ge(slots_moved, 1)
                experts(CROWD0, NEXP)
            for t in range(2):
                normalise_tile(4, t)


_INS = ["x", "mix_norm_w", "w_in", "conv_w", "conv_b", "ret_norm_w", "w_br_attn", "w_br_conv", "w_br_ret",
        "w_out", "ffn_norm_w", "dense_w_gate", "dense_w_up", "dense_w_down", "moe_router", "moe_w_gate",
        "moe_w_up", "moe_w_down", "final_norm_w"]


def kernel(**inputs):
    import numpy as _np
    import concourse.bacc as _bacc
    from concourse import mybir as _mybir
    from concourse.bass_utils import run_bass_kernel_spmd as _run

    nc = _bacc.Bacc("TRN2", target_bir_lowering=False, num_devices=1)
    consts, masks = shape_constants()
    arrays, args = {}, []
    for name, a in [(n, inputs[n]) for n in _INS] + [("consts", consts), ("masks", masks)]:
        a = _np.ascontiguousarray(a)
        arrays[f"in_{name}_dram"] = a
        args.append(nc.dram_tensor(f"in_{name}_dram", a.shape, _mybir.dt.from_np(a.dtype), kind="ExternalInput").ap())
    args.append(nc.dram_tensor("out_0_dram", (1, SEQ, D), F32, kind="ExternalOutput").ap())
    hybrid_trunk_kernel(nc, *args)
    r = _run(nc, [arrays], core_ids=[0])
    return r.results[0]["out_0_dram"]
```
